# Optimizing a Trainium2 kernel written in Bass

```python
import math
import jax, jax.numpy as jnp
from jax import lax
import numpy as np

D_MODEL = 1024
BATCH = 1
SEQ = 256
DEPTH = 4

GRID_W = 64
CTX_LEN = 256
N_MIXERS = 4
NORM_EPS = 1e-6
N_MOD = 6
FFN_HIDDEN = ((8 * D_MODEL // 3 + 255) // 256) * 256

MLA_HEADS = D_MODEL // 128
MLA_NOPE = 128
MLA_ROPE = 64
MLA_V = 128
KV_LORA_RANK = D_MODEL // 4
Q_LORA_RANK = 3 * KV_LORA_RANK
ROPE_THETA = 10000.0
Q_BLOCK = 128

HYENA_ORDER = 2
HYENA_BANDS = 16
HYENA_EMB = 2 * HYENA_BANDS + 1
HYENA_FILTER_WIDTH = 64
HYENA_INNER = 2
HYENA_TARGET = 1e-2
HYENA_FAST = 0.3
HYENA_SLOW = 1.5
SHORT_CONV = 3

S5_GROUP = 16
S5_GROUPS = D_MODEL // S5_GROUP
S5_STATE = 64
S5_DT_MIN = 1e-3
S5_DT_MAX = 1e-1

FNET_GROUPS = 8
FNET_GC = D_MODEL // FNET_GROUPS

kernel_name = "hybrid_interleaved_mla_hyena_s5_fnet_dit"

def _n_layers_of(m):
    return (DEPTH - m + N_MIXERS - 1) // N_MIXERS

def rmsnorm(x, g):
    xf = x.astype(jnp.float32)
    y = xf * lax.rsqrt(jnp.mean(jnp.square(xf), axis=-1, keepdims=True) + NORM_EPS)
    return (y * g.astype(jnp.float32)).astype(x.dtype)

def modulate(h, shift, scale):
    return h * (1.0 + scale) + shift

def swiglu(h, w13, w2):
    a, b = jnp.split(h @ w13, 2, axis=-1)
    return (jax.nn.silu(a) * b) @ w2

def axial_rope(x, rope):
    cos_r, sin_r, cos_c, sin_c = rope
    if x.ndim == 4:
        cos_r, sin_r, cos_c, sin_c = (t[:, None, :] for t in rope)
    half = x.shape[-1] // 2

    def rot(xa, cs, sn):
        x1, x2 = jnp.split(xa, 2, axis=-1)
        return jnp.concatenate([x1 * cs - x2 * sn, x2 * cs + x1 * sn], axis=-1)

    out = jnp.concatenate([rot(x[..., :half], cos_r, sin_r), rot(x[..., half:], cos_c, sin_c)], axis=-1)
    return out.astype(x.dtype)

def mla_mixer(h_ctx, h_lat, rope, need_ctx, w_in, q_g, kv_g, w_uq, w_ukv, w_o):
    B, L, _ = h_lat.shape
    C = h_ctx.shape[1]
    H = MLA_HEADS

    def queries(zq, n):
        q = (rmsnorm(zq, q_g) @ w_uq).reshape(B, n, H, MLA_NOPE + MLA_ROPE)
        return q[..., :MLA_NOPE], q[..., MLA_NOPE:]

    def keys_values(zkv, n):
        ckv, k_rope = zkv[..., :KV_LORA_RANK], zkv[..., KV_LORA_RANK:]
        kv = (rmsnorm(ckv, kv_g) @ w_ukv).reshape(B, n, H, MLA_NOPE + MLA_V)
        return kv[..., :MLA_NOPE], k_rope, kv[..., MLA_NOPE:]

    z_lat = h_lat @ w_in
    ql_nope, ql_rope = queries(z_lat[..., :Q_LORA_RANK], L)
    kl_nope, kl_rope, vl = keys_values(z_lat[..., Q_LORA_RANK:], L)
    ql_rope_pos = axial_rope(ql_rope, rope)
    kl_rope_pos = axial_rope(kl_rope, rope)
    z_ctx = h_ctx @ (w_in if need_ctx else w_in[:, Q_LORA_RANK:])
    kc_nope, kc_rope, vc = keys_values(z_ctx[..., -(KV_LORA_RANK + MLA_ROPE):], C)
    scale = (MLA_NOPE + MLA_ROPE) ** -0.5

    def attend_block(blk):
        qn, qr_pos, qr = blk
        s_ctx = jnp.einsum('bqhd,bkhd->bhqk', qn, kc_nope) + jnp.einsum('bqhr,bkr->bhqk', qr, kc_rope)
        s_lat = jnp.einsum('bqhd,bkhd->bhqk', qn, kl_nope) + jnp.einsum('bqhr,bkr->bhqk', qr_pos, kl_rope_pos)
        s = jnp.concatenate([s_ctx, s_lat], axis=-1).astype(jnp.float32) * scale
        p = jax.nn.softmax(s, axis=-1).astype(vl.dtype)
        return jnp.einsum('bhqk,bkhd->bqhd', p[..., :C], vc) + jnp.einsum('bhqk,bkhd->bqhd', p[..., C:], vl)

    nb = L // Q_BLOCK

    def to_blocks(t):
        return jnp.moveaxis(t.reshape(B, nb, Q_BLOCK, *t.shape[2:]), 1, 0)

    o = lax.map(attend_block, (to_blocks(ql_nope), to_blocks(ql_rope_pos), to_blocks(ql_rope)))
    o_lat = jnp.moveaxis(o, 0, 1).reshape(B, L, H * MLA_V) @ w_o
    if not need_ctx:
        return None, o_lat
    qc_nope, qc_rope = queries(z_ctx[..., :Q_LORA_RANK], C)
    s = (jnp.einsum('bqhd,bkhd->bhqk', qc_nope, kc_nope)
         + jnp.einsum('bqhr,bkr->bhqk', qc_rope, kc_rope)).astype(jnp.float32) * scale
    p = jax.nn.softmax(s, axis=-1).astype(vc.dtype)
    o_ctx = jnp.einsum('bhqk,bkhd->bqhd', p, vc).reshape(B, C, H * MLA_V) @ w_o
    return o_ctx, o_lat

def short_conv(u, w, b):
    n = u.shape[1]
    pad = SHORT_CONV // 2
    up = jnp.pad(u, ((0, 0), (pad, pad), (0, 0)))
    out = b
    for k in range(SHORT_CONV):
        out = out + up[:, k:k + n] * w[k]
    return out

def hyena_kernel(n, f_w1, f_b1, f_freq, f_w2, f_b2, f_w3):
    f32 = jnp.float32
    t = jnp.linspace(0.0, 1.0, n, dtype=f32)[:, None]
    w = (2.0 * math.pi / n) * jnp.arange(n, dtype=f32)[:, None]
    bands = jnp.linspace(1e-4, HYENA_BANDS - 1, HYENA_BANDS, dtype=f32)[None, :]
    z = jnp.concatenate([t, jnp.cos(w * bands), -jnp.sin(w * bands)], axis=-1)
    freq = f_freq.astype(f32)
    a = jnp.sin(freq * (z @ f_w1.astype(f32) + f_b1.astype(f32)))
    for k in range(HYENA_INNER):
        a = jnp.sin(freq * (a @ f_w2[k].astype(f32) + f_b2[k].astype(f32)))
    h = (a @ f_w3.astype(f32)).reshape(n, HYENA_ORDER - 1, 2, D_MODEL)
    deltas = jnp.abs(jnp.linspace(math.log(HYENA_TARGET) / HYENA_SLOW, math.log(HYENA_TARGET) / HYENA_FAST,
                                  D_MODEL, dtype=f32))
    h = h * jnp.exp(-t * deltas)[:, None, None, :]
    k = jnp.concatenate([h[:, :, 0], jnp.zeros((1, HYENA_ORDER - 1, D_MODEL), f32), h[:0:-1, :, 1]], axis=0)
    return k / jnp.sum(jnp.abs(k), axis=0, keepdims=True)

def hyena_seq(h, w_in, b_in, conv_w, conv_b, filt, skip, w_out, b_out):
    f32 = jnp.float32
    n = h.shape[1]
    u = short_conv(h @ w_in + b_in, conv_w, conv_b)
    chunks = jnp.split(u, HYENA_ORDER + 1, axis=-1)
    gates, v = chunks[:-1], chunks[-1]
    kf = jnp.fft.rfft(hyena_kernel(n, *filt), n=2 * n, axis=0)
    for o, g in enumerate(reversed(gates[1:])):
        v = v * g
        vf = jnp.fft.rfft(v.astype(f32), n=2 * n, axis=1)
        y = jnp.fft.irfft(vf * kf[None, :, o, :], n=2 * n, axis=1)[:, :n]
        v = (y + v.astype(f32) * skip[o].astype(f32)).astype(h.dtype)
    return (v * gates[0]) @ w_out + b_out

def _lin_rec(e1, e2):
    a1, b1 = e1
    a2, b2 = e2
    return a1 * a2, a2 * b1 + b2

def s5_scan(u, lam_bar, b_bar, h0, reverse):
    bu = jnp.einsum('bngc,gsc->bngs', u.astype(jnp.complex64), b_bar)
    a = jnp.broadcast_to(lam_bar, bu.shape)
    a_cum, xs = lax.associative_scan(_lin_rec, (a, bu), axis=1, reverse=reverse)
    if h0 is None:
        return xs
    return xs + a_cum * h0[:, None]

def s5_mixer(h_ctx, h_lat, need_ctx, lam_re, lam_im, log_dt, b_re, b_im, c_re, c_im, d_skip, w_glu, b_glu):
    f32 = jnp.float32
    B, L, D = h_lat.shape
    C = h_ctx.shape[1]
    u_lat = h_lat.astype(f32).reshape(B, L, S5_GROUPS, S5_GROUP)
    u_ctx = h_ctx.astype(f32).reshape(B, C, S5_GROUPS, S5_GROUP)
    dsk = d_skip.astype(f32)
    y_lat = dsk * h_lat.astype(f32)
    y_ctx = dsk * h_ctx.astype(f32) if need_ctx else None
    for direction, reverse in ((0, False), (1, True)):
        lam = lax.complex(lam_re[direction].astype(f32), lam_im[direction].astype(f32))
        dt = jnp.exp(log_dt[direction].astype(f32))[:, None]
        lam_bar = jnp.exp(lam * dt)
        b_bar = ((lam_bar - 1.0) / lam)[..., None] * lax.complex(b_re[direction].astype(f32), b_im[direction].astype(f32))
        c_mat = lax.complex(c_re[direction].astype(f32), c_im[direction].astype(f32))
        xs_ctx = s5_scan(u_ctx, lam_bar, b_bar, None, reverse)
        h0 = xs_ctx[:, 0] if reverse else xs_ctx[:, -1]
        xs_lat = s5_scan(u_lat, lam_bar, b_bar, h0, reverse)
        y_lat = y_lat + jnp.einsum('bngs,gcs->bngc', xs_lat, c_mat).real.reshape(B, L, D)
        if need_ctx:
            y_ctx = y_ctx + jnp.einsum('bngs,gcs->bngc', xs_ctx, c_mat).real.reshape(B, C, D)

    def glu(y, dtype):
        g = jax.nn.gelu(y.astype(dtype), approximate=False)
        a, b = jnp.split(g @ w_glu + b_glu, 2, axis=-1)
        return a * jax.nn.sigmoid(b)

    return (glu(y_ctx, h_ctx.dtype) if need_ctx else None), glu(y_lat, h_lat.dtype)

def fnet_seq(h, w_o, b_o):
    B, n, D = h.shape
    hg = h.astype(jnp.float32).reshape(B, n, FNET_GROUPS, FNET_GC)
    f = jnp.fft.fftn(hg, axes=(1, 3), norm="ortho").real
    return f.reshape(B, n, D).astype(h.dtype) @ w_o + b_o

def setup_inputs(seed: int = 0) -> dict:
    key = jax.random.key(seed)
    ks = iter(jax.random.split(key, 64))
    f32 = jnp.float32

    def nrm(shape, scale):
        return scale * jax.random.normal(next(ks), shape, f32)

    nA, nB, nC, nD = (_n_layers_of(m) for m in range(N_MIXERS))
    D, F, H, G, N = D_MODEL, FFN_HIDDEN, MLA_HEADS, S5_GROUPS, S5_STATE
    P = (HYENA_ORDER + 1) * D
    return {
        "x": nrm((BATCH, SEQ, D), 1.0),
        "c": nrm((BATCH, D), 1.0),
        "ctx": nrm((BATCH, CTX_LEN, D), 1.0),
        "c_ctx": nrm((D,), 1.0),
        "mod_w": nrm((DEPTH, D, N_MOD * D), D ** -0.5),
        "mod_b": nrm((DEPTH, N_MOD * D), 0.02),
        "mix_pre_g": 1.0 + nrm((DEPTH, D), 0.02),
        "mix_post_g": 1.0 + nrm((DEPTH, D), 0.02),
        "ffn_pre_g": 1.0 + nrm((DEPTH, D), 0.02),
        "ffn_post_g": 1.0 + nrm((DEPTH, D), 0.02),
        "ffn_w13": nrm((DEPTH, D, 2 * F), D ** -0.5),
        "ffn_w2": nrm((DEPTH, F, D), F ** -0.5),
        "mla_w_in": nrm((nA, D, Q_LORA_RANK + KV_LORA_RANK + MLA_ROPE), D ** -0.5),
        "mla_q_norm_g": 1.0 + nrm((nA, Q_LORA_RANK), 0.02),
        "mla_kv_norm_g": 1.0 + nrm((nA, KV_LORA_RANK), 0.02),
        "mla_w_uq": nrm((nA, Q_LORA_RANK, H * (MLA_NOPE + MLA_ROPE)), Q_LORA_RANK ** -0.5),
        "mla_w_ukv": nrm((nA, KV_LORA_RANK, H * (MLA_NOPE + MLA_V)), KV_LORA_RANK ** -0.5),
        "mla_w_o": nrm((nA, H * MLA_V, D), (H * MLA_V) ** -0.5),
        "hy_w_in": nrm((nB, D, P), D ** -0.5),
        "hy_b_in": nrm((nB, P), 0.02),
        "hy_conv_w": nrm((nB, SHORT_CONV, P), SHORT_CONV ** -0.5),
        "hy_conv_b": nrm((nB, P), 0.02),
        "hy_f_w1": nrm((nB, HYENA_EMB, HYENA_FILTER_WIDTH), HYENA_EMB ** -0.5),
        "hy_f_b1": nrm((nB, HYENA_FILTER_WIDTH), 0.02),
        "hy_f_freq": 1.0 + nrm((nB, HYENA_FILTER_WIDTH), 0.02),
        "hy_f_w2": nrm((nB, HYENA_INNER, HYENA_FILTER_WIDTH, HYENA_FILTER_WIDTH), HYENA_FILTER_WIDTH ** -0.5),
        "hy_f_b2": nrm((nB, HYENA_INNER, HYENA_FILTER_WIDTH), 0.02),
        "hy_f_w3": nrm((nB, HYENA_FILTER_WIDTH, (HYENA_ORDER - 1) * 2 * D), HYENA_FILTER_WIDTH ** -0.5),
        "hy_skip": nrm((nB, HYENA_ORDER - 1, D), 0.5),
        "hy_w_out": nrm((nB, D, D), D ** -0.5),
        "hy_b_out": nrm((nB, D), 0.02),
        "s5_lambda_re": -0.5 + nrm((nC, 2, G, N), 0.01),
        "s5_lambda_im": jnp.broadcast_to(math.pi * jnp.arange(N, dtype=f32), (nC, 2, G, N)),
        "s5_log_dt": jax.random.uniform(next(ks), (nC, 2, G), f32, math.log(S5_DT_MIN), math.log(S5_DT_MAX)),
        "s5_b_re": nrm((nC, 2, G, N, S5_GROUP), (2 * S5_GROUP) ** -0.5),
        "s5_b_im": nrm((nC, 2, G, N, S5_GROUP), (2 * S5_GROUP) ** -0.5),
        "s5_c_re": nrm((nC, 2, G, S5_GROUP, N), (2 * N) ** -0.5),
        "s5_c_im": nrm((nC, 2, G, S5_GROUP, N), (2 * N) ** -0.5),
        "s5_d": nrm((nC, D), 1.0),
        "s5_w_glu": nrm((nC, D, 2 * D), D ** -0.5),
        "s5_b_glu": nrm((nC, 2 * D), 0.02),
        "fn_w_o": nrm((nD, D, D), D ** -0.5),
        "fn_b_o": nrm((nD, D), 0.02),
    }

def reference(x, c, ctx, c_ctx, mod_w, mod_b, mix_pre_g, mix_post_g, ffn_pre_g, ffn_post_g, ffn_w13, ffn_w2,
              mla_w_in, mla_q_norm_g, mla_kv_norm_g, mla_w_uq, mla_w_ukv, mla_w_o,
              hy_w_in, hy_b_in, hy_conv_w, hy_conv_b, hy_f_w1, hy_f_b1, hy_f_freq, hy_f_w2, hy_f_b2, hy_f_w3,
              hy_skip, hy_w_out, hy_b_out,
              s5_lambda_re, s5_lambda_im, s5_log_dt, s5_b_re, s5_b_im, s5_c_re, s5_c_im, s5_d, s5_w_glu, s5_b_glu,
              fn_w_o, fn_b_o):
    f32 = jnp.float32
    n_lat = x.shape[1]
    ROWS = n_lat // GRID_W
    row = jnp.repeat(jnp.arange(ROWS, dtype=f32), GRID_W)
    col = jnp.tile(jnp.arange(GRID_W, dtype=f32), ROWS)
    axis_dim = MLA_ROPE // 2
    inv_freq = 1.0 / (ROPE_THETA ** (jnp.arange(0, axis_dim, 2, dtype=f32) / axis_dim))
    ang_r = row[:, None] * inv_freq
    ang_c = col[:, None] * inv_freq
    rope = (jnp.cos(ang_r), jnp.sin(ang_r), jnp.cos(ang_c), jnp.sin(ang_c))

    silu_c = jax.nn.silu(c)
    silu_cc = jax.nn.silu(c_ctx)
    reads_ctx = (0, 2)
    xl, xc = x, ctx
    for i in range(DEPTH):
        m, j = i % N_MIXERS, i // N_MIXERS
        ctx_read = m in reads_ctx
        ctx_out = any((k % N_MIXERS) in reads_ctx for k in range(i + 1, DEPTH))
        mod_l = jnp.split((silu_c @ mod_w[i] + mod_b[i])[:, None, :], N_MOD, axis=-1)
        hl = modulate(rmsnorm(xl, mix_pre_g[i]), mod_l[0], mod_l[1])
        hc = None
        if ctx_read or ctx_out:
            mod_c = jnp.split((silu_cc @ mod_w[i] + mod_b[i])[None, None, :], N_MOD, axis=-1)
            hc = modulate(rmsnorm(xc, mix_pre_g[i]), mod_c[0], mod_c[1])

        if m == 0:
            yc, yl = mla_mixer(hc, hl, rope, ctx_out, mla_w_in[j], mla_q_norm_g[j], mla_kv_norm_g[j],
                               mla_w_uq[j], mla_w_ukv[j], mla_w_o[j])
        elif m == 1:
            filt = (hy_f_w1[j], hy_f_b1[j], hy_f_freq[j], hy_f_w2[j], hy_f_b2[j], hy_f_w3[j])
            hy_args = (hy_w_in[j], hy_b_in[j], hy_conv_w[j], hy_conv_b[j], filt, hy_skip[j], hy_w_out[j], hy_b_out[j])
            yl = hyena_seq(hl, *hy_args)
            yc = hyena_seq(hc, *hy_args) if ctx_out else None
        elif m == 2:
            yc, yl = s5_mixer(hc, hl, ctx_out, s5_lambda_re[j], s5_lambda_im[j], s5_log_dt[j], s5_b_re[j],
                              s5_b_im[j], s5_c_re[j], s5_c_im[j], s5_d[j], s5_w_glu[j], s5_b_glu[j])
        else:
            yl = fnet_seq(hl, fn_w_o[j], fn_b_o[j])
            yc = fnet_seq(hc, fn_w_o[j], fn_b_o[j]) if ctx_out else None

        xl = xl + mod_l[2] * rmsnorm(yl, mix_post_g[i])
        hl = modulate(rmsnorm(xl, ffn_pre_g[i]), mod_l[3], mod_l[4])
        xl = xl + mod_l[5] * rmsnorm(swiglu(hl, ffn_w13[i], ffn_w2[i]), ffn_post_g[i])
        if ctx_out:
            xc = xc + mod_c[2] * rmsnorm(yc, mix_post_g[i])
            hc = modulate(rmsnorm(xc, ffn_pre_g[i]), mod_c[3], mod_c[4])
            xc = xc + mod_c[5] * rmsnorm(swiglu(hc, ffn_w13[i], ffn_w2[i]), ffn_post_g[i])
    return xl


_drawn_inputs = setup_inputs


def setup_inputs(seed=0):
    import zlib

    import numpy as np

    out = dict(_drawn_inputs(seed))
    spreads = {}
    factors = {'mix_pre_g': 2.947,
     'mix_post_g': 3.058,
     'ffn_post_g': 3.446,
     'mla_q_norm_g': 8.0,
     'mla_kv_norm_g': 4.156,
     'hy_b_in': 5.293,
     'hy_conv_b': 4.565,
     'hy_f_b1': 8.0,
     'hy_f_freq': 8.0,
     'hy_f_b2': 2.83,
     'hy_b_out': 62.36,
     's5_lambda_re': 200.0,
     's5_b_glu': 7.466,
     'fn_b_o': 18.992,
     's5_lambda_im': 29.008,
     's5_log_dt': 34.032,
     's5_b_re': 40.448,
     's5_b_im': 41.704,
     's5_c_re': 40.744,
     's5_c_im': 40.376}
    for name, (base, spread) in spreads.items():
        noise = np.random.default_rng([zlib.crc32(name.encode()), seed]).standard_normal(out[name].shape)
        drawn = base * np.exp(spread * noise) if base else spread * noise
        out[name] = __import__('jax').numpy.asarray(drawn.astype(out[name].dtype))
    for name, factor in factors.items():
        out[name] = (out[name] * factor).astype(out[name].dtype)
    return out
```

```python
import math
from contextlib import ExitStack

import numpy as np

import concourse.bass as bass
from concourse import mybir

F32 = mybir.dt.float32
ACT = mybir.ActivationFunctionType
ALU = mybir.AluOpType
AX = mybir.AxisListType

P = 128
D = 1024
KD = D // P
LAT = 256
CTX = 256
TOK = LAT + CTX
DEPTH = 4
MODS = 6
FFN = 2816
KF = FFN // P
EPS = 1e-6

HEADS = 8
NOPE = 128
ROPE = 64
VDIM = 128
KVR = 256
QR = 768

BANDS = 16
EMB = 2 * BANDS + 1
WIDTH = 64

GROUPS = 64
GC = 16
STATE = 64
STEP = 8
CH = LAT // STEP
HALF = GROUPS // 2
LAGS = 2 * STEP + 2

RING = 2
SLOT = KF * 256
ARENA = 31600

TWO_PI = 2.0 * math.pi
ROUND = 1.5 * 2.0 ** 23
PI_HI = 6.28125
PI_MID = float(np.float32(TWO_PI - PI_HI))
PI_LO = float(np.float32(TWO_PI - PI_HI - PI_MID))
PI_IN = 3.1415925

VEC = {}


def _rows():
    tiles = [
        [("mod_b01", 2 * MODS * KD)],
        [("mod_b23", 2 * MODS * KD)],
        [("mix_pre_g", DEPTH * KD), ("mix_post_g", DEPTH * KD), ("ffn_pre_g", DEPTH * KD), ("ffn_post_g", DEPTH * KD)],
        [("hy_b_in", 24), ("hy_conv_w", 72), ("hy_conv_b", 24)],
        [("hy_skip", 8), ("hy_b_out", 8), ("s5_d", 8), ("s5_b_glu", 16), ("fn_b_o", 8),
         ("mla_q_norm_g", 6), ("mla_kv_norm_g", 2), ("c", 8), ("c_ctx", 8)],
    ]
    for t, rows in enumerate(tiles):
        at = 0
        for name, n in rows:
            VEC[name] = (t, at, n)
            at += n
    return [sum(n for _, n in rows) for rows in tiles]


VEC_ROWS = _rows()


def build(nc, A, out, layers=(0, 1, 2, 3)):
    ctx = ExitStack()
    with ctx:
        def sb(name, shape):
            return ctx.enter_context(nc.sbuf_tensor(name, shape, F32))

        def sem(name):
            return ctx.enter_context(nc.semaphore(name))

        x = sb("x_sb", [P, KD, TOK])
        h = sb("h_sb", [P, KD, TOK])
        arena = sb("arena", [P, ARENA])
        ring = sb("ring", [P, RING, SLOT])
        vec = sb("vec", [P, 5, P])
        rstd = sb("rstd", [P, TOK])
        ident = sb("ident", [P, P])
        ones = sb("ones", [P, P])
        silu_c = sb("silu_c", [P, KD, 2])
        modv = sb("modv", [P, 2, MODS * KD, 2])
        affine = sb("affine", [P, 2, 4, KD, 2])
        small = sb("small", [P, 64])
        bank = [ctx.enter_context(nc.psum_tensor(f"bank{i}", [P, 512], F32)) for i in range(8)]
        SUMS, MODP = bank[6], bank[7]

        used = [0]

        def area(at, *dims):
            n = int(np.prod(dims))
            assert at + n <= ARENA, (at, n)
            used[0] = max(used[0], at + n)
            v = arena[:, at:at + n]
            if len(dims) == 2:
                v = v.rearrange("p (a b) -> p a b", b=dims[1])
            if len(dims) == 3:
                v = v.rearrange("p (a b c) -> p a b c", b=dims[1], c=dims[2])
            if len(dims) == 4:
                v = v.rearrange("p (a b c d) -> p a b c d", b=dims[1], c=dims[2], d=dims[3])
            return v

        def vcol(name, j, n=1):
            t, at, _ = VEC[name]
            return vec[:, t, at + j:at + j + n]

        w_arrived = [sem(f"w_arrived{i}") for i in range(RING)]
        panels = []
        slot_count = [0] * RING

        class Weights:

            def __init__(self, sources, freed):
                self.p0 = len(panels)
                self.arrived = []
                for i, loads in enumerate(sources):
                    slot = len(panels) % RING
                    slot_count[slot] += 16 * len(loads)
                    self.arrived.append((slot, slot_count[slot]))
                    panels.append((loads, freed(i)))

            def slot(self, i):
                return ring[:, (self.p0 + i) % RING, :]

            def view(self, i, kk, width):
                return self.slot(i)[:, 0:kk * width].rearrange("p (k n) -> p k n", n=width)

            def wait(self, pe, i):
                slot, value = self.arrived[i]
                pe.wait_ge(w_arrived[slot], value)

        def cols_of(w, c0, n):
            return w[:, c0:c0 + n].rearrange("(k p) n -> p k n", p=P)

        issued = [0]

        def sp_issue(sp, upto):
            while issued[0] < min(upto, len(panels)):
                p = issued[0]
                if p >= RING:
                    sp.wait_ge(*panels[p - RING][1])
                at = 0
                for src in panels[p][0]:
                    kk, nn = src.shape[1], src.shape[2]
                    dst = ring[:, p % RING, at:at + kk * nn].rearrange("p (k n) -> p k n", n=nn)
                    at += kk * nn
                    sp.dma_start(dst, src).then_inc(w_arrived[p % RING], 16)
                issued[0] += 1

        vec_loaded = sem("vec_loaded")
        consts_set = sem("consts_set")
        vec_turned = sem("vec_turned")
        vec_ready = sem("vec_ready")
        silu_ready = sem("silu_ready")
        x_loaded = sem("x_loaded")
        rows = area(0, 5, P)
        xrow = area(2 * KD * TOK, 4, D)
        x_turned = sem("x_turned")
        x_ready = sem("x_ready")

        class Setup:
            def sync(self, sp):
                sp.dma_start(xrow[:, 0:2, :], A["x"][0].rearrange("(b p) d -> p b d", p=P)).then_inc(x_loaded, 16)
                sp.dma_start(xrow[:, 2:4, :], A["ctx"][0].rearrange("(b p) d -> p b d", p=P)).then_inc(x_loaded, 16)

            def scalar(self, act):
                loads = [
                    ("mod_b01", A["mod_b"][0:2].rearrange("l (j p) -> (l j) p", p=P)),
                    ("mod_b23", A["mod_b"][2:4].rearrange("l (j p) -> (l j) p", p=P)),
                    ("mix_pre_g", A["mix_pre_g"].rearrange("l (j p) -> (l j) p", p=P)),
                    ("mix_post_g", A["mix_post_g"].rearrange("l (j p) -> (l j) p", p=P)),
                    ("ffn_pre_g", A["ffn_pre_g"].rearrange("l (j p) -> (l j) p", p=P)),
                    ("ffn_post_g", A["ffn_post_g"].rearrange("l (j p) -> (l j) p", p=P)),
                    ("hy_b_in", A["hy_b_in"][0].rearrange("(j p) -> j p", p=P)),
                    ("hy_conv_w", A["hy_conv_w"][0].rearrange("w (j p) -> (w j) p", p=P)),
                    ("hy_conv_b", A["hy_conv_b"][0].rearrange("(j p) -> j p", p=P)),
                    ("hy_skip", A["hy_skip"][0, 0].rearrange("(j p) -> j p", p=P)),
                    ("hy_b_out", A["hy_b_out"][0].rearrange("(j p) -> j p", p=P)),
                    ("s5_d", A["s5_d"][0].rearrange("(j p) -> j p", p=P)),
                    ("s5_b_glu", A["s5_b_glu"][0].rearrange("(j p) -> j p", p=P)),
                    ("fn_b_o", A["fn_b_o"][0].rearrange("(j p) -> j p", p=P)),
                    ("mla_q_norm_g", A["mla_q_norm_g"][0].rearrange("(j p) -> j p", p=P)),
                    ("mla_kv_norm_g", A["mla_kv_norm_g"][0].rearrange("(j p) -> j p", p=P)),
                    ("c", A["c"][0].rearrange("(j p) -> j p", p=P)),
                    ("c_ctx", A["c_ctx"].rearrange("(j p) -> j p", p=P)),
                ]
                for name, src in loads:
                    t, at, n = VEC[name]
                    act.dma_start(rows[at:at + n, t, :], src).then_inc(vec_loaded, 16)
                self.n_loads = len(loads)
                act.wait_ge(vec_ready, 5)
                nc.scalar.activation(silu_c[:, :, 0], vcol("c", 0, KD), ACT.Silu).then_inc(silu_ready, 1)
                nc.scalar.activation(silu_c[:, :, 1], vcol("c_ctx", 0, KD), ACT.Silu).then_inc(silu_ready, 1)

            def gpsimd(self, pool):
                nc.gpsimd.memset(ones[:, :], 1.0).then_inc(consts_set, 1)
                nc.gpsimd.memset(ident[:, :], 0.0).then_inc(consts_set, 1)
                pool.wait_ge(consts_set, 2)
                nc.gpsimd.affine_select(out=ident[:, :], in_=ident[:, :], compare_op=ALU.not_equal, fill=1.0, base=0,
                                        pattern=[[-1, P]], channel_multiplier=1).then_inc(consts_set, 1)

            def tensor(self, pe):
                pe.wait_ge(consts_set, 3)
                pe.wait_ge(vec_loaded, 16 * 18)
                for t, n in enumerate(VEC_ROWS):
                    nc.tensor.transpose(bank[t][:, 0:n], rows[0:n, t, :], ident[0:n, 0:n]).then_inc(vec_turned, 1)
                pe.wait_ge(x_loaded, 32)
                for k in range(KD):
                    b = 5 if k % 2 else 6
                    if k >= 2:
                        pe.wait_ge(x_ready, k - 1)
                    for t in range(4):
                        last = nc.tensor.transpose(bank[b][:, t * P:(t + 1) * P], xrow[:, t, k * P:(k + 1) * P], ident[:, :])
                    last.then_inc(x_turned, 1)

            def vector(self, dve):
                for t, n in enumerate(VEC_ROWS):
                    dve.wait_ge(vec_turned, t + 1)
                    nc.vector.tensor_copy(vec[:, t, 0:n], bank[t][:, 0:n]).then_inc(vec_ready, 1)
                for k in range(KD):
                    b = 5 if k % 2 else 6
                    dve.wait_ge(x_turned, k + 1)
                    nc.vector.tensor_copy(x[:, k, :], bank[b][:, :]).then_inc(x_ready, 1)

        mod_summed = sem("mod_summed")
        mod_ready = sem("mod_ready")
        mod_count = [0]
        MOD_COLS = 512
        MOD_PANELS = MODS * D // MOD_COLS
        MOD_STEPS = 5

        class Modulation:

            def __init__(self, layer):
                self.layer, self.u = layer, mod_count[0]
                mod_count[0] += 1
                w = A["mod_w"][layer]
                self.w = Weights([[cols_of(w, i * MOD_COLS, MOD_COLS)] for i in range(MOD_PANELS)],
                                 lambda i: (mod_summed, MOD_PANELS * self.u + i + 1))
                self.buf = self.u % 2

            def tensor(self, pe):
                if self.u == 0:
                    pe.wait_ge(silu_ready, 2)
                else:
                    pe.wait_ge(mod_ready, MOD_STEPS * (self.u - 1) + 1)
                for i in range(MOD_PANELS):
                    self.w.wait(pe, i)
                    v = self.w.view(i, KD, MOD_COLS)
                    for q in range(MOD_COLS // P):
                        j = i * (MOD_COLS // P) + q
                        for k in range(KD):
                            last = nc.tensor.matmul(MODP[:, 2 * j:2 * j + 2], v[:, k, q * P:(q + 1) * P],
                                                    silu_c[:, k, :], start=(k == 0), stop=(k == KD - 1))
                    last.then_inc(mod_summed, 1)

            def vector(self, dve):
                l, b = self.layer, self.buf
                m = modv[:, b]
                name = "mod_b01" if l < 2 else "mod_b23"
                base = MOD_STEPS * self.u
                dve.wait_ge(mod_summed, MOD_PANELS * (self.u + 1))
                bias = vcol(name, (l % 2) * MODS * KD, MODS * KD).unsqueeze(2).to_broadcast([P, MODS * KD, 2])
                nc.vector.tensor_tensor(m, MODP[:, 0:96].rearrange("p (j s) -> p j s", s=2), bias,
                                        ALU.add).then_inc(mod_ready, 1)
                dve.wait_ge(mod_ready, base + 1)
                for n, (g, at, plus) in enumerate([("mix_pre_g", 1, 1.0), ("mix_post_g", 2, 0.0),
                                                   ("ffn_pre_g", 4, 1.0), ("ffn_post_g", 5, 0.0)]):
                    gv = vcol(g, l * KD, KD).unsqueeze(2).to_broadcast([P, KD, 2])
                    nc.vector.scalar_tensor_tensor(affine[:, b, n], m[:, at * KD:(at + 1) * KD, :], plus, gv,
                                                   ALU.add, ALU.mult).then_inc(mod_ready, 1)

            def wait(self, eng):
                eng.wait_ge(mod_ready, MOD_STEPS * (self.u + 1))

            def shift(self, ffn, k, s):
                j = (3 if ffn else 0) * KD + k
                return modv[:, self.buf, j, s:s + 1]

            def factor(self, n, k, s):
                return affine[:, self.buf, n, k, s:s + 1]

        squared = sem("squared")
        sq_added = sem("sq_added")
        sq_summed = sem("sq_summed")
        rms_step = sem("rms_step")
        rms_root = sem("rms_root")
        n_sq, n_add, n_rms = [0], [0], [0]

        class Rms:

            def __init__(self, src, kk, n, sq, ready, feats):
                self.src, self.kk, self.n, self.sq, self.ready, self.feats = src, kk, n, sq, ready, feats
                self.sq0, self.add0, self.u = n_sq[0], n_add[0], n_rms[0]
                n_sq[0] += kk
                n_add[0] += kk - 1
                n_rms[0] += 1

            def scalar(self, act):
                for k in range(self.kk):
                    self.ready(act, k)
                    nc.scalar.activation(self.sq[:, k, 0:self.n], self.src[:, k, 0:self.n], ACT.Square).then_inc(squared, 1)
                act.wait_ge(rms_step, 2 * self.u + 1)
                nc.scalar.activation(rstd[:, 0:self.n], rstd[:, 0:self.n], ACT.Sqrt).then_inc(rms_root, 1)

            def vector(self, dve):
                n = self.n
                acc = self.sq[:, 0, 0:n]
                for k in range(1, self.kk):
                    dve.wait_ge(squared, self.sq0 + k + 1)
                    if k > 1:
                        dve.wait_ge(sq_added, self.add0 + k - 1)
                    nc.vector.tensor_tensor(acc, acc, self.sq[:, k, 0:n], ALU.add).then_inc(sq_added, 1)
                dve.wait_ge(sq_summed, self.u + 1)
                nc.vector.tensor_scalar(rstd[:, 0:n], SUMS[:, 0:n], 1.0 / self.feats, EPS,
                                        ALU.mult, ALU.add).then_inc(rms_step, 1)
                dve.wait_ge(rms_root, self.u + 1)
                nc.vector.reciprocal(rstd[:, 0:n], rstd[:, 0:n]).then_inc(rms_step, 1)
                dve.wait_ge(rms_step, 2 * self.u + 2)

            def tensor(self, pe):
                pe.wait_ge(sq_added, self.add0 + self.kk - 1)
                nc.tensor.matmul(SUMS[:, 0:self.n], ones[:, :], self.sq[:, 0, 0:self.n],
                                 start=True, stop=True).then_inc(sq_summed, 1)

        normed = sem("normed")
        h_ready = sem("h_ready")
        n_pre = [0]
        x_updated = sem("x_updated")
        n_post = [0]

        SQ = area(0, KD, TOK)

        def segments(n):
            return [(0, 0, LAT)] + ([(1, LAT, TOK)] if n == TOK else [])

        class PreNorm:

            def __init__(self, mod, ffn, n, split=False):
                self.mod, self.ffn, self.n, self.split = mod, ffn, n, split
                self.u = n_pre[0]
                n_pre[0] += 1
                posts = self.posts = n_post[0]

                def ready(eng, k):
                    if posts == 0:
                        eng.wait_ge(x_ready, k + 1)
                    else:
                        eng.wait_ge(x_updated, KD * (posts - 1) + k + 1)
                self.rms = Rms(x, KD, n, SQ, ready, D)

            def dst(self, k, a, b):
                if not self.split:
                    return h[:, k, a:b]
                return h[:, k, :].rearrange("p (s z m) -> p z m s", z=2, m=CH)[:, a // LAT]

            def src(self, k, a, b):
                if not self.split:
                    return SQ[:, k, a:b]
                return SQ[:, k, a:b].rearrange("p (m s) -> p m s", s=STEP)

            def wait_x(self, eng):
                if self.posts:
                    eng.wait_ge(x_updated, KD * self.posts)
                else:
                    eng.wait_ge(x_ready, KD)

            def vector(self, dve):
                self.rms.vector(dve)
                for k in range(KD):
                    nc.vector.tensor_tensor(SQ[:, k, 0:self.n], x[:, k, 0:self.n], rstd[:, 0:self.n],
                                            ALU.mult).then_inc(normed, 1)

            def tensor(self, pe):
                self.rms.tensor(pe)

            def scalar(self, act):
                self.rms.scalar(act)
                self.mod.wait(act)
                for k in range(KD):
                    act.wait_ge(normed, KD * self.u + k + 1)
                    for s, a, b in segments(self.n):
                        last = nc.scalar.activation(self.dst(k, a, b), self.src(k, a, b), ACT.Identity,
                                                    bias=self.mod.shift(self.ffn, k, s),
                                                    scale=self.mod.factor(2 if self.ffn else 0, k, s))
                    last.then_inc(h_ready, 1)

            def wait(self, eng, k=KD - 1):
                eng.wait_ge(h_ready, KD * self.u + k + 1)

        Y = area(KD * TOK, KD, TOK)
        y_normed = sem("y_normed")

        class PostNorm:

            def __init__(self, mod, ffn, n, y_ready):
                self.mod, self.ffn, self.n = mod, ffn, n
                self.u = n_post[0]
                n_post[0] += 1
                self.rms = Rms(Y, KD, n, SQ, y_ready, D)

            def scalar(self, act):
                self.rms.scalar(act)

            def tensor(self, pe):
                self.rms.tensor(pe)

            def vector(self, dve):
                self.rms.vector(dve)
                n = self.n
                self.mod.wait(dve)

                def norm(k):
                    nc.vector.tensor_tensor(SQ[:, k, 0:n], Y[:, k, 0:n], rstd[:, 0:n], ALU.mult).then_inc(y_normed, 1)
                norm(0)
                for k in range(KD):
                    if k + 1 < KD:
                        norm(k + 1)
                    dve.wait_ge(y_normed, KD * self.u + k + 1)
                    for s, a, b in segments(n):
                        last = nc.vector.scalar_tensor_tensor(x[:, k, a:b], SQ[:, k, a:b],
                                                              self.mod.factor(3 if self.ffn else 1, k, s),
                                                              x[:, k, a:b], ALU.mult, ALU.add)
                    last.then_inc(x_updated, 1)

            def wait(self, eng, k=KD - 1):
                eng.wait_ge(x_updated, KD * self.u + k + 1)

        class Linear:

            def __init__(self, name, w, kk, c0, cols, rhs, n, ready, move, width=256):
                self.mm, self.moved = sem(name + "_summed"), sem(name + "_moved")
                self.kk, self.rhs, self.n, self.ready, self.move = kk, rhs, n, ready, move
                self.width = width
                self.w = Weights([[cols_of(w, c0 + i * width, width)] for i in range(cols // width)],
                                 lambda i: (self.mm, width // P * (i + 1)))
                self.chunks = cols // P

            def tensor(self, pe):
                self.ready(pe)
                per = self.width // P
                for c in range(self.chunks):
                    i, q = divmod(c, per)
                    if q == 0:
                        self.w.wait(pe, i)
                    v = self.w.view(i, self.kk, self.width)
                    if c >= 4:
                        pe.wait_ge(self.moved, c - 3)
                    for k in range(self.kk):
                        last = nc.tensor.matmul(bank[c % 4][:, 0:self.n], v[:, k, q * P:(q + 1) * P], self.rhs(k),
                                                start=(k == 0), stop=(k == self.kk - 1))
                    last.then_inc(self.mm, 1)

            def scalar(self, act):
                for c in range(self.chunks):
                    act.wait_ge(self.mm, c + 1)
                    self.move(act, c, bank[c % 4]).then_inc(self.moved, 1)

            def wait(self, eng, c=None):
                eng.wait_ge(self.moved, (self.chunks if c is None else c + 1))

        def to_y(n, bias=None):
            def move(act, c, b):
                if bias is None:
                    return nc.scalar.activation(Y[:, c, 0:n], b[:, 0:n], ACT.Copy)
                return nc.scalar.activation(Y[:, c, 0:n], b[:, 0:n], ACT.Identity, bias=vcol(bias, c))
            return move

        GT = area(2 * KD * TOK, KF, TOK)

        class Ffn:

            def __init__(self, layer, n, pre):
                self.n, self.pre = n, pre
                self.ab = sem(f"ffn{layer}_summed")
                self.silu = sem(f"ffn{layer}_silu")
                self.g = sem(f"ffn{layer}_gated")
                w = A["ffn_w13"][layer]
                self.w = Weights([[cols_of(w, t * FFN + i * 256, 256) for t in range(2)] for i in range(KF // 2)],
                                 lambda i: (self.ab, 4 * (i + 1)))
                self.silus = area(0, 2, TOK)
                self.down = Linear(f"ffn{layer}_down", A["ffn_w2"][layer], KF, 0, D, lambda k: GT[:, k, 0:n], n,
                                   lambda pe: pe.wait_ge(self.g, KF), to_y(n))

            def tensor(self, pe):
                n = self.n
                self.pre.wait(pe)
                for f in range(KF):
                    i, q = divmod(f, 2)
                    if q == 0:
                        self.w.wait(pe, i)
                    v = self.w.slot(i)[:, 0:2 * KD * 256].rearrange("p (t k f) -> p t k f", t=2, f=256)
                    if f >= 2:
                        pe.wait_ge(self.g, f - 1)
                    for t in range(2):
                        for k in range(KD):
                            last = nc.tensor.matmul(bank[2 * (f % 2) + t][:, 0:n], v[:, t, k, q * P:(q + 1) * P],
                                                    h[:, k, 0:n], start=(k == 0), stop=(k == KD - 1))
                        last.then_inc(self.ab, 1)
                self.down.tensor(pe)

            def scalar(self, act):
                n = self.n
                for f in range(KF):
                    act.wait_ge(self.ab, 2 * f + 1)
                    if f >= 2:
                        act.wait_ge(self.g, f - 1)
                    nc.scalar.activation(self.silus[:, f % 2, 0:n], bank[2 * (f % 2)][:, 0:n], ACT.Silu).then_inc(self.silu, 1)
                self.down.scalar(act)

            def vector(self, dve):
                n = self.n
                for f in range(KF):
                    dve.wait_ge(self.ab, 2 * f + 2)
                    dve.wait_ge(self.silu, f + 1)
                    nc.vector.tensor_tensor(GT[:, f, 0:n], self.silus[:, f % 2, 0:n], bank[2 * (f % 2) + 1][:, 0:n],
                                            ALU.mult).then_inc(self.g, 1)
        class Mla:

            def __init__(self, pre, n_in, n):
                self.pre = pre
                at = KD * TOK
                self.z = area(at, 8, TOK)
                at = 2 * KD * TOK
                self.v = area(at, 4, D)
                self.kn = area(at + 4096, HEADS, TOK)
                self.qn = area(at + 8192, HEADS, TOK)
                self.qr = area(at + 12288, HEADS, TOK)
                self.qrot = area(at + 16384, HEADS, LAT)
                self.kr = area(at + 18432, TOK)
                self.krot = area(at + 18944, LAT)
                self.tab = area(at + 19200, 2, LAT)
                self.turn = area(at + 19712, ROPE)
                self.tmp = area(at + 19776, 2, 2, LAT)
                self.e = area(at + 20800, 2, TOK)
                self.pt = area(at + 21824, 2, TOK)
                self.mx = small[:, 0:2]
                self.sm = small[:, 2:4]
                self.loaded = sem("mla_tables_loaded")
                w = A["mla_w_in"][0]
                self.z_summed, self.z_moved = sem("mla_z_summed"), sem("mla_z_moved")
                self.win = Weights([[cols_of(w, i * 256, 256)] for i in range(4)] + [[cols_of(w, 1024, ROPE)]],
                                   lambda i: (self.z_summed, min(2 * (i + 1), 9)))
                self.rms_q = Rms(self.z, 6, TOK, SQ, lambda eng, k: eng.wait_ge(self.z_moved, k + 1), QR)
                self.zn, self.z_ready = sem("mla_z_normed"), sem("mla_z_ready")
                self.rms_kv = Rms(self.z[:, 6:8, :], 2, TOK, SQ[:, 6:8, :], lambda eng, k: eng.wait_ge(self.z_moved, k + 7), KVR)
                self.q_summed, self.q_moved = sem("mla_q_summed"), sem("mla_q_moved")
                self.wuq = Weights([[cols_of(A["mla_w_uq"][0], i * 384, 384)] for i in range(4)],
                                   lambda i: (self.q_summed, 4 * (i + 1)))
                self.kv_summed, self.kv_moved = sem("mla_kv_summed"), sem("mla_kv_moved")
                self.wukv = Weights([[cols_of(A["mla_w_ukv"][0], 0, 2048)]], lambda i: (self.kv_summed, 16))
                self.turned, self.rot = sem("mla_turned"), sem("mla_rotated")
                self.rot_step = sem("mla_rot_step")
                self.scored, self.maxed, self.negated = sem("mla_scored"), sem("mla_maxed"), sem("mla_negated")
                self.exped, self.recip, self.probs = sem("mla_exped"), sem("mla_recip"), sem("mla_probs")
                self.p_turned, self.p_moved = sem("mla_p_turned"), sem("mla_p_moved")
                self.o_summed, self.o_moved = sem("mla_o_summed"), sem("mla_o_moved")
                self.proj = Linear("mla_out", A["mla_w_o"][0], KD, 0, D, lambda k: h[:, k, :], TOK,
                                   lambda pe: pe.wait_ge(self.o_moved, 32), to_y(TOK))
                self.y_ready = lambda eng, k: self.proj.wait(eng, k)
                self.units = [(hd, qb, 0 if qb < 2 else LAT, 4 if qb < 2 else 2) for hd in range(HEADS) for qb in range(4)]

            def gpsimd(self, pool):
                pool.wait_ge(x_ready, KD)
                pool.dma_start(self.tab[0:ROPE], A["k_rope"]).then_inc(self.loaded, 16)
                pool.dma_start(self.turn[0:ROPE], A["k_turn"]).then_inc(self.loaded, 16)

            def tensor(self, pe):
                self.pre.wait(pe)
                for c in range(9):
                    if c % 2 == 0:
                        self.win.wait(pe, c // 2)
                    m = ROPE if c == 8 else P
                    v = self.win.view(c // 2, KD, ROPE if c == 8 else 256)
                    if c >= 4:
                        pe.wait_ge(self.z_moved, c - 3)
                    for k in range(KD):
                        last = nc.tensor.matmul(bank[c % 4][0:m, :], v[:, k, (c % 2) * P:(c % 2) * P + m], h[:, k, :],
                                                start=(k == 0), stop=(k == KD - 1))
                    last.then_inc(self.z_summed, 1)
                self.rms_q.tensor(pe)
                self.rms_kv.tensor(pe)
                pe.wait_ge(self.z_ready, 6)
                for c in range(16):
                    hd, part = divmod(c, 2)
                    if c % 4 == 0:
                        self.wuq.wait(pe, c // 4)
                    v = self.wuq.view(c // 4, 6, 384)
                    c0 = (hd % 2) * 192 + part * P
                    m = ROPE if part else P
                    if c < 4:
                        pe.wait_ge(self.z_moved, 9)
                    else:
                        pe.wait_ge(self.q_moved, c - 3)
                    for k in range(6):
                        last = nc.tensor.matmul(bank[c % 4][0:m, :], v[:, k, c0:c0 + m], self.z[:, k, :],
                                                start=(k == 0), stop=(k == 5))
                    last.then_inc(self.q_summed, 1)
                pe.wait_ge(self.z_ready, 8)
                self.wukv.wait(pe, 0)
                wv = self.wukv.view(0, 2, 2048)
                for c in range(16):
                    if c < 4:
                        pe.wait_ge(self.q_moved, 13 + c)
                    else:
                        pe.wait_ge(self.kv_moved, c - 3)
                    for k in range(2):
                        if c < 8:
                            last = nc.tensor.matmul(bank[c % 4][:, :], wv[:, k, c * 256:c * 256 + P], self.z[:, 6 + k, :],
                                                    start=(k == 0), stop=(k == 1))
                        else:
                            t, half = divmod(c - 8, 2)
                            vals = wv[:, k, half * 1024:(half + 1) * 1024].rearrange("p (h n) -> p h n", n=256)[:, :, P:256]
                            last = nc.tensor.matmul(bank[c % 4][:, :].rearrange("p (h n) -> p h n", n=P),
                                                    self.z[:, 6 + k, t * P:(t + 1) * P], vals, start=(k == 0), stop=(k == 1))
                    last.then_inc(self.kv_summed, 1)
                pe.wait_ge(self.loaded, 32)
                for i in range(9):
                    if i >= 2:
                        pe.wait_ge(self.rot, i - 1)
                    src = self.kr[0:ROPE, 0:LAT] if i == 0 else self.qr[0:ROPE, i - 1, 0:LAT]
                    nc.tensor.matmul(bank[4 + i % 2][0:ROPE, 0:LAT], self.turn[0:ROPE, :], src,
                                     start=True, stop=True).then_inc(self.turned, 1)

                def scores(u):
                    hd, qb, k0, nk = self.units[u]
                    if u < 2:
                        pe.wait_ge(self.kv_moved, 16)
                        pe.wait_ge(self.rot, 9)
                    else:
                        pe.wait_ge(self.exped, u - 1)
                    b = bank[u % 2]
                    q = slice(qb * P, (qb + 1) * P)
                    if qb < 2:
                        nc.tensor.matmul(b[:, :], self.qn[:, hd, q], self.kn[:, hd, :], start=True, stop=False)
                        nc.tensor.matmul(b[:, 0:LAT], self.qrot[0:ROPE, hd, q], self.krot[0:ROPE, :], start=False, stop=False)
                        nc.tensor.matmul(b[:, LAT:TOK], self.qr[0:ROPE, hd, q], self.kr[0:ROPE, LAT:TOK],
                                         start=False, stop=True).then_inc(self.scored, 1)
                    else:
                        nc.tensor.matmul(b[:, 0:LAT], self.qn[:, hd, q], self.kn[:, hd, LAT:TOK], start=True, stop=False)
                        nc.tensor.matmul(b[:, 0:LAT], self.qr[0:ROPE, hd, q], self.kr[0:ROPE, LAT:TOK],
                                         start=False, stop=True).then_inc(self.scored, 1)

                def weigh(u):
                    hd, qb, k0, nk = self.units[u]
                    pe.wait_ge(self.probs, u + 1)
                    if u >= 2:
                        pe.wait_ge(self.p_moved, u - 1)
                    for j in range(nk):
                        last = nc.tensor.transpose(bank[2 + u % 2][:, j * P:(j + 1) * P], self.e[:, u % 2, j * P:(j + 1) * P], ident[:, :])
                    last.then_inc(self.p_turned, 1)

                def values(u):
                    hd, qb, k0, nk = self.units[u]
                    pe.wait_ge(self.p_moved, u + 1)
                    if u >= 2:
                        pe.wait_ge(self.o_moved, u - 1)
                    for j in range(nk):
                        last = nc.tensor.matmul(bank[4 + u % 2][:, 0:P], self.v[:, k0 // P + j, hd * P:(hd + 1) * P],
                                                self.pt[:, u % 2, j * P:(j + 1) * P], start=(j == 0), stop=(j == nk - 1))
                    last.then_inc(self.o_summed, 1)
                n = len(self.units)
                scores(0)
                scores(1)
                for u in range(n):
                    weigh(u)
                    if u + 2 < n:
                        scores(u + 2)
                    if u >= 1:
                        values(u - 1)
                values(n - 1)
                self.proj.tensor(pe)

            def scalar(self, act):
                for c in range(9):
                    act.wait_ge(self.z_summed, c + 1)
                    dst = self.kr[0:ROPE, :] if c == 8 else self.z[:, c, :]
                    m = ROPE if c == 8 else P
                    nc.scalar.activation(dst, bank[c % 4][0:m, :], ACT.Copy).then_inc(self.z_moved, 1)
                self.rms_q.scalar(act)
                for k in range(6):
                    act.wait_ge(self.zn, k + 1)
                    nc.scalar.activation(self.z[:, k, :], self.z[:, k, :], ACT.Copy, scale=vcol("mla_q_norm_g", k)).then_inc(self.z_ready, 1)
                self.rms_kv.scalar(act)
                for k in range(2):
                    act.wait_ge(self.zn, 6 + k + 1)
                    nc.scalar.activation(self.z[:, 6 + k, :], self.z[:, 6 + k, :], ACT.Copy, scale=vcol("mla_kv_norm_g", k)).then_inc(self.z_ready, 1)
                for c in range(16):
                    act.wait_ge(self.q_summed, c + 1)
                    hd, part = divmod(c, 2)
                    dst, m = (self.qr[0:ROPE, hd, :], ROPE) if part else (self.qn[:, hd, :], P)
                    nc.scalar.activation(dst, bank[c % 4][0:m, :], ACT.Copy).then_inc(self.q_moved, 1)
                for c in range(16):
                    act.wait_ge(self.kv_summed, c + 1)
                    if c < 8:
                        dst = self.kn[:, c, :]
                    else:
                        t, half = divmod(c - 8, 2)
                        dst = self.v[:, t, half * 512:(half + 1) * 512]
                    nc.scalar.activation(dst, bank[c % 4][:, :], ACT.Copy).then_inc(self.kv_moved, 1)
                scale = float((NOPE + ROPE) ** -0.5)

                def out(u):
                    hd, qb, k0, nk = self.units[u]
                    act.wait_ge(self.o_summed, u + 1)
                    nc.scalar.activation(h[:, hd, qb * P:(qb + 1) * P], bank[4 + u % 2][:, 0:P], ACT.Copy).then_inc(self.o_moved, 1)
                for u, (hd, qb, k0, nk) in enumerate(self.units):
                    act.wait_ge(self.negated, u + 1)
                    if u >= 2:
                        act.wait_ge(self.p_turned, u - 1)
                    nc.scalar.activation(self.e[:, u % 2, 0:nk * P], bank[u % 2][:, 0:nk * P], ACT.Exp, bias=self.mx[:, u % 2:u % 2 + 1],
                                         scale=scale, accum_out=self.sm[:, u % 2:u % 2 + 1]).then_inc(self.exped, 1)
                    if u >= 2:
                        out(u - 2)
                out(len(self.units) - 2)
                out(len(self.units) - 1)
                self.proj.scalar(act)

            def vector(self, dve):
                self.rms_q.vector(dve)
                for k in range(6):
                    nc.vector.tensor_tensor(self.z[:, k, :], self.z[:, k, :], rstd[:, :], ALU.mult).then_inc(self.zn, 1)
                dve.wait_ge(self.zn, 6)
                self.rms_kv.vector(dve)
                for k in range(2):
                    nc.vector.tensor_tensor(self.z[:, 6 + k, :], self.z[:, 6 + k, :], rstd[:, :], ALU.mult).then_inc(self.zn, 1)
                cos, sin = self.tab[0:ROPE, 0, :], self.tab[0:ROPE, 1, :]
                dve.wait_ge(self.loaded, 32)
                for i in range(9):
                    src = self.kr[0:ROPE, 0:LAT] if i == 0 else self.qr[0:ROPE, i - 1, 0:LAT]
                    dst = self.krot[0:ROPE, :] if i == 0 else self.qrot[0:ROPE, i - 1, :]
                    dve.wait_ge(self.turned, i + 1)
                    if i >= 2:
                        dve.wait_ge(self.rot, i - 1)
                    nc.vector.tensor_tensor(self.tmp[0:ROPE, i % 2, 0, :], bank[4 + i % 2][0:ROPE, 0:LAT], sin, ALU.mult).then_inc(self.rot_step, 1)
                    nc.vector.tensor_tensor(self.tmp[0:ROPE, i % 2, 1, :], src, cos, ALU.mult).then_inc(self.rot_step, 1)
                    dve.wait_ge(self.rot_step, 2 * i + 2)
                    nc.vector.tensor_tensor(dst, self.tmp[0:ROPE, i % 2, 0, :], self.tmp[0:ROPE, i % 2, 1, :], ALU.add).then_inc(self.rot, 1)
                scale = float((NOPE + ROPE) ** -0.5)
                n = len(self.units)

                def peak(u):
                    hd, qb, k0, nk = self.units[u]
                    dve.wait_ge(self.scored, u + 1)
                    nc.vector.reduce_max(self.mx[:, u % 2:u % 2 + 1], bank[u % 2][:, 0:nk * P], axis=AX.X).then_inc(self.maxed, 1)
                    dve.wait_ge(self.maxed, u + 1)
                    nc.vector.tensor_scalar(self.mx[:, u % 2:u % 2 + 1], self.mx[:, u % 2:u % 2 + 1], -scale, None, ALU.mult).then_inc(self.negated, 1)
                peak(0)
                peak(1)
                for u, (hd, qb, k0, nk) in enumerate(self.units):
                    dve.wait_ge(self.exped, u + 1)
                    nc.vector.reciprocal(self.sm[:, u % 2:u % 2 + 1], self.sm[:, u % 2:u % 2 + 1]).then_inc(self.recip, 1)
                    dve.wait_ge(self.recip, u + 1)
                    nc.vector.tensor_scalar(self.e[:, u % 2, 0:nk * P], self.e[:, u % 2, 0:nk * P], self.sm[:, u % 2:u % 2 + 1],
                                            None, ALU.mult).then_inc(self.probs, 1)
                    if u + 2 < n:
                        peak(u + 2)
                    dve.wait_ge(self.p_turned, u + 1)
                    if u >= 2:
                        dve.wait_ge(self.o_summed, u - 1)
                    nc.vector.tensor_copy(self.pt[:, u % 2, 0:nk * P], bank[2 + u % 2][:, 0:nk * P]).then_inc(self.p_moved, 1)

        class Hyena:

            SEQS = 2
            SIN_STEPS = 6

            def __init__(self, pre, n_in, n):
                self.pre = pre
                self.pad = area(0, 2, 2, LAT + 2)
                self.w3 = area(2048, 2 * D)
                self.absh = area(0, 4, D)
                self.tmp = area(0, 4, 512)
                self.zt = area(4096, LAT)
                self.w1 = area(4352, WIDTH)
                self.w2 = area(4416, 2, WIDTH)
                self.fcol = area(4544, 8)
                self.a = area(4608, LAT)
                self.k = area(4864, LAT)
                self.sd = area(4096, 2, 2, D)
                self.u = area(8192, 24, TOK)
                self.v = area(8192 + 16 * TOK, 8, TOK)
                self.vt = area(8192 + 8 * TOK, 4, D)
                self.kf = area(20480, 4, D)
                self.dec = area(20480, 2, D)
                self.hfb = area(24576, 2, 2, D)
                self.prod = area(24576, 4, D)
                self.cs = area(28672, 2, 2, LAT)
                self.ics = area(29696, 2, 2, LAT)
                self.loaded, self.loaded2 = sem("hy_small_loaded"), sem("hy_tables_loaded")
                self.padded = sem("hy_pads_zeroed")
                self.u_summed, self.u_moved, self.conv_step = sem("hy_u_summed"), sem("hy_u_moved"), sem("hy_conv_step")
                self.conv = sem("hy_convolved")
                self.win = Weights([[cols_of(A["hy_w_in"][0], i * 256, 256)] for i in range(12)],
                                   lambda i: (self.u_summed, 2 * (i + 1)))
                self.v_gated, self.v_turned, self.v_moved = sem("hy_v_gated"), sem("hy_v_turned"), sem("hy_v_moved")
                self.f_summed, self.f_step, self.f_sin = sem("hy_f_summed"), sem("hy_f_step"), sem("hy_f_sin")
                self.t_summed, self.t_decayed, self.t_masked = sem("hy_taps_summed"), sem("hy_taps_decayed"), sem("hy_taps_masked")
                self.t_abs, self.t_norm, self.t_inv, self.t_mixed = sem("hy_taps_abs"), sem("hy_taps_normed"), sem("hy_taps_inverse"), sem("hy_taps_mixed")
                self.k_summed, self.k_moved = sem("hy_k_summed"), sem("hy_k_moved")
                self.s_summed, self.s_prod, self.s_step = sem("hy_spectrum_summed"), sem("hy_spectrum_product"), sem("hy_product_step")
                self.y_summed, self.y_scaled, self.y_skip, self.y_gated = sem("hy_y_summed"), sem("hy_y_scaled"), sem("hy_y_skip"), sem("hy_y_gated")
                self.ytmp = area(2048, 2, LAT)
                self.proj = Linear("hy_out", A["hy_w_out"][0], KD, 0, D, lambda k: h[:, k, :], TOK,
                                   lambda pe: pe.wait_ge(self.y_gated, 16), to_y(TOK, "hy_b_out"))
                self.y_ready = lambda eng, k: self.proj.wait(eng, k)

            def gpsimd(self, pool):
                self.pre.wait(pool)
                one = lambda v: v.rearrange("(p o) -> p o", o=1)
                with nc.allow_non_contiguous_dma(reason="64 words"):
                    for j, v in enumerate([A["hy_f_b1"][0], A["hy_f_b2"][0, 0], A["hy_f_b2"][0, 1], A["hy_f_freq"][0]]):
                        pool.dma_start(self.fcol[0:WIDTH, j:j + 1], one(v)).then_inc(self.loaded, 16)
                pool.dma_start(self.zt[0:EMB, :], A["k_hyena_z"]).then_inc(self.loaded, 16)
                pool.dma_start(self.w1[0:EMB, :], A["hy_f_w1"][0]).then_inc(self.loaded, 16)
                pool.dma_start(self.w2[0:WIDTH], A["hy_f_w2"][0].rearrange("i p n -> p i n")).then_inc(self.loaded, 16)
                pool.dma_start(self.w3[0:WIDTH], A["hy_f_w3"][0]).then_inc(self.loaded, 16)
                pool.dma_start(self.dec, A["k_hyena_decay"]).then_inc(self.loaded2, 16)
                pool.dma_start(self.cs, A["k_dft_odd"]).then_inc(self.loaded2, 16)
                pool.dma_start(self.ics, A["k_idft_odd"]).then_inc(self.loaded2, 16)
                for b in range(2):
                    nc.gpsimd.memset(self.pad[:, b, :, 0:1], 0.0).then_inc(self.padded, 1)
                    nc.gpsimd.memset(self.pad[:, b, :, LAT + 1:LAT + 2], 0.0).then_inc(self.padded, 1)

            def tensor(self, pe):
                self.pre.wait(pe)
                for c in range(24):
                    i, q = divmod(c, 2)
                    if q == 0:
                        self.win.wait(pe, i)
                    v = self.win.view(i, KD, 256)
                    if c >= 4:
                        pe.wait_ge(self.u_moved, c - 3)
                    for k in range(KD):
                        last = nc.tensor.matmul(bank[c % 4][:, :], v[:, k, q * P:(q + 1) * P], h[:, k, :],
                                                start=(k == 0), stop=(k == KD - 1))
                    last.then_inc(self.u_summed, 1)
                pe.wait_ge(self.loaded, 16 * 8)
                for r in range(3):
                    lhs = self.w1[0:EMB, :] if r == 0 else self.w2[0:WIDTH, r - 1, :]
                    rhs = self.zt[0:EMB, :] if r == 0 else self.a[0:WIDTH, :]
                    if r:
                        pe.wait_ge(self.f_sin, r)
                    nc.tensor.matmul(bank[5][0:WIDTH, 0:LAT], lhs, rhs, start=True, stop=True).then_inc(self.f_summed, 1)
                pe.wait_ge(self.u_moved, 24)
                pe.wait_ge(self.f_sin, 3)
                for n in range(8):
                    t, q = divmod(n, 4)
                    if n >= 4:
                        pe.wait_ge(self.t_decayed, n - 3)
                    nc.tensor.matmul(bank[n % 4][:, :], self.a[0:WIDTH, t * P:(t + 1) * P], self.w3[0:WIDTH, q * 512:(q + 1) * 512],
                                     start=True, stop=True).then_inc(self.t_summed, 1)
                pe.wait_ge(self.t_abs, 1)
                for c in range(KD):
                    for j in range(4):
                        last = nc.tensor.matmul(bank[5][:, c:c + 1], self.absh[:, j, c * P:(c + 1) * P], ones[:, 0:1],
                                                start=(j == 0), stop=(j == 3))
                last.then_inc(self.t_norm, 1)
                pe.wait_ge(self.t_mixed, 2)
                pe.wait_ge(self.loaded2, 48)
                for n in range(8):
                    part, fb, half = n // 4, n // 2 % 2, n % 2
                    if n >= 4:
                        pe.wait_ge(self.k_moved, n - 3)
                    for t in range(2):
                        last = nc.tensor.matmul(bank[n % 4][:, :], self.cs[:, part, t, fb * P:(fb + 1) * P],
                                                self.sd[:, part, t, half * 512:(half + 1) * 512], start=(t == 0), stop=(t == 1))
                    last.then_inc(self.k_summed, 1)
                pe.wait_ge(self.v_gated, KD)
                for n in range(8):
                    t, half = divmod(n, 2)
                    if n < 4:
                        pe.wait_ge(self.k_moved, 5 + n)
                    else:
                        pe.wait_ge(self.v_moved, n - 3)
                    for q in range(4):
                        last = nc.tensor.transpose(bank[n % 4][:, q * P:(q + 1) * P], self.v[:, 4 * half + q, t * P:(t + 1) * P], ident[:, :])
                    last.then_inc(self.v_turned, 1)
                for s in range(self.SEQS):
                    for n in range(4):
                        fb, half = divmod(n, 2)
                        m = 4 * s + n
                        if m == 0:
                            pe.wait_ge(self.v_moved, 8)
                        if m >= 2:
                            pe.wait_ge(self.s_prod, m - 1)
                        for part in range(2):
                            for t in range(2):
                                last = nc.tensor.matmul(bank[2 * (m % 2) + part][:, :], self.cs[:, part, t, fb * P:(fb + 1) * P],
                                                        self.vt[:, 2 * s + t, half * 512:(half + 1) * 512], start=(t == 0), stop=(t == 1))
                        last.then_inc(self.s_summed, 1)
                    for c in range(KD):
                        pe.wait_ge(self.s_prod, 4 * s + 4)
                        m = KD * s + c
                        if m >= 2:
                            pe.wait_ge(self.y_scaled, m - 1)
                        else:
                            pe.wait_ge(self.t_inv, 1)
                        for fb in range(2):
                            for part in range(2):
                                last = nc.tensor.matmul(bank[4 + m % 2][:, 0:LAT], self.prod[:, 2 * part + fb, c * P:(c + 1) * P],
                                                        self.ics[:, part, fb, :], start=(fb + part == 0), stop=(fb + part == 2))
                        last.then_inc(self.y_summed, 1)
                self.proj.tensor(pe)

            def scalar(self, act):
                act.wait_ge(self.padded, 4)
                for c in range(24):
                    act.wait_ge(self.u_summed, c + 1)
                    if c >= 2:
                        act.wait_ge(self.conv, c - 1)
                    nc.scalar.activation(self.pad[:, c % 2, :, 1:LAT + 1], bank[c % 4][:, :].rearrange("p (s t) -> p s t", s=2),
                                         ACT.Identity, bias=vcol("hy_b_in", c)).then_inc(self.u_moved, 1)
                for r in range(3):
                    act.wait_ge(self.f_step, self.SIN_STEPS * (r + 1))
                    nc.scalar.activation(self.a[0:WIDTH, :], self.a[0:WIDTH, :], ACT.Sin).then_inc(self.f_sin, 1)
                act.wait_ge(self.t_masked, 1)
                nc.scalar.activation(self.absh.rearrange("p a b -> p (a b)"), self.hfb.rearrange("p a b c -> p (a b c)"), ACT.Abs).then_inc(self.t_abs, 1)
                for n in range(8):
                    part, fb, half = n // 4, n // 2 % 2, n % 2
                    act.wait_ge(self.k_summed, n + 1)
                    nc.scalar.activation(self.kf[:, 2 * part + fb, half * 512:(half + 1) * 512], bank[n % 4][:, :], ACT.Copy).then_inc(self.k_moved, 1)
                for n in range(8):
                    t, half = divmod(n, 2)
                    act.wait_ge(self.v_turned, n + 1)
                    nc.scalar.activation(self.vt[:, t, half * 512:(half + 1) * 512], bank[n % 4][:, :], ACT.Copy).then_inc(self.v_moved, 1)
                act.wait_ge(self.t_inv, 1)
                for m in range(2 * KD):
                    s, c = divmod(m, KD)
                    act.wait_ge(self.y_summed, m + 1)
                    if m >= 2:
                        act.wait_ge(self.y_skip, m - 1)
                    nc.scalar.activation(self.ytmp[:, m % 2, :], bank[4 + m % 2][:, 0:LAT], ACT.Copy, scale=small[:, 8 + c:9 + c]).then_inc(self.y_scaled, 1)
                self.proj.scalar(act)

            def vector(self, dve):
                for c in range(24):
                    dve.wait_ge(self.u_moved, c + 1)
                    p, dst = self.pad[:, c % 2], self.u[:, c, :].rearrange("p (s t) -> p s t", s=2)
                    nc.vector.tensor_scalar(dst, p[:, :, 1:LAT + 1], vcol("hy_conv_w", 24 + c), vcol("hy_conv_b", c),
                                            ALU.mult, ALU.add).then_inc(self.conv_step, 1)
                    dve.wait_ge(self.conv_step, 2 * c + 1)
                    nc.vector.scalar_tensor_tensor(dst, p[:, :, 0:LAT], vcol("hy_conv_w", c), dst, ALU.mult, ALU.add).then_inc(self.conv_step, 1)
                    dve.wait_ge(self.conv_step, 2 * c + 2)
                    nc.vector.scalar_tensor_tensor(dst, p[:, :, 2:LAT + 2], vcol("hy_conv_w", 48 + c), dst, ALU.mult, ALU.add).then_inc(self.conv, 1)
                    if c >= 16:
                        dve.wait_ge(self.conv, c + 1)
                        nc.vector.tensor_tensor(self.u[:, c, :], self.u[:, c, :], self.u[:, c - 8, :], ALU.mult).then_inc(self.v_gated, 1)
                dve.wait_ge(self.loaded, 16 * 8)
                a, k = self.a[0:WIDTH, :], self.k[0:WIDTH, :]
                for r in range(3):
                    dve.wait_ge(self.f_summed, r + 1)
                    at = self.SIN_STEPS * r
                    nc.vector.tensor_scalar(a, bank[5][0:WIDTH, 0:LAT], self.fcol[0:WIDTH, r:r + 1], self.fcol[0:WIDTH, 3:4],
                                            ALU.add, ALU.mult).then_inc(self.f_step, 1)
                    dve.wait_ge(self.f_step, at + 1)
                    nc.vector.tensor_scalar(k, a, 1.0 / TWO_PI, ROUND, ALU.mult, ALU.add).then_inc(self.f_step, 1)
                    dve.wait_ge(self.f_step, at + 2)
                    nc.vector.tensor_scalar(k, k, -ROUND, None, ALU.add).then_inc(self.f_step, 1)
                    for n, c in enumerate((PI_HI, PI_MID)):
                        dve.wait_ge(self.f_step, at + 3 + n)
                        nc.vector.scalar_tensor_tensor(a, k, -c, a, ALU.mult, ALU.add).then_inc(self.f_step, 1)
                    dve.wait_ge(self.f_step, at + 5)
                    nc.vector.tensor_scalar(a, a, PI_IN, -PI_IN, ALU.min, ALU.max).then_inc(self.f_step, 1)
                dve.wait_ge(self.loaded2, 48)
                for n in range(8):
                    t, q = divmod(n, 4)
                    dr, half = divmod(q, 2)
                    dve.wait_ge(self.t_summed, n + 1)
                    nc.vector.tensor_tensor(self.hfb[:, t, dr, half * 512:(half + 1) * 512], bank[n % 4][:, :],
                                            self.dec[:, t, half * 512:(half + 1) * 512], ALU.mult).then_inc(self.t_decayed, 1)
                dve.wait_ge(self.t_decayed, 8)
                nc.vector.memset(self.hfb[0:1, 0, 1, :], 0.0).then_inc(self.t_masked, 1)
                dve.wait_ge(self.t_masked, 1)
                hf, hb = self.hfb[:, :, 0, :], self.hfb[:, :, 1, :]
                nc.vector.tensor_tensor(self.sd[:, 0], hf, hb, ALU.add).then_inc(self.t_mixed, 1)
                nc.vector.tensor_tensor(self.sd[:, 1], hb, hf, ALU.subtract).then_inc(self.t_mixed, 1)
                dve.wait_ge(self.t_norm, 1)
                nc.vector.reciprocal(small[:, 8:16], bank[5][:, 0:KD]).then_inc(self.t_inv, 1)
                dve.wait_ge(self.k_moved, 8)
                for s in range(self.SEQS):
                    for n in range(4):
                        fb, half = divmod(n, 2)
                        m = 4 * s + n
                        cols = slice(half * 512, (half + 1) * 512)
                        vr, vi = bank[2 * (m % 2)][:, :], bank[2 * (m % 2) + 1][:, :]
                        kr, ki = self.kf[:, fb, cols], self.kf[:, 2 + fb, cols]
                        dve.wait_ge(self.s_summed, m + 1)
                        if m == 4:
                            dve.wait_ge(self.y_summed, KD)
                        if m >= 1:
                            dve.wait_ge(self.s_prod, m)
                        nc.vector.tensor_tensor(self.tmp[:, 0, :], vr, kr, ALU.mult).then_inc(self.s_step, 1)
                        nc.vector.tensor_tensor(self.tmp[:, 1, :], vi, ki, ALU.mult).then_inc(self.s_step, 1)
                        nc.vector.tensor_tensor(self.tmp[:, 2, :], vr, ki, ALU.mult).then_inc(self.s_step, 1)
                        nc.vector.tensor_tensor(self.tmp[:, 3, :], vi, kr, ALU.mult).then_inc(self.s_step, 1)
                        dve.wait_ge(self.s_step, 5 * m + 2)
                        nc.vector.tensor_tensor(self.prod[:, fb, cols], self.tmp[:, 0, :], self.tmp[:, 1, :], ALU.add).then_inc(self.s_step, 1)
                        dve.wait_ge(self.s_step, 5 * m + 5)
                        nc.vector.tensor_tensor(self.prod[:, 2 + fb, cols], self.tmp[:, 2, :], self.tmp[:, 3, :], ALU.subtract).then_inc(self.s_prod, 1)
                    for c in range(KD):
                        m = KD * s + c
                        v = self.v[:, c, s * LAT:(s + 1) * LAT]
                        dve.wait_ge(self.y_scaled, m + 1)
                        nc.vector.scalar_tensor_tensor(v, v, vcol("hy_skip", c), self.ytmp[:, m % 2, :], ALU.mult, ALU.add).then_inc(self.y_skip, 1)
                        dve.wait_ge(self.y_skip, m + 1)
                        nc.vector.tensor_tensor(h[:, c, s * LAT:(s + 1) * LAT], v, self.u[:, c, s * LAT:(s + 1) * LAT], ALU.mult).then_inc(self.y_gated, 1)

        class S5:

            BATCH = 4
            NB = HALF // BATCH

            def __init__(self, pre, n_in, n):
                self.pre = pre
                self.u = area(0, GROUPS, 2 * CH)
                self.yf = area(0, KD, LAT)
                self.t = area(4096, 2, LAGS, GROUPS)
                self.b = area(6400, 2, GROUPS, GC)
                self.c = area(8448, 2, GROUPS, GC)
                self.f = area(10496, HALF, 2, P)
                self.m0 = area(18688, HALF, P)
                self.e = area(22784, HALF, 2, 2 * CH)
                self.pw = area(26880, self.BATCH, 2, P)
                self.et = area(27904, self.BATCH, 2, P)
                self.s2 = area(26880, HALF, 2, CH)
                self.t0 = area(28928, 512)
                self.gst = area(29440, self.BATCH, 240)
                self.mi = area(30400, 18, GROUPS)
                self.t1 = rstd
                self.lags = small[:, 20:20 + LAGS]
                self.rc = area(10496, 2, 8, P)
                self.rl = area(12544, 2, P)
                self.ldt = area(12800, GROUPS)
                self.rb = area(12864, 2, GROUPS, GC)
                self.w = area(14912, 5, LAGS, GROUPS)
                self.h_view = h[:, :, :].rearrange("p k (s z m) -> p (k s) z m", z=2, m=CH)
                s = lambda n: sem("s5_" + n)
                self.loaded, self.u_loaded, self.m_loaded, self.y_loaded = s("loaded"), s("u_loaded"), s("toeplitz_loaded"), s("y_loaded")
                self.turned, self.param, self.prep, self.act_prep = s("params_turned"), s("params_moved"), s("prep_step"), s("prep_act")
                self.in_step, self.in_ready, self.out_step, self.out_ready = s("in_step"), s("in_ready"), s("out_step"), s("out_ready")
                self.in_turned, self.et_moved = s("in_turned"), s("in_moved")
                self.g_summed, self.g_moved = s("taps_summed"), s("taps_moved")
                self.e_summed, self.e_moved = s("inject_summed"), s("inject_moved")
                self.step, self.s_moved = s("scan_step"), s("states_moved")
                self.y_summed, self.y_moved, self.skipped, self.gelu = s("y_summed"), s("y_moved"), s("skipped"), s("gelu")
                self.glu_summed, self.gate, self.glu = s("glu_summed"), s("glu_gate"), s("glu")
                self.w_glu = Weights([[cols_of(A["s5_w_glu"][0], t * D + i * 256, 256) for t in range(2)] for i in range(4)],
                                     lambda i: (self.glu_summed, 4 * (i + 1)))
                self.y_ready = lambda eng, k: eng.wait_ge(self.glu, k + 1)

            def sync(self, sp):
                sp_issue(sp, self.w_glu.p0 + RING)
                self.pre.wait(sp)
                for gl in range(8):
                    for st in range(STEP):
                        src = h[gl * GC:(gl + 1) * GC, :, st * 64:(st + 1) * 64]
                        dst = self.u[st * GC:(st + 1) * GC].rearrange("p (k g) j -> p k g j", g=8)[:, :, gl, :]
                        sp.dma_start(dst, src).then_inc(self.u_loaded, 16)
                for n in range(2 * self.NB):
                    hf, b = divmod(n, self.NB)
                    sp.wait_ge(self.g_moved, 2 * n + 2)
                    if n == self.NB:
                        sp.wait_ge(self.y_summed, 2)
                    for k in range(STEP):
                        sp.dma_start(self.m0[k * GC:(k + 1) * GC, b * self.BATCH:(b + 1) * self.BATCH, :],
                                     self.gst[0:GC, :, (7 - k) * GC:(7 - k) * GC + P]).then_inc(self.m_loaded, 16)
                sp.wait_ge(self.y_moved, 4)
                for gl in range(8):
                    for st in range(STEP):
                        src = h[st * GC:(st + 1) * GC, :, gl * 64 + CH:gl * 64 + 2 * CH]
                        dst = self.yf[gl * GC:(gl + 1) * GC, :, st * CH:(st + 1) * CH]
                        sp.dma_start(dst, src).then_inc(self.y_loaded, 16)

            def gpsimd(self, pool):
                self.pre.wait(pool)
                for i, (lam, cc, bb) in enumerate((("s5_lambda_re", "s5_c_re", "s5_b_re"), ("s5_lambda_im", "s5_c_im", "s5_b_im"))):
                    pool.dma_start(self.rl[0:GROUPS, i].rearrange("g (d s) -> g d s", d=2), A[lam][0].rearrange("d g s -> g d s")).then_inc(self.loaded, 16)
                    for d in range(2):
                        pool.dma_start(self.rc[:, i].rearrange("p k (d s) -> p k d s", d=2)[:, :, d, :],
                                       A[cc][0, d].rearrange("(k g) c s -> (g c) k s", k=8)).then_inc(self.loaded, 16)
                        pool.dma_start(self.rb[d * STATE:(d + 1) * STATE, i], A[bb][0, d].rearrange("g s c -> s g c")).then_inc(self.loaded, 16)
                for d in range(2):
                    pool.dma_start(self.ldt[d * STATE:(d + 1) * STATE], A["s5_log_dt"][0, d:d + 1, :].to_broadcast([STATE, GROUPS])).then_inc(self.loaded, 16)
                pool.dma_start(self.lags, A["k_s5_lags"]).then_inc(self.loaded, 16)
                pool.wait_ge(self.prep, self.PREP)
                for n in range(2 * self.NB):
                    hf, b = divmod(n, self.NB)
                    if n == self.NB:
                        pool.wait_ge(self.y_summed, 2)
                    g0 = n * self.BATCH
                    pr, pi = (self.lag(i, STEP, g0) for i in range(2))
                    cr, ci = (self.chan(self.c, i, g0) for i in range(2))
                    dst = [self.f[:, b * self.BATCH:(b + 1) * self.BATCH, i].rearrange("p g (s c) -> p g s c", c=GC) for i in range(2)]
                    t1 = self.t1[:, :].rearrange("p (g s c) -> p g s c", s=STEP, c=GC)
                    at = 6 * n
                    tt = nc.gpsimd.tensor_tensor
                    if n:
                        pool.wait_ge(self.out_step, at)
                    tt(dst[0], pr, cr, ALU.mult).then_inc(self.out_step, 1)
                    tt(dst[1], pr, ci, ALU.mult).then_inc(self.out_step, 1)
                    tt(t1, pi, ci, ALU.mult).then_inc(self.out_step, 1)
                    pool.wait_ge(self.out_step, at + 3)
                    tt(dst[0], dst[0], t1, ALU.add).then_inc(self.out_step, 1)
                    pool.wait_ge(self.out_step, at + 4)
                    tt(t1, pi, cr, ALU.mult).then_inc(self.out_step, 1)
                    pool.wait_ge(self.out_step, at + 5)
                    tt(dst[1], dst[1], t1, ALU.subtract).then_inc(self.out_step, 1)

            def lag(self, i, slot, g0):
                return self.t[:, i, slot:slot + STEP, g0:g0 + self.BATCH].rearrange("p s g -> p g s").unsqueeze(3) \
                    .to_broadcast([P, self.BATCH, STEP, GC])

            def chan(self, src, i, g0):
                return src[:, i, g0:g0 + self.BATCH, :].unsqueeze(2).to_broadcast([P, self.BATCH, STEP, GC])

            PREP = 43

            def vector(self, dve):
                V = nc.vector
                for i in range(2):
                    dve.wait_ge(self.turned, 1 + i)
                    V.tensor_copy(self.mi[:, i, :], bank[i][:, 0:GROUPS]).then_inc(self.param, 1)
                for n in range(4):
                    i, half = divmod(n, 2)
                    dve.wait_ge(self.turned, 3 + n)
                    dst = self.c[:, i, half * 32:(half + 1) * 32, :].rearrange("p g c -> p (g c)")
                    V.tensor_scalar(dst, bank[2 + n][:, :], -1.0 if i else 1.0, None, ALU.mult).then_inc(self.param, 1)
                dve.wait_ge(self.param, 6)
                dve.wait_ge(self.act_prep, 1)
                dve.wait_ge(self.loaded, 16 * 13)
                steps = [0]

                def then(ins):
                    steps[0] += 1
                    ins.then_inc(self.prep, 1)
                    dve.wait_ge(self.prep, steps[0])
                m = lambda j: self.mi[:, j, :]
                w = lambda j: self.w[:, j]
                lr, li, dt = m(0), m(1), m(2)
                lag3 = self.lags.unsqueeze(2).to_broadcast([P, LAGS, GROUPS])
                per = lambda v: v.unsqueeze(1).to_broadcast([P, LAGS, GROUPS])
                then(V.tensor_tensor(m(3), lr, dt, ALU.mult))
                then(V.tensor_tensor(m(4), li, dt, ALU.mult))
                then(V.tensor_tensor(w(0), lag3, per(m(3)), ALU.mult))
                then(V.tensor_tensor(w(1), lag3, per(m(4)), ALU.mult))
                then(V.tensor_scalar(w(2), w(1), 1.0 / TWO_PI, ROUND, ALU.mult, ALU.add))
                then(V.tensor_scalar(w(2), w(2), -ROUND, None, ALU.add))
                for c in (PI_HI, PI_MID, PI_LO):
                    then(V.scalar_tensor_tensor(w(1), w(2), -c, w(1), ALU.mult, ALU.add))
                then(V.tensor_scalar(w(1), w(1), PI_IN, -PI_IN, ALU.min, ALU.max))
                assert steps[0] == 10
                dve.wait_ge(self.act_prep, 5)
                then(V.tensor_tensor(w(4), w(2), w(2), ALU.mult))
                then(V.tensor_scalar(w(1), w(4), -2.0, 1.0, ALU.mult, ALU.add))
                then(V.tensor_tensor(self.t[:, 0], w(0), w(1), ALU.mult))
                then(V.tensor_tensor(self.t[:, 1], w(0), w(3), ALU.mult))
                e1, c1, q1 = self.w[:, 0, 16, :], self.w[:, 1, 16, :], self.w[:, 4, 16, :]
                then(V.scalar_tensor_tensor(m(5), e1, 1.0, m(5), ALU.add, ALU.mult))
                then(V.tensor_tensor(m(5), m(5), c1, ALU.mult))
                then(V.scalar_tensor_tensor(m(5), q1, -2.0, m(5), ALU.mult, ALU.add))
                xr, xi = m(5), self.t[:, 1, 16, :]
                then(V.tensor_tensor(m(8), lr, lr, ALU.mult))
                then(V.tensor_tensor(m(9), li, li, ALU.mult))
                then(V.tensor_tensor(m(8), m(8), m(9), ALU.add))
                then(V.reciprocal(m(8), m(8)))
                then(V.tensor_tensor(m(6), xr, lr, ALU.mult))
                then(V.tensor_tensor(m(9), xi, li, ALU.mult))
                then(V.tensor_tensor(m(6), m(6), m(9), ALU.add))
                then(V.tensor_tensor(m(6), m(6), m(8), ALU.mult))
                then(V.tensor_tensor(m(7), xi, lr, ALU.mult))
                then(V.tensor_tensor(m(9), xr, li, ALU.mult))
                then(V.tensor_tensor(m(7), m(7), m(9), ALU.subtract))
                then(V.tensor_tensor(m(7), m(7), m(8), ALU.mult))
                qr, qi = (m(j).unsqueeze(2).to_broadcast([P, GROUPS, GC]) for j in (6, 7))
                br, bi = self.rb[:, 0], self.rb[:, 1]
                tmp = self.w[:, 0:1].rearrange("p a b c -> p (a b c)")[:, 0:GROUPS * GC].rearrange("p (g c) -> p g c", c=GC)
                then(V.tensor_tensor(self.b[:, 0], qr, br, ALU.mult))
                then(V.tensor_tensor(tmp, qi, bi, ALU.mult))
                then(V.tensor_tensor(self.b[:, 0], self.b[:, 0], tmp, ALU.subtract))
                then(V.tensor_tensor(self.b[:, 1], qr, bi, ALU.mult))
                then(V.tensor_tensor(tmp, qi, br, ALU.mult))
                then(V.tensor_tensor(self.b[:, 1], self.b[:, 1], tmp, ALU.add))
                la = self.mi[:, 10:12, :].rearrange("p a g -> p (a g)").rearrange("p (g r) -> p g r", r=2)
                lb = self.mi[:, 12:14, :].rearrange("p a g -> p (a g)").rearrange("p (g r) -> p g r", r=2)
                l8r, l8i = self.t[:, 0, 17, :], self.t[:, 1, 17, :]
                then(V.tensor_copy(la[:, :, 0], l8r))
                then(V.tensor_copy(la[:, :, 1], l8r))
                then(V.tensor_copy(lb[:, :, 0], l8i))
                then(V.tensor_scalar(lb[:, :, 1], l8i, -1.0, None, ALU.mult))
                while steps[0] < self.PREP:
                    then(V.tensor_copy(m(14), m(0)))
                assert steps[0] == self.PREP, steps[0]
                t0 = self.t0[:, :].rearrange("p (g s c) -> p g s c", s=STEP, c=GC)
                for hf in range(2):
                    for b in range(self.NB):
                        n = hf * self.NB + b
                        g0 = n * self.BATCH
                        pr, pi = (self.lag(i, 0, g0) for i in range(2))
                        br, bi = (self.chan(self.b, i, g0) for i in range(2))
                        dst = [self.pw[:, :, i].rearrange("p g (s c) -> p g s c", c=GC) for i in range(2)]
                        at = 5 * n
                        if n:
                            dve.wait_ge(self.in_turned, 2 * n)
                        if b == 0 and hf:
                            dve.wait_ge(self.y_summed, 2)
                        tt = V.tensor_tensor
                        tt(dst[0], pr, br, ALU.mult).then_inc(self.in_step, 1)
                        tt(dst[1], pr, bi, ALU.mult).then_inc(self.in_step, 1)
                        tt(t0, pi, bi, ALU.mult).then_inc(self.in_step, 1)
                        dve.wait_ge(self.in_step, at + 3)
                        tt(dst[0], dst[0], t0, ALU.subtract).then_inc(self.in_step, 1)
                        dve.wait_ge(self.in_step, at + 4)
                        tt(t0, pi, br, ALU.mult).then_inc(self.in_step, 1)
                        dve.wait_ge(self.in_step, at + 5)
                        tt(dst[1], dst[1], t0, ALU.add).then_inc(self.in_ready, 1)
                        for q in range(2):
                            dve.wait_ge(self.g_summed, 2 * n + q + 1)
                            if n and q == 0:
                                dve.wait_ge(self.m_loaded, 16 * STEP * n)
                            taps = [bank[i + q][0:GC, 0:480].rearrange("p (g n) -> p g n", g=2) for i in (2, 5)]
                            V.tensor_copy(self.gst[0:GC, 2 * q:2 * q + 2, 0:112], taps[1][:, :, 0:112])
                            V.tensor_copy(self.gst[0:GC, 2 * q:2 * q + 2, 112:240], taps[0][:, :, 112:240]).then_inc(self.g_moved, 1)
                    dve.wait_ge(self.e_moved, 2 * self.NB * (hf + 1))
                    sa = la[:, hf * HALF:(hf + 1) * HALF, :]
                    sb_ = lb[:, hf * HALF:(hf + 1) * HALF, :]
                    ta = self.t0[:, 0:64].rearrange("p (g r) -> p g r", r=2)
                    tb = self.t0[:, 64:128].rearrange("p (g r) -> p g r", r=2)
                    base = 4 * (2 * CH - 1) * hf
                    with dve.Fori(1, 2 * CH) as i:
                        prev = self.e[:, :, :, bass.ds(i - 1, 1)].rearrange("p g r o -> p g (r o)")
                        cur = self.e[:, :, :, bass.ds(i, 1)].rearrange("p g r o -> p g (r o)")
                        V.tensor_tensor(ta, sa, prev, ALU.mult).then_inc(self.step, 1)
                        V.tensor_tensor(tb[:, :, ::-1], sb_, prev, ALU.mult).then_inc(self.step, 1)
                        dve.wait_ge(self.step, base + 4 * i - 2)
                        V.tensor_tensor(ta, ta, tb, ALU.add).then_inc(self.step, 1)
                        dve.wait_ge(self.step, base + 4 * i - 1)
                        V.tensor_tensor(cur, cur, ta, ALU.add).then_inc(self.step, 1)
                        dve.wait_ge(self.step, base + 4 * i)
                    V.tensor_copy(self.s2[0:STATE], self.e[0:STATE, :, :, CH - 1:2 * CH - 1]).then_inc(self.s_moved, 1)
                    V.tensor_copy(self.s2[STATE:P], self.e[STATE:P, :, :, 2 * CH - 2:CH - 2:-1]).then_inc(self.s_moved, 1)
                    for q in range(2):
                        dve.wait_ge(self.y_summed, 2 * hf + q + 1)
                        g0 = hf * HALF + q * 16
                        V.tensor_copy(self.h_view[:, g0:g0 + 16, 1, :], bank[5 + q][:, :].rearrange("p (g m) -> p g m", m=CH)).then_inc(self.y_moved, 1)
                dve.wait_ge(self.y_loaded, 16 * 64)
                for k in range(KD):
                    yv = self.yf[:, k, :].rearrange("p (s m) -> p s m", m=CH)
                    V.scalar_tensor_tensor(yv, self.h_view[:, k * 8:(k + 1) * 8, 0, :], vcol("s5_d", k), yv, ALU.mult, ALU.add).then_inc(self.skipped, 1)
                for c in range(KD):
                    dve.wait_ge(self.gate, c + 1)
                    dst = Y[:, c, 0:LAT].rearrange("p (m s) -> p s m", s=STEP)
                    V.scalar_tensor_tensor(dst, bank[2 * (c % 2)][:, 0:LAT].rearrange("p (s m) -> p s m", m=CH), vcol("s5_b_glu", c),
                                           self.sig[:, c % 2, :].rearrange("p (s m) -> p s m", m=CH), ALU.add, ALU.mult).then_inc(self.glu, 1)

            def tensor(self, pe):
                self.pre.wait(pe)
                pe.wait_ge(self.loaded, 16 * 13)
                for i in range(2):
                    nc.tensor.transpose(bank[i][:, 0:GROUPS], self.rl[0:GROUPS, i, :], ident[0:GROUPS, 0:GROUPS]).then_inc(self.turned, 1)
                for n in range(4):
                    i, half = divmod(n, 2)
                    for q in range(4):
                        last = nc.tensor.transpose(bank[2 + n][:, q * P:(q + 1) * P], self.rc[:, i, 4 * half + q, :], ident[:, :])
                    last.then_inc(self.turned, 1)
                pe.wait_ge(self.param, 6)
                pe.wait_ge(self.u_loaded, 16 * 64)
                for hf in range(2):
                    for b in range(self.NB):
                        n = hf * self.NB + b
                        g0 = n * self.BATCH
                        pe.wait_ge(self.in_ready, n + 1)
                        for q in range(2):
                            if n:
                                pe.wait_ge(self.et_moved, 2 * n)
                            for j in range(4):
                                last = nc.tensor.transpose(bank[q][:, j * P:(j + 1) * P], self.pw[:, 2 * q + j // 2, j % 2, :], ident[:, :])
                            last.then_inc(self.in_turned, 1)
                        pe.wait_ge(self.out_step, 6 * (n + 1))
                        for q in range(2):
                            if n:
                                pe.wait_ge(self.g_moved, 2 * n - 1 + q)
                            for j in range(2):
                                gb = 2 * q + j
                                g, gh = g0 + gb, b * self.BATCH + gb
                                if n == self.NB:
                                    pe.wait_ge(self.y_moved, 2)
                                for lo, hi, rows, rhs in (
                                        (112, 128, slice(0, P), lambda i: self.c[:, i, g, :]),
                                        (128, 240, slice(0, STATE), lambda i: self.f[0:STATE, gh, i, 0:112]),
                                        (0, 112, slice(STATE, P), lambda i: self.f[STATE:P, gh, i, 16:P])):
                                    for i in range(2):
                                        last = nc.tensor.matmul(bank[(2 if lo else 5) + q][0:GC, j * 240 + lo:j * 240 + hi], self.b[rows, i, g, :], rhs(i),
                                                                start=(i == 0), stop=(i == 1))
                            last.then_inc(self.g_summed, 1)
                        pe.wait_ge(self.et_moved, 2 * n + 2)
                        if n:
                            pe.wait_ge(self.e_moved, 2 * n)
                        for gb in range(self.BATCH):
                            for i in range(2):
                                o = (2 * gb + i) * 2 * CH
                                last = nc.tensor.matmul(bank[4][:, o:o + 2 * CH], self.et[:, gb, i, :], self.u[:, g0 + gb, :],
                                                        start=True, stop=True)
                        last.then_inc(self.e_summed, 1)
                    pe.wait_ge(self.m_loaded, 16 * STEP * self.NB * (hf + 1))
                    pe.wait_ge(self.s_moved, 2 * hf + 2)
                    for q in range(2):
                        for j in range(16):
                            gh = q * 16 + j
                            g = hf * HALF + gh
                            o = bank[5 + q][:, j * CH:(j + 1) * CH]
                            nc.tensor.matmul(o, self.m0[:, gh, :], self.u[:, g, 0:CH], start=True, stop=False)
                            nc.tensor.matmul(o, self.f[:, gh, 0, :], self.s2[:, gh, 0, :], start=False, stop=False)
                            last = nc.tensor.matmul(o, self.f[:, gh, 1, :], self.s2[:, gh, 1, :], start=False, stop=True)
                        last.then_inc(self.y_summed, 1)
                pe.wait_ge(self.gelu, KD)
                for c in range(KD):
                    i, q = divmod(c, 2)
                    if q == 0:
                        self.w_glu.wait(pe, i)
                    v = self.w_glu.slot(i)[:, 0:2 * KD * 256].rearrange("p (t k f) -> p t k f", t=2, f=256)
                    if c >= 2:
                        pe.wait_ge(self.glu, c - 1)
                    for t in range(2):
                        for k in range(KD):
                            last = nc.tensor.matmul(bank[2 * (c % 2) + t][:, 0:LAT], v[:, t, k, q * P:(q + 1) * P],
                                                    self.yf[:, k, :], start=(k == 0), stop=(k == KD - 1))
                        last.then_inc(self.glu_summed, 1)

            @property
            def sig(self):
                return area(22784, 2, LAT)

            def scalar(self, act):
                act.wait_ge(self.loaded, 16 * 13)
                nc.scalar.activation(self.mi[:, 2, :], self.ldt, ACT.Exp).then_inc(self.act_prep, 1)
                act.wait_ge(self.prep, 10)
                nc.scalar.activation(self.w[:, 0], self.w[:, 0], ACT.Exp).then_inc(self.act_prep, 1)
                nc.scalar.activation(self.mi[:, 5, :], self.mi[:, 3, :], ACT.Tanh, scale=0.5).then_inc(self.act_prep, 1)
                nc.scalar.activation(self.w[:, 2], self.w[:, 1], ACT.Sin, scale=0.5).then_inc(self.act_prep, 1)
                nc.scalar.activation(self.w[:, 3], self.w[:, 1], ACT.Sin).then_inc(self.act_prep, 1)
                for n in range(2 * self.NB):
                    hf, b = divmod(n, self.NB)
                    for q in range(2):
                        act.wait_ge(self.in_turned, 2 * n + q + 1)
                        if n:
                            act.wait_ge(self.e_summed, n)
                        if n == self.NB:
                            act.wait_ge(self.y_summed, 2)
                        nc.scalar.activation(self.et[:, 2 * q:2 * q + 2].rearrange("p g i n -> p (g i n)"), bank[q][:, :], ACT.Copy).then_inc(self.et_moved, 1)
                    act.wait_ge(self.e_summed, n + 1)
                    if n == self.NB:
                        act.wait_ge(self.s_moved, 2)
                    dst = self.e[:, b * self.BATCH:(b + 1) * self.BATCH]
                    src = bank[4][:, :].rearrange("p (g z m) -> p g z m", z=2, m=CH)
                    fw = dst[0:STATE].rearrange("p g r (z m) -> p (g r) z m", m=CH)
                    nc.scalar.activation(fw[:, :, ::-1, :], src[0:STATE], ACT.Copy).then_inc(self.e_moved, 1)
                    bw = dst[STATE:P].rearrange("p g r j -> p (g r) j")
                    nc.scalar.activation(bw[:, :, ::-1], bank[4][STATE:P, :].rearrange("p (g j) -> p g j", j=2 * CH), ACT.Copy).then_inc(self.e_moved, 1)
                for k in range(KD):
                    act.wait_ge(self.skipped, k + 1)
                    nc.scalar.activation(self.yf[:, k, :], self.yf[:, k, :], ACT.Gelu).then_inc(self.gelu, 1)
                for c in range(KD):
                    act.wait_ge(self.glu_summed, 2 * c + 2)
                    if c >= 2:
                        act.wait_ge(self.glu, c - 1)
                    nc.scalar.activation(self.sig[:, c % 2, :], bank[2 * (c % 2) + 1][:, 0:LAT], ACT.Sigmoid,
                                         bias=vcol("s5_b_glu", KD + c)).then_inc(self.gate, 1)

        class Fnet:

            def __init__(self, pre, n_in, n):
                self.pre = pre
                self.loaded, self.chan, self.chan_moved = sem("fn_loaded"), sem("fn_channels"), sem("fn_channels_moved")
                self.tok, self.tok_moved = sem("fn_tokens"), sem("fn_tokens_moved")
                at = 2 * KD * TOK
                self.cs = area(at, 2 * P)
                self.tt = area(at + 256, 2, 2, LAT)
                self.a = area(at + 1280, 2, KD, 2 * P)
                self.f = area(at + 1280 + 4096, KD, LAT)
                self.proj = Linear("fn_out", A["fn_w_o"][0], KD, 0, D, lambda k: self.f[:, k, :], LAT,
                                   lambda pe: pe.wait_ge(self.tok_moved, 4), to_y(LAT, "fn_b_o"))
                self.y_ready = lambda eng, k: self.proj.wait(eng, k)

            def sync(self, sp):
                sp_issue(sp, self.proj.w.p0 - MOD_PANELS)
                self.pre.wait_x(sp)
                sp.dma_start(self.cs, A["k_dft128"]).then_inc(self.loaded, 16)
                sp.dma_start(self.tt, A["k_dft256"]).then_inc(self.loaded, 16)

            def tensor(self, pe):
                self.pre.wait(pe)
                pe.wait_ge(self.loaded, 32)
                for t in range(2):
                    for g2 in range(KD // 2):
                        n = 4 * t + g2
                        if n >= 4:
                            pe.wait_ge(self.chan_moved, n - 3)
                        for q in range(2):
                            g = 2 * g2 + q
                            last = nc.tensor.matmul(bank[n % 4][:, q * 256:(q + 1) * 256], h[:, g, t * P:(t + 1) * P],
                                                    self.cs[:, :], start=True, stop=True)
                        last.then_inc(self.chan, 1)
                for g2 in range(KD // 2):
                    pe.wait_ge(self.chan_moved, 5 + g2)
                    for q in range(2):
                        g = 2 * g2 + q
                        for t in range(2):
                            for part in range(2):
                                last = nc.tensor.matmul(bank[g2][:, q * 256:(q + 1) * 256],
                                                        self.a[:, t, g, part * P:(part + 1) * P],
                                                        self.tt[:, part, t, :], start=(t + part == 0), stop=(t + part == 2))
                    last.then_inc(self.tok, 1)
                self.proj.tensor(pe)

            def vector(self, dve):
                for n in range(8):
                    t, g2 = divmod(n, 4)
                    dve.wait_ge(self.chan, n + 1)
                    nc.vector.tensor_copy(self.a[:, t, 2 * g2:2 * g2 + 2, :].rearrange("p g c -> p (g c)"), bank[n % 4][:, :]).then_inc(self.chan_moved, 1)
                for g2 in range(KD // 2):
                    dve.wait_ge(self.tok, g2 + 1)
                    nc.vector.tensor_copy(self.f[:, 2 * g2:2 * g2 + 2, :].rearrange("p g c -> p (g c)"), bank[g2][:, :]).then_inc(self.tok_moved, 1)

            def scalar(self, act):
                self.proj.scalar(act)

        MIXER = {0: Mla, 1: Hyena, 2: S5, 3: Fnet}
        stages = [Setup()]
        live = [l for l in range(DEPTH) if l in layers]
        for l in live:
            mod = Modulation(l)
            n_in = TOK if l < 3 else LAT
            n_out = TOK if l < 2 else LAT
            pre = PreNorm(mod, False, n_in, split=(l == 2))
            mixer = MIXER[l](pre, n_in, n_out)
            post = PostNorm(mod, False, n_out, mixer.y_ready)
            pre2 = PreNorm(mod, True, n_out)
            ffn = Ffn(l, n_out, pre2)
            post2 = PostNorm(mod, True, n_out, lambda eng, k, f=ffn: f.down.wait(eng, k))
            stages += [mod, pre, mixer, post, pre2, ffn, post2]

        out_turned = sem("out_turned")
        out_moved = sem("out_moved")
        stored = sem("stored")
        orow = area(2 * KD * TOK, 2, D)

        class Store:

            def tensor(self, pe):
                for t in range(2):
                    for half in range(2):
                        for q in range(4):
                            k = 4 * half + q
                            if t == 0:
                                post2.wait(pe, k)
                            last = nc.tensor.transpose(bank[2 * t + half][:, q * P:(q + 1) * P],
                                                       x[:, k, t * P:(t + 1) * P], ident[:, :])
                        last.then_inc(out_turned, 1)

            def vector(self, dve):
                for t in range(2):
                    for half in range(2):
                        dve.wait_ge(out_turned, 2 * t + half + 1)
                        nc.vector.tensor_copy(orow[:, t, half * 512:(half + 1) * 512], bank[2 * t + half][:, :]).then_inc(out_moved, 1)

            def sync(self, sp):
                for t in range(2):
                    sp.wait_ge(out_moved, 2 * t + 2)
                    sp.dma_start(out[0, t * P:(t + 1) * P, :], orow[:, t, :]).then_inc(stored, 16)
                sp.wait_ge(stored, 32)
        stages.append(Store())

        block = ctx.enter_context(nc.Block())

        @block.sync
        def _(sp):
            for s in stages[:-1]:
                if hasattr(s, "sync"):
                    s.sync(sp)
            sp_issue(sp, len(panels))
            stages[-1].sync(sp)

        @block.scalar
        def _(act):
            for s in stages:
                if hasattr(s, "scalar"):
                    s.scalar(act)

        @block.vector
        def _(dve):
            for s in stages:
                if hasattr(s, "vector"):
                    s.vector(dve)

        @block.gpsimd
        def _(pool):
            for s in stages:
                if hasattr(s, "gpsimd"):
                    s.gpsimd(pool)

        @block.tensor
        def _(pe):
            for s in stages:
                if hasattr(s, "tensor"):
                    s.tensor(pe)


def constants():
    f8 = np.float64
    c = {}
    ch = np.arange(P, dtype=f8)
    ang = 2 * np.pi * np.outer(ch, ch) / P
    c["k_dft128"] = np.concatenate([np.cos(ang), np.sin(ang)], axis=1) / math.sqrt(LAT * P)
    t = np.arange(LAT, dtype=f8)
    ang = 2 * np.pi * (np.outer(t, t) % LAT) / LAT
    c["k_dft256"] = np.stack([np.cos(ang), -np.sin(ang)]).reshape(2, 2, P, LAT).transpose(2, 0, 1, 3)
    tok = np.arange(LAT)
    freq = 1.0 / 10000.0 ** (np.arange(0, 32, 2, dtype=f8) / 32)
    row, col = np.outer(freq, tok // 64), np.outer(freq, tok % 64)
    ang = np.concatenate([row, row, col, col])
    c["k_rope"] = np.stack([np.cos(ang), np.sin(ang)], axis=1)
    turn = np.zeros((ROPE, ROPE))
    for b in (0, 32):
        for i in range(16):
            turn[b + 16 + i, b + i] = -1.0
            turn[b + i, b + 16 + i] = 1.0
    c["k_turn"] = turn
    f4 = np.float32
    tt = np.linspace(0.0, 1.0, LAT, dtype=f4)[:, None]
    w = f4(2.0 * math.pi / LAT) * np.arange(LAT, dtype=f4)[:, None]
    bands = np.linspace(1e-4, BANDS - 1, BANDS, dtype=f4)[None, :]
    c["k_hyena_z"] = np.concatenate([tt, np.cos(w * bands), -np.sin(w * bands)], axis=1).T
    deltas = np.abs(np.linspace(math.log(1e-2) / 1.5, math.log(1e-2) / 0.3, D, dtype=f4))
    c["k_hyena_decay"] = np.exp(-tt * deltas).reshape(2, P, D).transpose(1, 0, 2)
    ang = np.pi * (np.outer(t, 2 * np.arange(LAT) + 1) % (4 * LAT)) / (2 * LAT)
    cs = np.stack([np.cos(ang), np.sin(ang)])
    c["k_dft_odd"] = cs.reshape(2, 2, P, LAT).transpose(2, 0, 1, 3)
    ics = np.stack([cs[0].T, -cs[1].T]) / LAT
    c["k_idft_odd"] = ics.reshape(2, 2, P, LAT).transpose(2, 0, 1, 3)
    k = np.arange(STEP)
    fwd = np.concatenate([STEP - 1 - k, k + 1, [1, STEP]])
    bwd = np.concatenate([k, STEP - k, [1, STEP]])
    c["k_s5_lags"] = np.repeat(np.stack([fwd, bwd]), STATE, axis=0)
    return {k: np.ascontiguousarray(v.astype(np.float32)) for k, v in c.items()}


def kernel(**inputs):
    import concourse.bacc as bacc
    from concourse.bass_utils import run_bass_kernel_spmd

    nc = bacc.Bacc("TRN2", target_bir_lowering=False, num_devices=1)
    arrays = {name: np.ascontiguousarray(a) for name, a in inputs.items()}
    arrays.update(constants())
    A = {name: nc.dram_tensor(name, a.shape, mybir.dt.from_np(a.dtype), kind="ExternalInput").ap()
         for name, a in arrays.items()}
    out = nc.dram_tensor("out", (1, LAT, D), F32, kind="ExternalOutput").ap()
    build(nc, A, out)
    r = run_bass_kernel_spmd(nc, [arrays], core_ids=[0])
    return r.results[0]["out"]
```

```python
import math
from contextlib import ExitStack

import numpy as np

import concourse.bass as bass
from concourse import mybir

F32 = mybir.dt.float32
ACT = mybir.ActivationFunctionType
ALU = mybir.AluOpType
AX = mybir.AxisListType

P = 128
D = 1024
KD = D // P
LAT = 256
CTX = 256
TOK = LAT + CTX
DEPTH = 4
MODS = 6
FFN = 2816
KF = FFN // P
EPS = 1e-6

HEADS = 8
NOPE = 128
ROPE = 64
VDIM = 128
KVR = 256
QR = 768

BANDS = 16
EMB = 2 * BANDS + 1
WIDTH = 64

GROUPS = 64
GC = 16
STATE = 64
STEP = 8
CH = LAT // STEP
HALF = GROUPS // 2
BLK = 8
LAGS = 2 * STEP + 1 + BLK

RING = 4
SLOT = 11 * 256
ARENA = 31600

TWO_PI = 2.0 * math.pi
ROUND = 1.5 * 2.0 ** 23
PI_HI = 6.28125
PI_MID = float(np.float32(TWO_PI - PI_HI))
PI_LO = float(np.float32(TWO_PI - PI_HI - PI_MID))
PI_IN = 3.1415925

VEC = {}


def _rows():
    tiles = [
        [("mod_b01", 2 * MODS * KD)],
        [("mod_b23", 2 * MODS * KD)],
        [("mix_pre_g", DEPTH * KD), ("mix_post_g", DEPTH * KD), ("ffn_pre_g", DEPTH * KD), ("ffn_post_g", DEPTH * KD)],
        [("hy_b_in", 24), ("hy_conv_w", 72), ("hy_conv_b", 24)],
        [("hy_skip", 8), ("hy_b_out", 8), ("s5_d", 8), ("s5_b_glu", 16), ("fn_b_o", 8),
         ("mla_q_norm_g", 6), ("mla_kv_norm_g", 2), ("c", 8), ("c_ctx", 8)],
    ]
    for t, rows in enumerate(tiles):
        at = 0
        for name, n in rows:
            VEC[name] = (t, at, n)
            at += n
    return [sum(n for _, n in rows) for rows in tiles]


VEC_ROWS = _rows()


def build(nc, A, out, layers=(0, 1, 2, 3)):
    ctx = ExitStack()
    with ctx:
        def sb(name, shape):
            return ctx.enter_context(nc.sbuf_tensor(name, shape, F32))

        def sem(name):
            return ctx.enter_context(nc.semaphore(name))

        x = sb("x_sb", [P, KD, TOK])
        h = sb("h_sb", [P, KD, TOK])
        arena = sb("arena", [P, ARENA])
        ring = sb("ring", [P, RING, SLOT])
        vec = sb("vec", [P, 5, P])
        rstd = sb("rstd", [P, TOK])
        ident = sb("ident", [P, P])
        ones = sb("ones", [P, P])
        silu_c = sb("silu_c", [P, KD, 2])
        modv = sb("modv", [P, 2, MODS * KD, 2])
        affine = sb("affine", [P, 2, 6, KD, 2])
        small = sb("small", [P, 64])
        bank = [ctx.enter_context(nc.psum_tensor(f"bank{i}", [P, 512], F32)) for i in range(8)]
        SUMS, MODP = bank[6], bank[7]

        used = [0]

        def area(at, *dims):
            n = int(np.prod(dims))
            assert at + n <= ARENA, (at, n)
            used[0] = max(used[0], at + n)
            v = arena[:, at:at + n]
            if len(dims) == 2:
                v = v.rearrange("p (a b) -> p a b", b=dims[1])
            if len(dims) == 3:
                v = v.rearrange("p (a b c) -> p a b c", b=dims[1], c=dims[2])
            if len(dims) == 4:
                v = v.rearrange("p (a b c d) -> p a b c d", b=dims[1], c=dims[2], d=dims[3])
            return v

        def vcol(name, j, n=1):
            t, at, _ = VEC[name]
            return vec[:, t, at + j:at + j + n]

        w_arrived = [sem(f"w_arrived{i}") for i in range(RING)]
        panels = []
        slot_count = [0] * RING

        class Weights:

            def __init__(self, sources, freed):
                self.p0 = len(panels)
                self.arrived = []
                for i, loads in enumerate(sources):
                    slot = len(panels) % RING
                    slot_count[slot] += 16 * len(loads)
                    self.arrived.append((slot, slot_count[slot]))
                    panels.append((loads, freed(i)))

            def slot(self, i):
                return ring[:, (self.p0 + i) % RING, :]

            def view(self, i, kk, width):
                return self.slot(i)[:, 0:kk * width].rearrange("p (k n) -> p k n", n=width)

            def wait(self, pe, i):
                slot, value = self.arrived[i]
                pe.wait_ge(w_arrived[slot], value)

        def cols_of(w, c0, n):
            return w[:, c0:c0 + n].rearrange("(k p) n -> p k n", p=P)

        issued = [0]

        def sp_issue(sp, upto):
            while issued[0] < min(upto, len(panels)):
                p = issued[0]
                if p >= RING:
                    sp.wait_ge(*panels[p - RING][1])
                at = 0
                for src in panels[p][0]:
                    kk, nn = src.shape[1], src.shape[2]
                    dst = ring[:, p % RING, at:at + kk * nn].rearrange("p (k n) -> p k n", n=nn)
                    at += kk * nn
                    sp.dma_start(dst, src).then_inc(w_arrived[p % RING], 16)
                issued[0] += 1

        vec_loaded = sem("vec_loaded")
        consts_set = sem("consts_set")
        vec_turned = sem("vec_turned")
        vec_ready = sem("vec_ready")
        silu_ready = sem("silu_ready")
        x_loaded = sem("x_loaded")
        rows = area(0, 5, P)
        xrow = area(2 * KD * TOK, 4, D)
        x_turned = sem("x_turned")
        x_ready = sem("x_ready")

        class Setup:
            def sync(self, sp):
                sp.dma_start(xrow[:, 0:2, :], A["x"][0].rearrange("(b p) d -> p b d", p=P)).then_inc(x_loaded, 16)
                sp.dma_start(xrow[:, 2:4, :], A["ctx"][0].rearrange("(b p) d -> p b d", p=P)).then_inc(x_loaded, 16)

            def scalar(self, act):
                loads = [
                    ("mod_b01", A["mod_b"][0:2].rearrange("l (j p) -> (l j) p", p=P)),
                    ("mod_b23", A["mod_b"][2:4].rearrange("l (j p) -> (l j) p", p=P)),
                    ("mix_pre_g", A["mix_pre_g"].rearrange("l (j p) -> (l j) p", p=P)),
                    ("mix_post_g", A["mix_post_g"].rearrange("l (j p) -> (l j) p", p=P)),
                    ("ffn_pre_g", A["ffn_pre_g"].rearrange("l (j p) -> (l j) p", p=P)),
                    ("ffn_post_g", A["ffn_post_g"].rearrange("l (j p) -> (l j) p", p=P)),
                    ("hy_b_in", A["hy_b_in"][0].rearrange("(j p) -> j p", p=P)),
                    ("hy_conv_w", A["hy_conv_w"][0].rearrange("w (j p) -> (w j) p", p=P)),
                    ("hy_conv_b", A["hy_conv_b"][0].rearrange("(j p) -> j p", p=P)),
                    ("hy_skip", A["hy_skip"][0, 0].rearrange("(j p) -> j p", p=P)),
                    ("hy_b_out", A["hy_b_out"][0].rearrange("(j p) -> j p", p=P)),
                    ("s5_d", A["s5_d"][0].rearrange("(j p) -> j p", p=P)),
                    ("s5_b_glu", A["s5_b_glu"][0].rearrange("(j p) -> j p", p=P)),
                    ("fn_b_o", A["fn_b_o"][0].rearrange("(j p) -> j p", p=P)),
                    ("mla_q_norm_g", A["mla_q_norm_g"][0].rearrange("(j p) -> j p", p=P)),
                    ("mla_kv_norm_g", A["mla_kv_norm_g"][0].rearrange("(j p) -> j p", p=P)),
                    ("c", A["c"][0].rearrange("(j p) -> j p", p=P)),
                    ("c_ctx", A["c_ctx"].rearrange("(j p) -> j p", p=P)),
                ]
                for name, src in loads:
                    t, at, n = VEC[name]
                    act.dma_start(rows[at:at + n, t, :], src).then_inc(vec_loaded, 16)
                self.n_loads = len(loads)
                act.wait_ge(vec_ready, 5)
                nc.scalar.activation(silu_c[:, :, 0], vcol("c", 0, KD), ACT.Silu).then_inc(silu_ready, 1)
                nc.scalar.activation(silu_c[:, :, 1], vcol("c_ctx", 0, KD), ACT.Silu).then_inc(silu_ready, 1)

            def gpsimd(self, pool):
                nc.gpsimd.memset(ones[:, :], 1.0).then_inc(consts_set, 1)
                nc.gpsimd.memset(ident[:, :], 0.0).then_inc(consts_set, 1)
                pool.wait_ge(consts_set, 2)
                nc.gpsimd.affine_select(out=ident[:, :], in_=ident[:, :], compare_op=ALU.not_equal, fill=1.0, base=0,
                                        pattern=[[-1, P]], channel_multiplier=1).then_inc(consts_set, 1)

            def tensor(self, pe):
                pe.wait_ge(consts_set, 3)
                pe.wait_ge(vec_loaded, 16 * 18)
                for t, n in enumerate(VEC_ROWS):
                    nc.tensor.transpose(bank[t][:, 0:n], rows[0:n, t, :], ident[0:n, 0:n]).then_inc(vec_turned, 1)
                pe.wait_ge(vec_ready, 5)
                pe.wait_ge(x_loaded, 32)
                for k in range(KD):
                    b = 4 + k % 2
                    if k >= 2:
                        pe.wait_ge(x_ready, k - 1)
                    for t in range(4):
                        last = nc.tensor.transpose(bank[b][:, t * P:(t + 1) * P], xrow[:, t, k * P:(k + 1) * P], ident[:, :])
                    last.then_inc(x_turned, 1)

            def vector(self, dve):
                for t, n in enumerate(VEC_ROWS):
                    dve.wait_ge(vec_turned, t + 1)
                    nc.vector.tensor_copy(vec[:, t, 0:n], bank[t][:, 0:n]).then_inc(vec_ready, 1)
                for k in range(KD):
                    b = 4 + k % 2
                    dve.wait_ge(x_turned, k + 1)
                    nc.vector.tensor_copy(x[:, k, :], bank[b][:, :]).then_inc(x_ready, 1)

        mod_summed = sem("mod_summed")
        mod_ready = sem("mod_ready")
        mod_parts = []
        PER_CHUNK = D // 256

        class Modulation:

            PARTS = ((0, 2), (2, 1), (3, 2), (5, 1))

            def __init__(self, layer):
                self.layer, self.buf = layer, layer % 2
                self.parts = {}

            def part(self, n):
                self.parts[n] = ModPart(self, n)
                return self.parts[n]

            def wait(self, eng, n):
                eng.wait_ge(mod_ready, 3 * (self.parts[n].u + 1))

            def shift(self, ffn, k, s):
                j = (3 if ffn else 0) * KD + k
                return modv[:, self.buf, j, s:s + 1]

            def factor(self, n, k, s):
                return affine[:, self.buf, n, k, s:s + 1]

        class ModPart:
            BIAS = {1: "hy_b_out", 3: "fn_b_o"}

            def __init__(self, mod, n):
                self.mod, self.n = mod, n
                self.first, self.count = Modulation.PARTS[n]
                self.u = len(mod_parts)
                mod_parts.append(self)
                self.p0 = PER_CHUNK * sum(p.count for p in mod_parts[:-1])
                w = A["mod_w"][mod.layer]
                self.w = Weights([[cols_of(w, self.first * D + i * 256, 256)] for i in range(PER_CHUNK * self.count)],
                                 lambda i: (mod_summed, self.p0 + i + 1))

            def tensor(self, pe):
                if self.u == 0:
                    pe.wait_ge(silu_ready, 2)
                else:
                    pe.wait_ge(mod_ready, 3 * (self.u - 1) + 1)
                for i in range(PER_CHUNK * self.count):
                    self.w.wait(pe, i)
                    v = self.w.view(i, KD, 256)
                    for q in range(2):
                        j = self.first * KD + 2 * i + q
                        for k in range(KD):
                            last = nc.tensor.matmul(MODP[:, 2 * j:2 * j + 2], v[:, k, q * P:(q + 1) * P],
                                                    silu_c[:, k, :], start=(k == 0), stop=(k == KD - 1))
                    last.then_inc(mod_summed, 1)

            def vector(self, dve):
                l, b, base = self.mod.layer, self.mod.buf, 3 * self.u
                j0, nj = self.first * KD, self.count * KD
                m = modv[:, b]
                dve.wait_ge(mod_summed, self.p0 + PER_CHUNK * self.count)
                bias = vcol("mod_b01" if l < 2 else "mod_b23", (l % 2) * MODS * KD + j0, nj).unsqueeze(2).to_broadcast([P, nj, 2])
                nc.vector.tensor_tensor(m[:, j0:j0 + nj, :], MODP[:, 2 * j0:2 * (j0 + nj)].rearrange("p (j s) -> p j s", s=2), bias,
                                        ALU.add).then_inc(mod_ready, 1)
                dve.wait_ge(mod_ready, base + 1)
                g, at, plus = (("mix_pre_g", 1, 1.0), ("mix_post_g", 2, 0.0), ("ffn_pre_g", 4, 1.0), ("ffn_post_g", 5, 0.0))[self.n]
                gv = vcol(g, l * KD, KD).unsqueeze(2).to_broadcast([P, KD, 2])
                nc.vector.scalar_tensor_tensor(affine[:, b, self.n], m[:, at * KD:(at + 1) * KD, :], plus, gv,
                                               ALU.add, ALU.mult).then_inc(mod_ready, 1)
                dve.wait_ge(mod_ready, base + 2)
                bo = vcol(self.BIAS.get(l, "hy_b_out"), 0, KD).unsqueeze(2).to_broadcast([P, KD, 2])
                nc.vector.tensor_tensor(affine[:, b, 4 + self.n // 2], affine[:, b, self.n], bo, ALU.mult).then_inc(mod_ready, 1)

        squared = sem("squared")
        sq_added = sem("sq_added")
        sq_summed = sem("sq_summed")
        rms_step = sem("rms_step")
        rms_root = sem("rms_root")
        n_sq, n_add, n_rms = [0], [0], [0]

        class Rms:

            def __init__(self, kk, n, sq, feats, src=None, ready=None, on_pe=False):
                self.src, self.kk, self.n, self.sq, self.ready, self.feats = src, kk, n, sq, ready, feats
                self.on_pe = on_pe
                self.sq0, self.add0, self.u = n_sq[0], n_add[0], n_rms[0]
                n_sq[0] += kk
                n_add[0] += 0 if on_pe else kk - 1
                n_rms[0] += 1

            def squares(self, act):
                for k in range(self.kk):
                    self.ready(act, k)
                    nc.scalar.activation(self.sq[:, k, 0:self.n], self.src[:, k, 0:self.n], ACT.Square).then_inc(squared, 1)

            def root(self, act):
                act.wait_ge(rms_step, 2 * self.u + 1)
                nc.scalar.activation(rstd[:, 0:self.n], rstd[:, 0:self.n], ACT.Sqrt).then_inc(rms_root, 1)

            def vector(self, dve):
                n = self.n
                acc = self.sq[:, 0, 0:n]
                for k in range(1, 0 if self.on_pe else self.kk):
                    dve.wait_ge(squared, self.sq0 + k + 1)
                    if k > 1:
                        dve.wait_ge(sq_added, self.add0 + k - 1)
                    nc.vector.tensor_tensor(acc, acc, self.sq[:, k, 0:n], ALU.add).then_inc(sq_added, 1)
                dve.wait_ge(sq_summed, self.u + 1)
                nc.vector.tensor_scalar(rstd[:, 0:n], SUMS[:, 0:n], 1.0 / self.feats, EPS,
                                        ALU.mult, ALU.add).then_inc(rms_step, 1)
                dve.wait_ge(rms_root, self.u + 1)
                nc.vector.reciprocal(rstd[:, 0:n], rstd[:, 0:n]).then_inc(rms_step, 1)
                dve.wait_ge(rms_step, 2 * self.u + 2)

            def tensor(self, pe):
                kk = self.kk if self.on_pe else 1
                for k in range(kk):
                    if self.on_pe:
                        pe.wait_ge(squared, self.sq0 + k + 1)
                    else:
                        pe.wait_ge(sq_added, self.add0 + self.kk - 1)
                    last = nc.tensor.matmul(SUMS[:, 0:self.n], ones[:, :], self.sq[:, k, 0:self.n],
                                            start=(k == 0), stop=(k == kk - 1))
                last.then_inc(sq_summed, 1)

        normed = sem("normed")
        h_ready = sem("h_ready")
        n_pre = [0]
        x_updated, x_updated_pool = sem("x_updated"), sem("x_updated_pool")
        POOL_CHUNKS = (3, 6)
        DVE_CHUNKS = tuple(k for k in range(KD) if k not in POOL_CHUNKS)

        def x_updated_wait(eng, posts, k):
            if k in POOL_CHUNKS:
                eng.wait_ge(x_updated_pool, len(POOL_CHUNKS) * posts + POOL_CHUNKS.index(k) + 1)
            else:
                eng.wait_ge(x_updated, len(DVE_CHUNKS) * posts + DVE_CHUNKS.index(k) + 1)
        n_post = [0]

        SQ = area(0, KD, TOK)

        def segments(n):
            return [(0, 0, LAT)] + ([(1, LAT, TOK)] if n == TOK else [])

        h_split = h[:, :, :].rearrange("p k t -> p (k t)").rearrange("p (s k z m) -> p s k z m", k=KD, z=2, m=CH)

        class PreNorm:

            def __init__(self, mod, ffn, n, split=False):
                self.mod, self.ffn, self.n, self.split = mod, ffn, n, split
                self.u = n_pre[0]
                n_pre[0] += 1
                posts = self.posts = n_post[0]

                def ready(eng, k):
                    if posts == 0:
                        eng.wait_ge(x_ready, k + 1)
                    else:
                        x_updated_wait(eng, posts - 1, k)
                self.rms = Rms(KD, n, SQ, D, x, ready, on_pe=True)

            def dst(self, k, a, b):
                if not self.split:
                    return h[:, k, a:b]
                return h_split[:, :, k, a // LAT, :].rearrange("p s m -> p m s")

            def src(self, k, a, b):
                if not self.split:
                    return SQ[:, k, a:b]
                return SQ[:, k, a:b].rearrange("p (m s) -> p m s", s=STEP)

            def wait_x(self, eng):
                if self.posts:
                    eng.wait_ge(x_updated, len(DVE_CHUNKS) * self.posts)
                    eng.wait_ge(x_updated_pool, len(POOL_CHUNKS) * self.posts)
                else:
                    eng.wait_ge(x_ready, KD)

            def vector(self, dve):
                self.rms.vector(dve)
                for k in range(KD):
                    nc.vector.tensor_tensor(SQ[:, k, 0:self.n], x[:, k, 0:self.n], rstd[:, 0:self.n],
                                            ALU.mult).then_inc(normed, 1)

            def tensor(self, pe):
                self.rms.tensor(pe)

            def scalar(self, act):
                self.rms.squares(act)
                self.rms.root(act)
                self.mod.wait(act, 2 if self.ffn else 0)
                for k in range(KD):
                    act.wait_ge(normed, KD * self.u + k + 1)
                    for s, a, b in segments(self.n):
                        last = nc.scalar.activation(self.dst(k, a, b), self.src(k, a, b), ACT.Identity,
                                                    bias=self.mod.shift(self.ffn, k, s),
                                                    scale=self.mod.factor(2 if self.ffn else 0, k, s))
                    last.then_inc(h_ready, 1)

            def wait(self, eng, k=KD - 1):
                eng.wait_ge(h_ready, KD * self.u + k + 1)

        Y = area(KD * TOK, KD, TOK)
        y_normed, y_normed_pool = sem("y_normed"), sem("y_normed_pool")

        class PostNorm:

            def __init__(self, mod, ffn, n):
                self.mod, self.ffn, self.n = mod, ffn, n

            def number(self):
                self.u = n_post[0]
                n_post[0] += 1
                self.rms = Rms(KD, self.n, SQ, D)

            def move(self, act, c, src, bias=None):
                n, f = self.n, 3 if self.ffn else 1
                if c == 0:
                    self.mod.wait(act, f)
                if bias is None:
                    nc.scalar.activation(SQ[:, c, 0:n], src[:, 0:n], ACT.Square).then_inc(squared, 1)
                else:
                    nc.scalar.activation(SQ[:, c, 0:n], src[:, 0:n], ACT.Square, bias=vcol(bias, c)).then_inc(squared, 1)
                for s, a, b in segments(n):
                    if bias is None:
                        last = nc.scalar.activation(Y[:, c, a:b], src[:, a:b], ACT.Copy, scale=self.mod.factor(f, c, s))
                    else:
                        last = nc.scalar.activation(Y[:, c, a:b], src[:, a:b], ACT.Identity,
                                                    bias=self.mod.factor(4 + f // 2, c, s), scale=self.mod.factor(f, c, s))
                return last

            def scalar(self, act):
                self.rms.root(act)

            def tensor(self, pe):
                self.rms.tensor(pe)

            def gpsimd(self, pool):
                n = self.n
                pool.wait_ge(rms_step, 2 * self.rms.u + 2)
                for i, k in enumerate(POOL_CHUNKS):
                    nc.gpsimd.tensor_tensor(Y[:, k, 0:n], Y[:, k, 0:n], rstd[:, 0:n], ALU.mult).then_inc(y_normed_pool, 1)
                for i, k in enumerate(POOL_CHUNKS):
                    pool.wait_ge(y_normed_pool, len(POOL_CHUNKS) * self.u + i + 1)
                    nc.gpsimd.tensor_tensor(x[:, k, 0:n], x[:, k, 0:n], Y[:, k, 0:n], ALU.add).then_inc(x_updated_pool, 1)

            def vector(self, dve):
                self.rms.vector(dve)
                n = self.n

                def norm(i):
                    k = DVE_CHUNKS[i]
                    nc.vector.tensor_tensor(Y[:, k, 0:n], Y[:, k, 0:n], rstd[:, 0:n], ALU.mult).then_inc(y_normed, 1)
                norm(0)
                for i, k in enumerate(DVE_CHUNKS):
                    if i + 1 < len(DVE_CHUNKS):
                        norm(i + 1)
                    dve.wait_ge(y_normed, len(DVE_CHUNKS) * self.u + i + 1)
                    nc.vector.tensor_tensor(x[:, k, 0:n], x[:, k, 0:n], Y[:, k, 0:n], ALU.add).then_inc(x_updated, 1)
                dve.wait_ge(y_normed_pool, len(POOL_CHUNKS) * (self.u + 1))

            def wait(self, eng, k=KD - 1):
                x_updated_wait(eng, self.u, k)

        class Linear:

            def __init__(self, name, w, kk, rhs, n, ready, move, banks=(0, 1, 2, 3)):
                self.mm, self.moved = sem(name + "_summed"), sem(name + "_moved")
                self.kk, self.rhs, self.n, self.ready, self.move = kk, rhs, n, ready, move
                self.banks = [bank[i] for i in banks]
                self.parts = (kk + 10) // 11
                self.kp = kk // self.parts
                self.chunks = w.shape[1] // P
                rows = self.kp * P
                self.w = Weights([[cols_of(w[r * rows:(r + 1) * rows, :], i * 256, 256)]
                                  for i in range(self.chunks // 2) for r in range(self.parts)],
                                 lambda i: (self.mm, self.nth(i // self.parts, i % self.parts, 1)))

            def nth(self, i, r, q):
                return 2 * (self.parts * i + r) + q + 1

            def tensor(self, pe):
                for i in range(self.chunks // 2):
                    for r in range(self.parts):
                        self.w.wait(pe, self.parts * i + r)
                        v = self.w.view(self.parts * i + r, self.kp, 256)
                        for q in range(2):
                            c = 2 * i + q
                            if c >= 4 and r == 0:
                                pe.wait_ge(self.moved, c - 3)
                            for kl in range(self.kp):
                                k = r * self.kp + kl
                                if c == 0:
                                    self.ready(pe, k)
                                last = nc.tensor.matmul(self.banks[c % 4][:, 0:self.n], v[:, kl, q * P:(q + 1) * P], self.rhs(k),
                                                        start=(k == 0), stop=(k == self.kk - 1))
                            last.then_inc(self.mm, 1)

            def scalar(self, act):
                for c in range(self.chunks):
                    act.wait_ge(self.mm, self.nth(c // 2, self.parts - 1, c % 2))
                    self.move(act, c, self.banks[c % 4]).then_inc(self.moved, 1)

            def wait(self, eng, c=None):
                eng.wait_ge(self.moved, (self.chunks if c is None else c + 1))

        class Gated:

            def __init__(self, name, w, cols, rhs, n, ready, done):
                self.mm, self.done = sem(name + "_summed"), done
                self.rhs, self.n, self.ready = rhs, n, ready
                self.chunks = cols // P
                self.w = Weights([[cols_of(w, t * cols + i * 256, 256)] for i in range(self.chunks // 2) for t in range(2)],
                                 lambda i: (self.mm, 2 * (i + 1)))

            def bank(self, c, t):
                return bank[2 * t + c % 2]

            def summed(self, eng, c, t):
                eng.wait_ge(self.mm, 4 * (c // 2) + 2 * t + c % 2 + 1)

            def tensor(self, pe):
                for c2 in range(self.chunks // 2):
                    for t in range(2):
                        self.w.wait(pe, 2 * c2 + t)
                        v = self.w.view(2 * c2 + t, KD, 256)
                        for q in range(2):
                            c = 2 * c2 + q
                            if c >= 2:
                                pe.wait_ge(self.done, c - 1)
                            for k in range(KD):
                                if c == 0 and t == 0:
                                    self.ready(pe, k)
                                last = nc.tensor.matmul(self.bank(c, t)[:, 0:self.n], v[:, k, q * P:(q + 1) * P], self.rhs(k),
                                                        start=(k == 0), stop=(k == KD - 1))
                            last.then_inc(self.mm, 1)

        GT = area(2 * KD * TOK, KF, TOK)

        class Ffn:

            def __init__(self, layer, n, pre, post):
                self.n, self.pre = n, pre
                self.silu = sem(f"ffn{layer}_silu")
                self.g = sem(f"ffn{layer}_gated")
                self.silus = area(0, 2, TOK)
                self.up = Gated(f"ffn{layer}_up", A["ffn_w13"][layer], FFN, lambda k: h[:, k, 0:n], n, pre.wait, self.g)
                self.down = Linear(f"ffn{layer}_down", A["ffn_w2"][layer], KF, lambda k: GT[:, k, 0:n], n,
                                   lambda pe, k: pe.wait_ge(self.g, k + 1), post.move, (4, 5, 0, 1))

            def tensor(self, pe):
                self.up.tensor(pe)
                self.down.tensor(pe)

            def scalar(self, act):
                n = self.n
                for f in range(KF):
                    self.up.summed(act, f, 0)
                    if f >= 2:
                        act.wait_ge(self.g, f - 1)
                    nc.scalar.activation(self.silus[:, f % 2, 0:n], self.up.bank(f, 0)[:, 0:n], ACT.Silu).then_inc(self.silu, 1)
                self.down.scalar(act)

            def vector(self, dve):
                n = self.n
                for f in range(KF):
                    self.up.summed(dve, f, 1)
                    dve.wait_ge(self.silu, f + 1)
                    nc.vector.tensor_tensor(GT[:, f, 0:n], self.silus[:, f % 2, 0:n], self.up.bank(f, 1)[:, 0:n],
                                            ALU.mult).then_inc(self.g, 1)
        class Mla:

            def __init__(self, pre, post, n_in, n):
                self.pre = pre
                at = KD * TOK
                self.z = area(at, 8, TOK)
                at = 2 * KD * TOK
                self.v = area(at, 4, D)
                self.kn = area(at + 4096, HEADS, TOK)
                self.qn = area(at + 8192, HEADS, TOK)
                self.qr = area(at + 12288, HEADS, TOK)
                self.qrot = area(at + 16384, HEADS, LAT)
                self.kr = area(at + 18432, TOK)
                self.krot = area(at + 18944, LAT)
                self.tab = area(at + 19200, 2, LAT)
                self.turn = area(at + 19712, ROPE)
                self.tmp = area(at + 19776, 2, 2, LAT)
                self.e = area(at + 20800, 2, TOK)
                self.pt = area(at + 21824, 2, TOK)
                self.mx = small[:, 0:2]
                self.sm = small[:, 2:4]
                self.loaded = sem("mla_tables_loaded")
                w = A["mla_w_in"][0]
                self.z_summed, self.z_moved = sem("mla_z_summed"), sem("mla_z_moved")
                self.win = Weights([[cols_of(w, i * 256, 256)] for i in range(4)] + [[cols_of(w, 1024, ROPE)]],
                                   lambda i: (self.z_summed, min(2 * (i + 1), 9)))
                self.rms_q = Rms(6, TOK, SQ, QR, self.z, lambda eng, k: eng.wait_ge(self.z_moved, k + 1))
                self.zn, self.z_ready = sem("mla_z_normed"), sem("mla_z_ready")
                self.rms_kv = Rms(2, TOK, SQ[:, 6:8, :], KVR, self.z[:, 6:8, :], lambda eng, k: eng.wait_ge(self.z_moved, k + 7))
                self.q_summed, self.q_moved = sem("mla_q_summed"), sem("mla_q_moved")
                self.wuq = Weights([[cols_of(A["mla_w_uq"][0], i * 384, 384)] for i in range(4)],
                                   lambda i: (self.q_summed, 4 * (i + 1)))
                self.kv_summed, self.kv_moved = sem("mla_kv_summed"), sem("mla_kv_moved")
                self.wukv = Weights([[cols_of(A["mla_w_ukv"][0], i * 1024, 1024)] for i in range(2)], lambda i: (self.kv_summed, 16))
                self.turned, self.rot = sem("mla_turned"), sem("mla_rotated")
                self.rot_step = sem("mla_rot_step")
                self.scored, self.maxed, self.negated = sem("mla_scored"), sem("mla_maxed"), sem("mla_negated")
                self.exped, self.recip, self.probs = sem("mla_exped"), sem("mla_recip"), sem("mla_probs")
                self.p_turned, self.p_moved = sem("mla_p_turned"), sem("mla_p_moved")
                self.o_summed, self.o_moved = sem("mla_o_summed"), sem("mla_o_moved")
                self.proj = Linear("mla_out", A["mla_w_o"][0], KD, lambda k: h[:, k, :], TOK,
                                   lambda pe, k: pe.wait_ge(self.o_moved, 4 * HEADS), post.move)
                self.units = [(hd, qb, 0 if qb < 2 else LAT, 4 if qb < 2 else 2) for hd in range(HEADS) for qb in range(4)]

            def gpsimd(self, pool):
                pool.wait_ge(x_ready, KD)
                pool.dma_start(self.tab[0:ROPE], A["k_rope"]).then_inc(self.loaded, 16)
                pool.dma_start(self.turn[0:ROPE], A["k_turn"]).then_inc(self.loaded, 16)

            def tensor(self, pe):
                for c in range(9):
                    if c % 2 == 0:
                        self.win.wait(pe, c // 2)
                    m = ROPE if c == 8 else P
                    v = self.win.view(c // 2, KD, ROPE if c == 8 else 256)
                    if c >= 4:
                        pe.wait_ge(self.z_moved, c - 3)
                    for k in range(KD):
                        if c == 0:
                            self.pre.wait(pe, k)
                        last = nc.tensor.matmul(bank[c % 4][0:m, :], v[:, k, (c % 2) * P:(c % 2) * P + m], h[:, k, :],
                                                start=(k == 0), stop=(k == KD - 1))
                    last.then_inc(self.z_summed, 1)
                self.rms_q.tensor(pe)
                self.rms_kv.tensor(pe)
                pe.wait_ge(self.z_ready, 6)
                for c in range(16):
                    hd, part = divmod(c, 2)
                    if c % 4 == 0:
                        self.wuq.wait(pe, c // 4)
                    v = self.wuq.view(c // 4, 6, 384)
                    c0 = (hd % 2) * 192 + part * P
                    m = ROPE if part else P
                    if c < 4:
                        pe.wait_ge(self.z_moved, 9)
                    else:
                        pe.wait_ge(self.q_moved, c - 3)
                    for k in range(6):
                        last = nc.tensor.matmul(bank[c % 4][0:m, :], v[:, k, c0:c0 + m], self.z[:, k, :],
                                                start=(k == 0), stop=(k == 5))
                    last.then_inc(self.q_summed, 1)
                pe.wait_ge(self.z_ready, 8)
                self.wukv.wait(pe, 0)
                self.wukv.wait(pe, 1)
                wv = [self.wukv.view(i, 2, 1024) for i in range(2)]
                for c in range(16):
                    if c < 4:
                        pe.wait_ge(self.q_moved, 13 + c)
                    else:
                        pe.wait_ge(self.kv_moved, c - 3)
                    for k in range(2):
                        if c < 8:
                            last = nc.tensor.matmul(bank[c % 4][:, :], wv[c // 4][:, k, c % 4 * 256:c % 4 * 256 + P], self.z[:, 6 + k, :],
                                                    start=(k == 0), stop=(k == 1))
                        else:
                            t, half = divmod(c - 8, 2)
                            vals = wv[half][:, k, :].rearrange("p (h n) -> p h n", n=256)[:, :, P:256]
                            last = nc.tensor.matmul(bank[c % 4][:, :].rearrange("p (h n) -> p h n", n=P),
                                                    self.z[:, 6 + k, t * P:(t + 1) * P], vals, start=(k == 0), stop=(k == 1))
                    last.then_inc(self.kv_summed, 1)
                pe.wait_ge(self.loaded, 32)
                for i in range(9):
                    if i >= 2:
                        pe.wait_ge(self.rot, i - 1)
                    src = self.kr[0:ROPE, 0:LAT] if i == 0 else self.qr[0:ROPE, i - 1, 0:LAT]
                    nc.tensor.matmul(bank[4 + i % 2][0:ROPE, 0:LAT], self.turn[0:ROPE, :], src,
                                     start=True, stop=True).then_inc(self.turned, 1)

                def scores(u):
                    hd, qb, k0, nk = self.units[u]
                    if u < 2:
                        pe.wait_ge(self.kv_moved, 16)
                        pe.wait_ge(self.rot, 9)
                    else:
                        pe.wait_ge(self.exped, u - 1)
                    b = bank[u % 2]
                    q = slice(qb * P, (qb + 1) * P)
                    if qb < 2:
                        nc.tensor.matmul(b[:, :], self.qn[:, hd, q], self.kn[:, hd, :], start=True, stop=False)
                        nc.tensor.matmul(b[:, 0:LAT], self.qrot[0:ROPE, hd, q], self.krot[0:ROPE, :], start=False, stop=False)
                        nc.tensor.matmul(b[:, LAT:TOK], self.qr[0:ROPE, hd, q], self.kr[0:ROPE, LAT:TOK],
                                         start=False, stop=True).then_inc(self.scored, 1)
                    else:
                        nc.tensor.matmul(b[:, 0:LAT], self.qn[:, hd, q], self.kn[:, hd, LAT:TOK], start=True, stop=False)
                        nc.tensor.matmul(b[:, 0:LAT], self.qr[0:ROPE, hd, q], self.kr[0:ROPE, LAT:TOK],
                                         start=False, stop=True).then_inc(self.scored, 1)

                def weigh(u):
                    hd, qb, k0, nk = self.units[u]
                    pe.wait_ge(self.probs, u + 1)
                    if u >= 2:
                        pe.wait_ge(self.p_moved, u - 1)
                    for j in range(nk):
                        last = nc.tensor.transpose(bank[2 + u % 2][:, j * P:(j + 1) * P], self.e[:, u % 2, j * P:(j + 1) * P], ident[:, :])
                    last.then_inc(self.p_turned, 1)

                def values(u):
                    hd, qb, k0, nk = self.units[u]
                    pe.wait_ge(self.p_moved, u + 1)
                    if u >= 2:
                        pe.wait_ge(self.o_moved, u - 1)
                    for j in range(nk):
                        last = nc.tensor.matmul(bank[4 + u % 2][:, 0:P], self.v[:, k0 // P + j, hd * P:(hd + 1) * P],
                                                self.pt[:, u % 2, j * P:(j + 1) * P], start=(j == 0), stop=(j == nk - 1))
                    last.then_inc(self.o_summed, 1)
                n = len(self.units)
                scores(0)
                scores(1)
                for u in range(n):
                    weigh(u)
                    if u + 2 < n:
                        scores(u + 2)
                    if u >= 1:
                        values(u - 1)
                values(n - 1)
                self.proj.tensor(pe)

            def scalar(self, act):
                for c in range(9):
                    act.wait_ge(self.z_summed, c + 1)
                    dst = self.kr[0:ROPE, :] if c == 8 else self.z[:, c, :]
                    m = ROPE if c == 8 else P
                    nc.scalar.activation(dst, bank[c % 4][0:m, :], ACT.Copy).then_inc(self.z_moved, 1)
                self.rms_q.squares(act)
                self.rms_q.root(act)
                for k in range(6):
                    act.wait_ge(self.zn, k + 1)
                    nc.scalar.activation(self.z[:, k, :], self.z[:, k, :], ACT.Copy, scale=vcol("mla_q_norm_g", k)).then_inc(self.z_ready, 1)
                self.rms_kv.squares(act)
                self.rms_kv.root(act)
                for k in range(2):
                    act.wait_ge(self.zn, 6 + k + 1)
                    nc.scalar.activation(self.z[:, 6 + k, :], self.z[:, 6 + k, :], ACT.Copy, scale=vcol("mla_kv_norm_g", k)).then_inc(self.z_ready, 1)
                for c in range(16):
                    act.wait_ge(self.q_summed, c + 1)
                    hd, part = divmod(c, 2)
                    dst, m = (self.qr[0:ROPE, hd, :], ROPE) if part else (self.qn[:, hd, :], P)
                    nc.scalar.activation(dst, bank[c % 4][0:m, :], ACT.Copy).then_inc(self.q_moved, 1)
                for c in range(16):
                    act.wait_ge(self.kv_summed, c + 1)
                    if c < 8:
                        dst = self.kn[:, c, :]
                    else:
                        t, half = divmod(c - 8, 2)
                        dst = self.v[:, t, half * 512:(half + 1) * 512]
                    nc.scalar.activation(dst, bank[c % 4][:, :], ACT.Copy).then_inc(self.kv_moved, 1)
                scale = float((NOPE + ROPE) ** -0.5)

                def out(u):
                    hd, qb, k0, nk = self.units[u]
                    act.wait_ge(self.o_summed, u + 1)
                    nc.scalar.activation(h[:, hd, qb * P:(qb + 1) * P], bank[4 + u % 2][:, 0:P], ACT.Copy).then_inc(self.o_moved, 1)
                for u, (hd, qb, k0, nk) in enumerate(self.units):
                    act.wait_ge(self.negated, u + 1)
                    if u >= 2:
                        act.wait_ge(self.p_turned, u - 1)
                    nc.scalar.activation(self.e[:, u % 2, 0:nk * P], bank[u % 2][:, 0:nk * P], ACT.Exp, bias=self.mx[:, u % 2:u % 2 + 1],
                                         scale=scale, accum_out=self.sm[:, u % 2:u % 2 + 1]).then_inc(self.exped, 1)
                    if u >= 2:
                        out(u - 2)
                out(len(self.units) - 2)
                out(len(self.units) - 1)
                self.proj.scalar(act)

            def vector(self, dve):
                self.rms_q.vector(dve)
                for k in range(6):
                    nc.vector.tensor_tensor(self.z[:, k, :], self.z[:, k, :], rstd[:, :], ALU.mult).then_inc(self.zn, 1)
                dve.wait_ge(self.zn, 6)
                self.rms_kv.vector(dve)
                for k in range(2):
                    nc.vector.tensor_tensor(self.z[:, 6 + k, :], self.z[:, 6 + k, :], rstd[:, :], ALU.mult).then_inc(self.zn, 1)
                cos, sin = self.tab[0:ROPE, 0, :], self.tab[0:ROPE, 1, :]
                dve.wait_ge(self.loaded, 32)
                for i in range(9):
                    src = self.kr[0:ROPE, 0:LAT] if i == 0 else self.qr[0:ROPE, i - 1, 0:LAT]
                    dst = self.krot[0:ROPE, :] if i == 0 else self.qrot[0:ROPE, i - 1, :]
                    dve.wait_ge(self.turned, i + 1)
                    if i >= 2:
                        dve.wait_ge(self.rot, i - 1)
                    nc.vector.tensor_tensor(self.tmp[0:ROPE, i % 2, 0, :], bank[4 + i % 2][0:ROPE, 0:LAT], sin, ALU.mult).then_inc(self.rot_step, 1)
                    nc.vector.tensor_tensor(self.tmp[0:ROPE, i % 2, 1, :], src, cos, ALU.mult).then_inc(self.rot_step, 1)
                    dve.wait_ge(self.rot_step, 2 * i + 2)
                    nc.vector.tensor_tensor(dst, self.tmp[0:ROPE, i % 2, 0, :], self.tmp[0:ROPE, i % 2, 1, :], ALU.add).then_inc(self.rot, 1)
                scale = float((NOPE + ROPE) ** -0.5)
                n = len(self.units)

                def peak(u):
                    hd, qb, k0, nk = self.units[u]
                    dve.wait_ge(self.scored, u + 1)
                    nc.vector.reduce_max(self.mx[:, u % 2:u % 2 + 1], bank[u % 2][:, 0:nk * P], axis=AX.X).then_inc(self.maxed, 1)
                    dve.wait_ge(self.maxed, u + 1)
                    nc.vector.tensor_scalar(self.mx[:, u % 2:u % 2 + 1], self.mx[:, u % 2:u % 2 + 1], -scale, None, ALU.mult).then_inc(self.negated, 1)
                peak(0)
                peak(1)
                for u, (hd, qb, k0, nk) in enumerate(self.units):
                    dve.wait_ge(self.exped, u + 1)
                    nc.vector.reciprocal(self.sm[:, u % 2:u % 2 + 1], self.sm[:, u % 2:u % 2 + 1]).then_inc(self.recip, 1)
                    dve.wait_ge(self.recip, u + 1)
                    nc.vector.tensor_scalar(self.e[:, u % 2, 0:nk * P], self.e[:, u % 2, 0:nk * P], self.sm[:, u % 2:u % 2 + 1],
                                            None, ALU.mult).then_inc(self.probs, 1)
                    if u + 2 < n:
                        peak(u + 2)
                    dve.wait_ge(self.p_turned, u + 1)
                    if u >= 2:
                        dve.wait_ge(self.o_summed, u - 1)
                    nc.vector.tensor_copy(self.pt[:, u % 2, 0:nk * P], bank[2 + u % 2][:, 0:nk * P]).then_inc(self.p_moved, 1)

        class Hyena:

            SEQS = 2
            SIN_STEPS = 6

            def __init__(self, pre, post, n_in, n):
                self.pre = pre
                self.pad = area(0, 2, 2, LAT + 2)
                self.w3 = area(2048, 2 * D)
                self.absh = area(0, 4, D)
                self.tmp = area(0, 4, 512)
                self.zt = area(4096, LAT)
                self.w1 = area(4352, WIDTH)
                self.w2 = area(4416, 2, WIDTH)
                self.fcol = area(4544, 8)
                self.a = area(4608, LAT)
                self.k = area(4864, LAT)
                self.sd = area(4096, 2, 2, D)
                self.u = area(8192, 24, TOK)
                self.v = area(8192 + 16 * TOK, 8, TOK)
                self.vt = area(8192 + 8 * TOK, 4, D)
                self.kf = area(20480, 4, D)
                self.dec = area(20480, 2, D)
                self.hfb = area(24576, 2, 2, D)
                self.prod = area(24576, 4, D)
                self.cs = area(28672, 2, 2, LAT)
                self.ics = area(29696, 2, 2, LAT)
                self.loaded, self.loaded2 = sem("hy_small_loaded"), sem("hy_tables_loaded")
                self.padded = sem("hy_pads_zeroed")
                self.u_summed, self.u_moved, self.conv_step = sem("hy_u_summed"), sem("hy_u_moved"), sem("hy_conv_step")
                self.conv = sem("hy_convolved")
                self.win = Weights([[cols_of(A["hy_w_in"][0], i * 256, 256)] for i in range(12)],
                                   lambda i: (self.u_summed, 2 * (i + 1)))
                self.v_gated, self.v_turned, self.v_moved = sem("hy_v_gated"), sem("hy_v_turned"), sem("hy_v_moved")
                self.f_summed, self.f_step, self.f_sin = sem("hy_f_summed"), sem("hy_f_step"), sem("hy_f_sin")
                self.t_summed, self.t_decayed, self.t_masked = sem("hy_taps_summed"), sem("hy_taps_decayed"), sem("hy_taps_masked")
                self.t_abs, self.t_norm, self.t_inv, self.t_mixed = sem("hy_taps_abs"), sem("hy_taps_normed"), sem("hy_taps_inverse"), sem("hy_taps_mixed")
                self.k_summed, self.k_moved = sem("hy_k_summed"), sem("hy_k_moved")
                self.s_summed, self.s_prod, self.s_step = sem("hy_spectrum_summed"), sem("hy_spectrum_product"), sem("hy_product_step")
                self.y_summed, self.y_scaled, self.y_skip, self.y_gated = sem("hy_y_summed"), sem("hy_y_scaled"), sem("hy_y_skip"), sem("hy_y_gated")
                self.ytmp = area(2048, 2, LAT)
                self.proj = Linear("hy_out", A["hy_w_out"][0], KD, lambda k: h[:, k, :], TOK,
                                   lambda pe, k: pe.wait_ge(self.y_gated, KD + k + 1),
                                   lambda act, c, b: post.move(act, c, b, "hy_b_out"))

            def gpsimd(self, pool):
                self.pre.wait(pool)
                one = lambda v: v.rearrange("(p o) -> p o", o=1)
                with nc.allow_non_contiguous_dma(reason="64 words"):
                    for j, v in enumerate([A["hy_f_b1"][0], A["hy_f_b2"][0, 0], A["hy_f_b2"][0, 1], A["hy_f_freq"][0]]):
                        pool.dma_start(self.fcol[0:WIDTH, j:j + 1], one(v)).then_inc(self.loaded, 16)
                pool.dma_start(self.zt[0:EMB, :], A["k_hyena_z"]).then_inc(self.loaded, 16)
                pool.dma_start(self.w1[0:EMB, :], A["hy_f_w1"][0]).then_inc(self.loaded, 16)
                pool.dma_start(self.w2[0:WIDTH], A["hy_f_w2"][0].rearrange("i p n -> p i n")).then_inc(self.loaded, 16)
                pool.dma_start(self.w3[0:WIDTH], A["hy_f_w3"][0]).then_inc(self.loaded, 16)
                pool.dma_start(self.dec, A["k_hyena_decay"]).then_inc(self.loaded2, 16)
                pool.dma_start(self.cs, A["k_dft_odd"]).then_inc(self.loaded2, 16)
                pool.dma_start(self.ics, A["k_idft_odd"]).then_inc(self.loaded2, 16)
                for b in range(2):
                    nc.gpsimd.memset(self.pad[:, b, :, 0:1], 0.0).then_inc(self.padded, 1)
                    nc.gpsimd.memset(self.pad[:, b, :, LAT + 1:LAT + 2], 0.0).then_inc(self.padded, 1)

            def tensor(self, pe):
                for c in range(24):
                    i, q = divmod(c, 2)
                    if q == 0:
                        self.win.wait(pe, i)
                    v = self.win.view(i, KD, 256)
                    if c >= 4:
                        pe.wait_ge(self.u_moved, c - 3)
                    for k in range(KD):
                        if c == 0:
                            self.pre.wait(pe, k)
                        last = nc.tensor.matmul(bank[c % 4][:, :], v[:, k, q * P:(q + 1) * P], h[:, k, :],
                                                start=(k == 0), stop=(k == KD - 1))
                    last.then_inc(self.u_summed, 1)
                pe.wait_ge(self.loaded, 16 * 8)
                for r in range(3):
                    lhs = self.w1[0:EMB, :] if r == 0 else self.w2[0:WIDTH, r - 1, :]
                    rhs = self.zt[0:EMB, :] if r == 0 else self.a[0:WIDTH, :]
                    if r:
                        pe.wait_ge(self.f_sin, r)
                    nc.tensor.matmul(bank[5][0:WIDTH, 0:LAT], lhs, rhs, start=True, stop=True).then_inc(self.f_summed, 1)
                pe.wait_ge(self.u_moved, 24)
                pe.wait_ge(self.f_sin, 3)
                for n in range(8):
                    t, q = divmod(n, 4)
                    if n >= 4:
                        pe.wait_ge(self.t_decayed, n - 3)
                    nc.tensor.matmul(bank[n % 4][:, :], self.a[0:WIDTH, t * P:(t + 1) * P], self.w3[0:WIDTH, q * 512:(q + 1) * 512],
                                     start=True, stop=True).then_inc(self.t_summed, 1)
                pe.wait_ge(self.t_abs, 1)
                for c in range(KD):
                    for j in range(4):
                        last = nc.tensor.matmul(bank[5][:, c:c + 1], self.absh[:, j, c * P:(c + 1) * P], ones[:, 0:1],
                                                start=(j == 0), stop=(j == 3))
                last.then_inc(self.t_norm, 1)
                pe.wait_ge(self.t_mixed, 2)
                pe.wait_ge(self.loaded2, 48)
                for n in range(8):
                    part, fb, half = n // 4, n // 2 % 2, n % 2
                    if n >= 4:
                        pe.wait_ge(self.k_moved, n - 3)
                    for t in range(2):
                        last = nc.tensor.matmul(bank[n % 4][:, :], self.cs[:, part, t, fb * P:(fb + 1) * P],
                                                self.sd[:, part, t, half * 512:(half + 1) * 512], start=(t == 0), stop=(t == 1))
                    last.then_inc(self.k_summed, 1)
                pe.wait_ge(self.v_gated, KD)
                for n in range(8):
                    t, half = divmod(n, 2)
                    if n < 4:
                        pe.wait_ge(self.k_moved, 5 + n)
                    else:
                        pe.wait_ge(self.v_moved, n - 3)
                    for q in range(4):
                        last = nc.tensor.transpose(bank[n % 4][:, q * P:(q + 1) * P], self.v[:, 4 * half + q, t * P:(t + 1) * P], ident[:, :])
                    last.then_inc(self.v_turned, 1)
                for s in range(self.SEQS):
                    for n in range(4):
                        fb, half = divmod(n, 2)
                        m = 4 * s + n
                        if m == 0:
                            pe.wait_ge(self.v_moved, 8)
                        if m >= 2:
                            pe.wait_ge(self.s_prod, m - 1)
                        for part in range(2):
                            for t in range(2):
                                last = nc.tensor.matmul(bank[2 * (m % 2) + part][:, :], self.cs[:, part, t, fb * P:(fb + 1) * P],
                                                        self.vt[:, 2 * s + t, half * 512:(half + 1) * 512], start=(t == 0), stop=(t == 1))
                        last.then_inc(self.s_summed, 1)
                    for c in range(KD):
                        pe.wait_ge(self.s_prod, 4 * s + 4)
                        m = KD * s + c
                        if m >= 2:
                            pe.wait_ge(self.y_scaled, m - 1)
                        else:
                            pe.wait_ge(self.t_inv, 1)
                        for fb in range(2):
                            for part in range(2):
                                last = nc.tensor.matmul(bank[4 + m % 2][:, 0:LAT], self.prod[:, 2 * part + fb, c * P:(c + 1) * P],
                                                        self.ics[:, part, fb, :], start=(fb + part == 0), stop=(fb + part == 2))
                        last.then_inc(self.y_summed, 1)
                self.proj.tensor(pe)

            def scalar(self, act):
                act.wait_ge(self.padded, 4)
                for c in range(24):
                    act.wait_ge(self.u_summed, c + 1)
                    if c >= 2:
                        act.wait_ge(self.conv, c - 1)
                    nc.scalar.activation(self.pad[:, c % 2, :, 1:LAT + 1], bank[c % 4][:, :].rearrange("p (s t) -> p s t", s=2),
                                         ACT.Identity, bias=vcol("hy_b_in", c)).then_inc(self.u_moved, 1)
                for r in range(3):
                    act.wait_ge(self.f_step, self.SIN_STEPS * (r + 1))
                    nc.scalar.activation(self.a[0:WIDTH, :], self.a[0:WIDTH, :], ACT.Sin).then_inc(self.f_sin, 1)
                act.wait_ge(self.t_masked, 1)
                nc.scalar.activation(self.absh.rearrange("p a b -> p (a b)"), self.hfb.rearrange("p a b c -> p (a b c)"), ACT.Abs).then_inc(self.t_abs, 1)
                for n in range(8):
                    part, fb, half = n // 4, n // 2 % 2, n % 2
                    act.wait_ge(self.k_summed, n + 1)
                    nc.scalar.activation(self.kf[:, 2 * part + fb, half * 512:(half + 1) * 512], bank[n % 4][:, :], ACT.Copy).then_inc(self.k_moved, 1)
                for n in range(8):
                    t, half = divmod(n, 2)
                    act.wait_ge(self.v_turned, n + 1)
                    nc.scalar.activation(self.vt[:, t, half * 512:(half + 1) * 512], bank[n % 4][:, :], ACT.Copy).then_inc(self.v_moved, 1)
                act.wait_ge(self.t_inv, 1)
                for m in range(2 * KD):
                    s, c = divmod(m, KD)
                    act.wait_ge(self.y_summed, m + 1)
                    if m >= 2:
                        act.wait_ge(self.y_skip, m - 1)
                    nc.scalar.activation(self.ytmp[:, m % 2, :], bank[4 + m % 2][:, 0:LAT], ACT.Copy, scale=small[:, 8 + c:9 + c]).then_inc(self.y_scaled, 1)
                self.proj.scalar(act)

            def vector(self, dve):
                for c in range(24):
                    dve.wait_ge(self.u_moved, c + 1)
                    p, dst = self.pad[:, c % 2], self.u[:, c, :].rearrange("p (s t) -> p s t", s=2)
                    nc.vector.tensor_scalar(dst, p[:, :, 1:LAT + 1], vcol("hy_conv_w", 24 + c), vcol("hy_conv_b", c),
                                            ALU.mult, ALU.add).then_inc(self.conv_step, 1)
                    dve.wait_ge(self.conv_step, 2 * c + 1)
                    nc.vector.scalar_tensor_tensor(dst, p[:, :, 0:LAT], vcol("hy_conv_w", c), dst, ALU.mult, ALU.add).then_inc(self.conv_step, 1)
                    dve.wait_ge(self.conv_step, 2 * c + 2)
                    nc.vector.scalar_tensor_tensor(dst, p[:, :, 2:LAT + 2], vcol("hy_conv_w", 48 + c), dst, ALU.mult, ALU.add).then_inc(self.conv, 1)
                    if c >= 16:
                        dve.wait_ge(self.conv, c + 1)
                        nc.vector.tensor_tensor(self.u[:, c, :], self.u[:, c, :], self.u[:, c - 8, :], ALU.mult).then_inc(self.v_gated, 1)
                dve.wait_ge(self.loaded, 16 * 8)
                a, k = self.a[0:WIDTH, :], self.k[0:WIDTH, :]
                for r in range(3):
                    dve.wait_ge(self.f_summed, r + 1)
                    at = self.SIN_STEPS * r
                    nc.vector.tensor_scalar(a, bank[5][0:WIDTH, 0:LAT], self.fcol[0:WIDTH, r:r + 1], self.fcol[0:WIDTH, 3:4],
                                            ALU.add, ALU.mult).then_inc(self.f_step, 1)
                    dve.wait_ge(self.f_step, at + 1)
                    nc.vector.tensor_scalar(k, a, 1.0 / TWO_PI, ROUND, ALU.mult, ALU.add).then_inc(self.f_step, 1)
                    dve.wait_ge(self.f_step, at + 2)
                    nc.vector.tensor_scalar(k, k, -ROUND, None, ALU.add).then_inc(self.f_step, 1)
                    for n, c in enumerate((PI_HI, PI_MID)):
                        dve.wait_ge(self.f_step, at + 3 + n)
                        nc.vector.scalar_tensor_tensor(a, k, -c, a, ALU.mult, ALU.add).then_inc(self.f_step, 1)
                    dve.wait_ge(self.f_step, at + 5)
                    nc.vector.tensor_scalar(a, a, PI_IN, -PI_IN, ALU.min, ALU.max).then_inc(self.f_step, 1)
                dve.wait_ge(self.loaded2, 48)
                for n in range(8):
                    t, q = divmod(n, 4)
                    dr, half = divmod(q, 2)
                    dve.wait_ge(self.t_summed, n + 1)
                    nc.vector.tensor_tensor(self.hfb[:, t, dr, half * 512:(half + 1) * 512], bank[n % 4][:, :],
                                            self.dec[:, t, half * 512:(half + 1) * 512], ALU.mult).then_inc(self.t_decayed, 1)
                dve.wait_ge(self.t_decayed, 8)
                nc.vector.memset(self.hfb[0:1, 0, 1, :], 0.0).then_inc(self.t_masked, 1)
                dve.wait_ge(self.t_masked, 1)
                hf, hb = self.hfb[:, :, 0, :], self.hfb[:, :, 1, :]
                nc.vector.tensor_tensor(self.sd[:, 0], hf, hb, ALU.add).then_inc(self.t_mixed, 1)
                nc.vector.tensor_tensor(self.sd[:, 1], hb, hf, ALU.subtract).then_inc(self.t_mixed, 1)
                dve.wait_ge(self.t_norm, 1)
                nc.vector.reciprocal(small[:, 8:16], bank[5][:, 0:KD]).then_inc(self.t_inv, 1)
                dve.wait_ge(self.k_moved, 8)
                for s in range(self.SEQS):
                    for n in range(4):
                        fb, half = divmod(n, 2)
                        m = 4 * s + n
                        cols = slice(half * 512, (half + 1) * 512)
                        vr, vi = bank[2 * (m % 2)][:, :], bank[2 * (m % 2) + 1][:, :]
                        kr, ki = self.kf[:, fb, cols], self.kf[:, 2 + fb, cols]
                        dve.wait_ge(self.s_summed, m + 1)
                        if m == 4:
                            dve.wait_ge(self.y_summed, KD)
                        if m >= 1:
                            dve.wait_ge(self.s_prod, m)
                        nc.vector.tensor_tensor(self.tmp[:, 0, :], vr, kr, ALU.mult).then_inc(self.s_step, 1)
                        nc.vector.tensor_tensor(self.tmp[:, 1, :], vi, ki, ALU.mult).then_inc(self.s_step, 1)
                        nc.vector.tensor_tensor(self.tmp[:, 2, :], vr, ki, ALU.mult).then_inc(self.s_step, 1)
                        nc.vector.tensor_tensor(self.tmp[:, 3, :], vi, kr, ALU.mult).then_inc(self.s_step, 1)
                        dve.wait_ge(self.s_step, 5 * m + 2)
                        nc.vector.tensor_tensor(self.prod[:, fb, cols], self.tmp[:, 0, :], self.tmp[:, 1, :], ALU.add).then_inc(self.s_step, 1)
                        dve.wait_ge(self.s_step, 5 * m + 5)
                        nc.vector.tensor_tensor(self.prod[:, 2 + fb, cols], self.tmp[:, 2, :], self.tmp[:, 3, :], ALU.subtract).then_inc(self.s_prod, 1)
                    for c in range(KD):
                        m = KD * s + c
                        v = self.v[:, c, s * LAT:(s + 1) * LAT]
                        dve.wait_ge(self.y_scaled, m + 1)
                        nc.vector.scalar_tensor_tensor(v, v, vcol("hy_skip", c), self.ytmp[:, m % 2, :], ALU.mult, ALU.add).then_inc(self.y_skip, 1)
                        dve.wait_ge(self.y_skip, m + 1)
                        nc.vector.tensor_tensor(h[:, c, s * LAT:(s + 1) * LAT], v, self.u[:, c, s * LAT:(s + 1) * LAT], ALU.mult).then_inc(self.y_gated, 1)

        class S5:

            BATCH = 4
            NB = HALF // BATCH

            def __init__(self, pre, post, n_in, n):
                self.pre = pre
                self.u = area(0, GROUPS, 2 * CH)
                self.yf = area(27776, STEP, KD * CH)
                self.t = area(4096, 2, LAGS, GROUPS)
                self.b = area(7296, 2, GROUPS, GC)
                self.c = area(9344, 2, GROUPS, GC)
                self.f = area(11392, HALF, 2, P)
                self.m0 = area(19584, HALF, P)
                self.e = area(23680, HALF, 2, 2 * CH)
                self.pw = area(27776, self.BATCH, 2, P)
                self.et = area(28800, self.BATCH, 2, P)
                self.s2 = area(27776, HALF, 2, CH)
                self.t0 = area(29824, 512)
                self.gst = area(30336, self.BATCH, 240)
                self.lab = area(31296, 2, GROUPS, 2)
                self.mi = area(26880, 15, GROUPS)
                self.t1 = rstd
                self.lags = small[:, 20:20 + LAGS]
                self.rc = area(11392, 2, 8, P)
                self.rl = area(13440, 2, P)
                self.ldt = area(13696, GROUPS)
                self.rb = area(13760, 2, GROUPS, GC)
                self.w = area(15808, 5, LAGS, GROUPS)
                self.y = x[:, :, LAT:TOK]
                self.h_dram = nc.dram_tensor("s5_tokens", [P, KD * TOK], F32, kind="Internal").ap()
                self.y_dram = nc.dram_tensor("s5_outputs", [P, KD * LAT], F32, kind="Internal").ap()
                s = lambda n: sem("s5_" + n)
                self.h_stored, self.y_stored = s("h_stored"), s("y_stored")
                self.loaded, self.u_loaded, self.m_loaded, self.y_loaded = s("loaded"), s("u_loaded"), s("toeplitz_loaded"), s("y_loaded")
                self.turned, self.param, self.prep, self.act_prep = s("params_turned"), s("params_moved"), s("prep_step"), s("prep_act")
                self.in_step, self.in_ready, self.out_step, self.out_ready = s("in_step"), s("in_ready"), s("out_step"), s("out_ready")
                self.in_turned, self.et_moved = s("in_turned"), s("in_moved")
                self.g_summed, self.g_moved = s("taps_summed"), s("taps_moved")
                self.e_summed, self.e_moved = s("inject_summed"), s("inject_moved")
                self.step, self.s_moved = s("scan_step"), s("states_moved")
                self.y_summed, self.y_moved, self.skipped, self.gelu = s("y_summed"), s("y_moved"), s("skipped"), s("gelu")
                self.gate, self.glu, self.moved = s("glu_gate"), s("glu"), s("glu_moved")
                self.up = Gated("s5_glu", A["s5_w_glu"][0], D, lambda k: self.yf.rearrange("p s (k m) -> p k s m", m=CH)[:, k], LAT,
                                lambda pe, k: pe.wait_ge(self.gelu, k + 1), self.glu)
                self.post = post
                self.yk = self.yf.rearrange("p s (k m) -> p k s m", m=CH)

            def sync(self, sp):
                sp_issue(sp, self.up.w.p0 + RING)
                self.pre.wait(sp)
                sp.dma_start(self.h_dram, h[:, :, :].rearrange("p k t -> p (k t)")).then_inc(self.h_stored, 16)
                sp.wait_ge(self.h_stored, 16)
                for gl in range(8):
                    src = self.h_dram.rearrange("(g c) (s n) -> g s c n", c=GC, s=STEP)[gl]
                    dst = self.u[:, gl * 8:(gl + 1) * 8, :].rearrange("p g j -> p (g j)")
                    sp.dma_start(dst, src).then_inc(self.u_loaded, 16)
                for n in range(2 * self.NB):
                    hf, b = divmod(n, self.NB)
                    sp.wait_ge(self.g_moved, 2 * n + 2)
                    if n == self.NB:
                        sp.wait_ge(self.y_summed, 2)
                    for k in range(STEP):
                        sp.dma_start(self.m0[k * GC:(k + 1) * GC, b * self.BATCH:(b + 1) * self.BATCH, :],
                                     self.gst[0:GC, :, (7 - k) * GC:(7 - k) * GC + P]).then_inc(self.m_loaded, 16)
                for hf in range(2):
                    sp.wait_ge(self.y_moved, 2 * (hf + 1))
                    sp.dma_start(self.y_dram[:, hf * D:(hf + 1) * D].rearrange("p (g n) -> p g n", g=4),
                                 self.y[:, 4 * hf:4 * hf + 4, :]).then_inc(self.y_stored, 16)
                    sp.wait_ge(self.y_stored, 16 * (hf + 1))
                    if hf == 0:
                        sp.wait_ge(self.y_summed, 4)
                    for gl in range(4 * hf, 4 * hf + 4):
                        src = self.y_dram.rearrange("(s c) (g n) -> g c s n", c=GC, g=8)[gl]
                        sp.dma_start(self.yf[gl * GC:(gl + 1) * GC], src).then_inc(self.y_loaded, 16)

            def gpsimd(self, pool):
                self.pre.wait(pool)
                for i, (lam, cc, bb) in enumerate((("s5_lambda_re", "s5_c_re", "s5_b_re"), ("s5_lambda_im", "s5_c_im", "s5_b_im"))):
                    pool.dma_start(self.rl[0:GROUPS, i].rearrange("g (d s) -> g d s", d=2), A[lam][0].rearrange("d g s -> g d s")).then_inc(self.loaded, 16)
                    for d in range(2):
                        pool.dma_start(self.rc[:, i].rearrange("p k (d s) -> p k d s", d=2)[:, :, d, :],
                                       A[cc][0, d].rearrange("(k g) c s -> (g c) k s", k=8)).then_inc(self.loaded, 16)
                        pool.dma_start(self.rb[d * STATE:(d + 1) * STATE, i], A[bb][0, d].rearrange("g s c -> s g c")).then_inc(self.loaded, 16)
                for d in range(2):
                    pool.dma_start(self.ldt[d * STATE:(d + 1) * STATE], A["s5_log_dt"][0, d:d + 1, :].to_broadcast([STATE, GROUPS])).then_inc(self.loaded, 16)
                pool.dma_start(self.lags, A["k_s5_lags"]).then_inc(self.loaded, 16)
                pool.wait_ge(self.prep, self.PREP)
                for n in range(2 * self.NB):
                    hf, b = divmod(n, self.NB)
                    if n == self.NB:
                        pool.wait_ge(self.y_summed, 2)
                    g0 = n * self.BATCH
                    pr, pi = (self.lag(i, STEP, g0) for i in range(2))
                    cr, ci = (self.chan(self.c, i, g0) for i in range(2))
                    dst = [self.f[:, b * self.BATCH:(b + 1) * self.BATCH, i].rearrange("p g (s c) -> p g s c", c=GC) for i in range(2)]
                    t1 = self.t1[:, :].rearrange("p (g s c) -> p g s c", s=STEP, c=GC)
                    at = 6 * n
                    tt = nc.gpsimd.tensor_tensor
                    if n:
                        pool.wait_ge(self.out_step, at)
                    tt(dst[0], pr, cr, ALU.mult).then_inc(self.out_step, 1)
                    tt(dst[1], pr, ci, ALU.mult).then_inc(self.out_step, 1)
                    tt(t1, pi, ci, ALU.mult).then_inc(self.out_step, 1)
                    pool.wait_ge(self.out_step, at + 3)
                    tt(dst[0], dst[0], t1, ALU.add).then_inc(self.out_step, 1)
                    pool.wait_ge(self.out_step, at + 4)
                    tt(t1, pi, cr, ALU.mult).then_inc(self.out_step, 1)
                    pool.wait_ge(self.out_step, at + 5)
                    tt(dst[1], dst[1], t1, ALU.subtract).then_inc(self.out_step, 1)

            def lag(self, i, slot, g0):
                return self.t[:, i, slot:slot + STEP, self.of(g0)].rearrange("p s g -> p g s").unsqueeze(3) \
                    .to_broadcast([P, self.BATCH, STEP, GC])

            def of(self, place, n=None):
                g = place % 8 * 8 + place // 8
                return slice(g, g + 8 * ((n or self.BATCH) - 1) + 1, 8)

            def chan(self, src, i, g0):
                return src[:, i, self.of(g0), :].unsqueeze(2).to_broadcast([P, self.BATCH, STEP, GC])

            PREP = 43

            def vector(self, dve):
                V = nc.vector
                for i in range(2):
                    dve.wait_ge(self.turned, 1 + i)
                    V.tensor_copy(self.mi[:, i, :], bank[i][:, 0:GROUPS]).then_inc(self.param, 1)
                for n in range(4):
                    i, half = divmod(n, 2)
                    dve.wait_ge(self.turned, 3 + n)
                    dst = self.c[:, i, half * 32:(half + 1) * 32, :].rearrange("p g c -> p (g c)")
                    V.tensor_scalar(dst, bank[2 + n][:, :], -1.0 if i else 1.0, None, ALU.mult).then_inc(self.param, 1)
                dve.wait_ge(self.param, 6)
                dve.wait_ge(self.act_prep, 1)
                dve.wait_ge(self.loaded, 16 * 13)
                steps = [0]

                def then(ins):
                    steps[0] += 1
                    ins.then_inc(self.prep, 1)
                    dve.wait_ge(self.prep, steps[0])
                m = lambda j: self.mi[:, j, :]
                w = lambda j: self.w[:, j]
                lr, li, dt = m(0), m(1), m(2)
                lag3 = self.lags.unsqueeze(2).to_broadcast([P, LAGS, GROUPS])
                per = lambda v: v.unsqueeze(1).to_broadcast([P, LAGS, GROUPS])
                then(V.tensor_tensor(m(3), lr, dt, ALU.mult))
                then(V.tensor_tensor(m(4), li, dt, ALU.mult))
                then(V.tensor_tensor(w(0), lag3, per(m(3)), ALU.mult))
                then(V.tensor_tensor(w(1), lag3, per(m(4)), ALU.mult))
                then(V.tensor_scalar(w(2), w(1), 1.0 / TWO_PI, ROUND, ALU.mult, ALU.add))
                then(V.tensor_scalar(w(2), w(2), -ROUND, None, ALU.add))
                for c in (PI_HI, PI_MID, PI_LO):
                    then(V.scalar_tensor_tensor(w(1), w(2), -c, w(1), ALU.mult, ALU.add))
                then(V.tensor_scalar(w(1), w(1), PI_IN, -PI_IN, ALU.min, ALU.max))
                assert steps[0] == 10
                dve.wait_ge(self.act_prep, 5)
                then(V.tensor_tensor(w(4), w(2), w(2), ALU.mult))
                then(V.tensor_scalar(w(1), w(4), -2.0, 1.0, ALU.mult, ALU.add))
                then(V.tensor_tensor(self.t[:, 0], w(0), w(1), ALU.mult))
                then(V.tensor_tensor(self.t[:, 1], w(0), w(3), ALU.mult))
                e1, c1, q1 = self.w[:, 0, 16, :], self.w[:, 1, 16, :], self.w[:, 4, 16, :]
                then(V.scalar_tensor_tensor(m(5), e1, 1.0, m(5), ALU.add, ALU.mult))
                then(V.tensor_tensor(m(5), m(5), c1, ALU.mult))
                then(V.scalar_tensor_tensor(m(5), q1, -2.0, m(5), ALU.mult, ALU.add))
                xr, xi = m(5), self.t[:, 1, 16, :]
                then(V.tensor_tensor(m(8), lr, lr, ALU.mult))
                then(V.tensor_tensor(m(9), li, li, ALU.mult))
                then(V.tensor_tensor(m(8), m(8), m(9), ALU.add))
                then(V.reciprocal(m(8), m(8)))
                then(V.tensor_tensor(m(6), xr, lr, ALU.mult))
                then(V.tensor_tensor(m(9), xi, li, ALU.mult))
                then(V.tensor_tensor(m(6), m(6), m(9), ALU.add))
                then(V.tensor_tensor(m(6), m(6), m(8), ALU.mult))
                then(V.tensor_tensor(m(7), xi, lr, ALU.mult))
                then(V.tensor_tensor(m(9), xr, li, ALU.mult))
                then(V.tensor_tensor(m(7), m(7), m(9), ALU.subtract))
                then(V.tensor_tensor(m(7), m(7), m(8), ALU.mult))
                qr, qi = (m(j).unsqueeze(2).to_broadcast([P, GROUPS, GC]) for j in (6, 7))
                br, bi = self.rb[:, 0], self.rb[:, 1]
                tmp = self.w[:, 0:1].rearrange("p a b c -> p (a b c)")[:, 0:GROUPS * GC].rearrange("p (g c) -> p g c", c=GC)
                then(V.tensor_tensor(self.b[:, 0], qr, br, ALU.mult))
                then(V.tensor_tensor(tmp, qi, bi, ALU.mult))
                then(V.tensor_tensor(self.b[:, 0], self.b[:, 0], tmp, ALU.subtract))
                then(V.tensor_tensor(self.b[:, 1], qr, bi, ALU.mult))
                then(V.tensor_tensor(tmp, qi, br, ALU.mult))
                then(V.tensor_tensor(self.b[:, 1], self.b[:, 1], tmp, ALU.add))
                la, lb = self.lab[:, 0], self.lab[:, 1]
                l8r, l8i = (self.t[:, i, 17, :].rearrange("p (k g) -> p g k", k=8) for i in range(2))
                then(V.tensor_copy(la[:, :, 0].rearrange("p (g k) -> p g k", k=8), l8r))
                then(V.tensor_copy(la[:, :, 1].rearrange("p (g k) -> p g k", k=8), l8r))
                then(V.tensor_copy(lb[:, :, 0].rearrange("p (g k) -> p g k", k=8), l8i))
                then(V.tensor_scalar(lb[:, :, 1].rearrange("p (g k) -> p g k", k=8), l8i, -1.0, None, ALU.mult))
                while steps[0] < self.PREP:
                    then(V.tensor_copy(m(14), m(0)))
                assert steps[0] == self.PREP, steps[0]
                t0 = self.t0[:, :].rearrange("p (g s c) -> p g s c", s=STEP, c=GC)

                def inputs(n):
                    g0 = n * self.BATCH
                    pr, pi = (self.lag(i, 0, g0) for i in range(2))
                    br, bi = (self.chan(self.b, i, g0) for i in range(2))
                    dst = [self.pw[:, :, i].rearrange("p g (s c) -> p g s c", c=GC) for i in range(2)]
                    at = 5 * n
                    if n:
                        dve.wait_ge(self.in_turned, 2 * n)
                    if n == self.NB:
                        dve.wait_ge(self.y_summed, 2)
                    tt = V.tensor_tensor
                    tt(dst[0], pr, br, ALU.mult).then_inc(self.in_step, 1)
                    tt(dst[1], pr, bi, ALU.mult).then_inc(self.in_step, 1)
                    tt(t0, pi, bi, ALU.mult).then_inc(self.in_step, 1)
                    dve.wait_ge(self.in_step, at + 3)
                    tt(dst[0], dst[0], t0, ALU.subtract).then_inc(self.in_step, 1)
                    dve.wait_ge(self.in_step, at + 4)
                    tt(t0, pi, br, ALU.mult).then_inc(self.in_step, 1)
                    dve.wait_ge(self.in_step, at + 5)
                    tt(dst[1], dst[1], t0, ALU.add).then_inc(self.in_ready, 1)

                def taps_out(n):
                    for q in range(2):
                        dve.wait_ge(self.g_summed, 2 * n + q + 1)
                        if n and q == 0:
                            dve.wait_ge(self.m_loaded, 16 * STEP * n)
                        taps = [bank[i + q][0:GC, 0:480].rearrange("p (g n) -> p g n", g=2) for i in (2, 5)]
                        V.tensor_copy(self.gst[0:GC, 2 * q:2 * q + 2, 0:112], taps[1][:, :, 0:112])
                        V.tensor_copy(self.gst[0:GC, 2 * q:2 * q + 2, 112:240], taps[0][:, :, 112:240]).then_inc(self.g_moved, 1)

                steps2 = [0]

                def scan(ins):
                    steps2[0] += 1
                    ins.then_inc(self.step, 1)
                    dve.wait_ge(self.step, steps2[0])
                for hf in range(2):
                    inputs(hf * self.NB)
                    for b in range(self.NB):
                        n = hf * self.NB + b
                        if b + 1 < self.NB:
                            inputs(n + 1)
                        taps_out(n)
                    dve.wait_ge(self.e_moved, 2 * self.NB * (hf + 1))
                    dve.wait_ge(self.out_step, 6 * self.NB * (hf + 1))
                    blocks = 2 * CH // BLK
                    sa, sb_ = (v[:, hf * HALF:(hf + 1) * HALF, :] for v in (la, lb))
                    wide = lambda v: v.unsqueeze(3).to_broadcast([P, HALF, 2, blocks])
                    ta, tb = (v[:, 0:HALF * 2 * blocks].rearrange("p (g r b) -> p g r b", r=2, b=blocks) for v in (self.t0, self.t1))
                    e5 = self.e.rearrange("p g r (b q) -> p g r b q", q=BLK)
                    base = steps2[0]
                    with dve.Fori(1, BLK) as i:
                        prev = e5[:, :, :, :, bass.ds(i - 1, 1)].rearrange("p g r b o -> p g r (b o)")
                        cur = e5[:, :, :, :, bass.ds(i, 1)].rearrange("p g r b o -> p g r (b o)")
                        V.tensor_tensor(ta, wide(sa), prev, ALU.mult).then_inc(self.step, 1)
                        V.tensor_tensor(tb[:, :, ::-1, :], wide(sb_), prev, ALU.mult).then_inc(self.step, 1)
                        dve.wait_ge(self.step, base + 4 * i - 2)
                        V.tensor_tensor(ta, ta, tb, ALU.add).then_inc(self.step, 1)
                        dve.wait_ge(self.step, base + 4 * i - 1)
                        V.tensor_tensor(cur, cur, ta, ALU.add).then_inc(self.step, 1)
                        dve.wait_ge(self.step, base + 4 * i)
                    steps2[0] += 4 * (BLK - 1)
                    def table(i, slot0, n):
                        v = self.t[:, i, slot0:slot0 + n, :].rearrange("p q (k g) -> p g k q", k=8)
                        return v[:, 4 * hf:4 * hf + 4]
                    halfv = lambda v: v.rearrange("p (g k) q -> p g k q", k=8)
                    er, ei = (self.e[:, :, r, :] for r in range(2))
                    s0, s1 = (v[:, 0:HALF].unsqueeze(2) for v in (self.t0, self.t1))
                    c_r, c_i = table(0, 24, 1), table(1, 24, 1)
                    for blk in range(1, blocks):
                        pcol, ccol = BLK * blk - 1, BLK * blk + BLK - 1
                        pr_, pi_ = halfv(er[:, :, pcol:pcol + 1]), halfv(ei[:, :, pcol:pcol + 1])
                        for c, (va, vb, op) in ((er, (pr_, pi_, ALU.subtract)), (ei, (pi_, pr_, ALU.add))):
                            cc = c[:, :, ccol:ccol + 1]
                            V.tensor_tensor(halfv(s0), c_r, va, ALU.mult)
                            scan(V.tensor_tensor(halfv(s1), c_i, vb, ALU.mult))
                            scan(V.tensor_tensor(s0, s0, s1, op))
                            scan(V.tensor_tensor(cc, cc, s0, ALU.add))
                    nq = BLK - 1
                    for b0 in range(4, 8, 2):
                        for gl in range(4):
                            gs = slice(8 * gl, 8 * gl + 8)
                            lv = lambda v: v[:, gs, BLK * b0:BLK * (b0 + 2)].rearrange("p g (b q) -> p g b q", q=BLK)[:, :, :, 0:nq]
                            ends = lambda v: v[:, gs, BLK * b0 - 1:BLK * b0 + BLK:BLK].unsqueeze(3).to_broadcast([P, 8, 2, nq])
                            tq = [self.t[:, i, 17:17 + nq, 4 * hf + gl:GROUPS:8].rearrange("p q k -> p k q").unsqueeze(2).to_broadcast([P, 8, 2, nq]) for i in range(2)]
                            u0, u1, u2, u3 = ((self.t0, self.t1)[i // 2][:, (i % 2) * 112:(i % 2) * 112 + 112].rearrange("p (g b q) -> p g b q", b=2, q=nq)
                                              for i in range(4))
                            V.tensor_tensor(u0, tq[0], ends(er), ALU.mult)
                            V.tensor_tensor(u1, tq[1], ends(ei), ALU.mult)
                            V.tensor_tensor(u2, tq[0], ends(ei), ALU.mult)
                            scan(V.tensor_tensor(u3, tq[1], ends(er), ALU.mult))
                            V.tensor_tensor(u0, u0, u1, ALU.subtract)
                            scan(V.tensor_tensor(u2, u2, u3, ALU.add))
                            V.tensor_tensor(lv(er), lv(er), u0, ALU.add)
                            scan(V.tensor_tensor(lv(ei), lv(ei), u2, ALU.add))
                    V.tensor_copy(self.s2[0:STATE], self.e[0:STATE, :, :, CH - 1:2 * CH - 1]).then_inc(self.s_moved, 1)
                    V.tensor_copy(self.s2[STATE:P], self.e[STATE:P, :, :, 2 * CH - 2:CH - 2:-1]).then_inc(self.s_moved, 1)
                    for q in range(2):
                        dve.wait_ge(self.y_summed, 2 * hf + q + 1)
                        gl = 4 * hf + 2 * q
                        V.tensor_copy(self.y[:, gl:gl + 2, :], bank[5 + q][:, :].rearrange("p (g n) -> p g n", g=2)).then_inc(self.y_moved, 1)
                dve.wait_ge(self.y_loaded, 16 * 8)
                for k in range(KD):
                    yv = self.yk[:, k]
                    V.scalar_tensor_tensor(yv, h_split[:, :, k, 0, :], vcol("s5_d", k), yv, ALU.mult, ALU.add).then_inc(self.skipped, 1)
                for c in range(KD):
                    dve.wait_ge(self.gate, c + 1)
                    dst = Y[:, c, 0:LAT].rearrange("p (m s) -> p s m", s=STEP)
                    V.scalar_tensor_tensor(dst, self.up.bank(c, 0)[:, 0:LAT].rearrange("p (s m) -> p s m", m=CH), vcol("s5_b_glu", c),
                                           self.sig[:, c % 2, :].rearrange("p (s m) -> p s m", m=CH), ALU.add, ALU.mult).then_inc(self.glu, 1)

            def tensor(self, pe):
                self.pre.wait(pe)
                pe.wait_ge(self.loaded, 16 * 13)
                for i in range(2):
                    nc.tensor.transpose(bank[i][:, 0:GROUPS], self.rl[0:GROUPS, i, :], ident[0:GROUPS, 0:GROUPS]).then_inc(self.turned, 1)
                for n in range(4):
                    i, half = divmod(n, 2)
                    for q in range(4):
                        last = nc.tensor.transpose(bank[2 + n][:, q * P:(q + 1) * P], self.rc[:, i, 4 * half + q, :], ident[:, :])
                    last.then_inc(self.turned, 1)
                pe.wait_ge(self.param, 6)
                pe.wait_ge(self.u_loaded, 16 * 8)
                for hf in range(2):
                    for b in range(self.NB):
                        n = hf * self.NB + b
                        g0 = n * self.BATCH
                        pe.wait_ge(self.in_ready, n + 1)
                        for q in range(2):
                            if n:
                                pe.wait_ge(self.et_moved, 2 * n)
                            for j in range(4):
                                last = nc.tensor.transpose(bank[q][:, j * P:(j + 1) * P], self.pw[:, 2 * q + j // 2, j % 2, :], ident[:, :])
                            last.then_inc(self.in_turned, 1)
                        pe.wait_ge(self.out_step, 6 * (n + 1))
                        for q in range(2):
                            if n:
                                pe.wait_ge(self.g_moved, 2 * n - 1 + q)
                            for j in range(2):
                                gb = 2 * q + j
                                g, gh = self.of(g0 + gb, 1).start, b * self.BATCH + gb
                                if n == self.NB:
                                    pe.wait_ge(self.y_moved, 2)
                                for lo, hi, rows, rhs in (
                                        (112, 128, slice(0, P), lambda i: self.c[:, i, g, :]),
                                        (128, 240, slice(0, STATE), lambda i: self.f[0:STATE, gh, i, 0:112]),
                                        (0, 112, slice(STATE, P), lambda i: self.f[STATE:P, gh, i, 16:P])):
                                    for i in range(2):
                                        last = nc.tensor.matmul(bank[(2 if lo else 5) + q][0:GC, j * 240 + lo:j * 240 + hi], self.b[rows, i, g, :], rhs(i),
                                                                start=(i == 0), stop=(i == 1))
                            last.then_inc(self.g_summed, 1)
                        pe.wait_ge(self.et_moved, 2 * n + 2)
                        if n:
                            pe.wait_ge(self.e_moved, 2 * n)
                        for gb in range(self.BATCH):
                            for i in range(2):
                                o = (2 * gb + i) * 2 * CH
                                last = nc.tensor.matmul(bank[4][:, o:o + 2 * CH], self.et[:, gb, i, :], self.u[:, g0 + gb, :],
                                                        start=True, stop=True)
                        last.then_inc(self.e_summed, 1)
                    pe.wait_ge(self.m_loaded, 16 * STEP * self.NB * (hf + 1))
                    pe.wait_ge(self.s_moved, 2 * hf + 2)
                    for q in range(2):
                        for j in range(16):
                            gh = q * 16 + j
                            g = hf * HALF + gh
                            o = bank[5 + q][:, j * CH:(j + 1) * CH]
                            nc.tensor.matmul(o, self.m0[:, gh, :], self.u[:, g, 0:CH], start=True, stop=False)
                            nc.tensor.matmul(o, self.f[:, gh, 0, :], self.s2[:, gh, 0, :], start=False, stop=False)
                            last = nc.tensor.matmul(o, self.f[:, gh, 1, :], self.s2[:, gh, 1, :], start=False, stop=True)
                        last.then_inc(self.y_summed, 1)
                self.up.tensor(pe)

            @property
            def sig(self):
                return area(23680, 2, LAT)

            def scalar(self, act):
                act.wait_ge(self.loaded, 16 * 13)
                nc.scalar.activation(self.mi[:, 2, :], self.ldt, ACT.Exp).then_inc(self.act_prep, 1)
                act.wait_ge(self.prep, 10)
                nc.scalar.activation(self.w[:, 0], self.w[:, 0], ACT.Exp).then_inc(self.act_prep, 1)
                nc.scalar.activation(self.mi[:, 5, :], self.mi[:, 3, :], ACT.Tanh, scale=0.5).then_inc(self.act_prep, 1)
                nc.scalar.activation(self.w[:, 2], self.w[:, 1], ACT.Sin, scale=0.5).then_inc(self.act_prep, 1)
                nc.scalar.activation(self.w[:, 3], self.w[:, 1], ACT.Sin).then_inc(self.act_prep, 1)
                for n in range(2 * self.NB):
                    hf, b = divmod(n, self.NB)
                    for q in range(2):
                        act.wait_ge(self.in_turned, 2 * n + q + 1)
                        if n:
                            act.wait_ge(self.e_summed, n)
                        if n == self.NB:
                            act.wait_ge(self.y_summed, 2)
                        nc.scalar.activation(self.et[:, 2 * q:2 * q + 2].rearrange("p g i n -> p (g i n)"), bank[q][:, :], ACT.Copy).then_inc(self.et_moved, 1)
                    act.wait_ge(self.e_summed, n + 1)
                    if n == self.NB:
                        act.wait_ge(self.s_moved, 2)
                    dst = self.e[:, b * self.BATCH:(b + 1) * self.BATCH]
                    src = bank[4][:, :].rearrange("p (g z m) -> p g z m", z=2, m=CH)
                    fw = dst[0:STATE].rearrange("p g r (z m) -> p (g r) z m", m=CH)
                    nc.scalar.activation(fw[:, :, ::-1, :], src[0:STATE], ACT.Copy).then_inc(self.e_moved, 1)
                    bw = dst[STATE:P].rearrange("p g r j -> p (g r) j")
                    nc.scalar.activation(bw[:, :, ::-1], bank[4][STATE:P, :].rearrange("p (g j) -> p g j", j=2 * CH), ACT.Copy).then_inc(self.e_moved, 1)
                for k in range(KD):
                    act.wait_ge(self.skipped, k + 1)
                    nc.scalar.activation(self.yk[:, k], self.yk[:, k], ACT.Gelu).then_inc(self.gelu, 1)
                def take(c):
                    act.wait_ge(self.glu, c + 1)
                    self.post.move(act, c, Y[:, c, :]).then_inc(self.moved, 1)
                for c in range(KD):
                    self.up.summed(act, c, 1)
                    if c >= 2:
                        act.wait_ge(self.glu, c - 1)
                    nc.scalar.activation(self.sig[:, c % 2, :], self.up.bank(c, 1)[:, 0:LAT], ACT.Sigmoid,
                                         bias=vcol("s5_b_glu", KD + c)).then_inc(self.gate, 1)
                    if c >= 1:
                        take(c - 1)
                take(KD - 1)

        class Fnet:

            def __init__(self, pre, post, n_in, n):
                self.pre = pre
                self.loaded, self.chan, self.chan_moved = sem("fn_loaded"), sem("fn_channels"), sem("fn_channels_moved")
                self.tok, self.tok_moved = sem("fn_tokens"), sem("fn_tokens_moved")
                at = 2 * KD * TOK
                self.cs = area(at, 2 * P)
                self.tt = area(at + 256, 2, 2, LAT)
                self.a = area(at + 1280, 2, KD, 2 * P)
                self.f = area(at + 1280 + 4096, KD, LAT)
                self.proj = Linear("fn_out", A["fn_w_o"][0], KD, lambda k: self.f[:, k, :], LAT,
                                   lambda pe, k: pe.wait_ge(self.tok_moved, k // 2 + 1),
                                   lambda act, c, b: post.move(act, c, b, "fn_b_o"))

            def sync(self, sp):
                sp_issue(sp, self.proj.w.p0)
                self.pre.wait_x(sp)
                sp.dma_start(self.cs, A["k_dft128"]).then_inc(self.loaded, 16)
                sp.dma_start(self.tt, A["k_dft256"]).then_inc(self.loaded, 16)

            def tensor(self, pe):
                self.pre.wait(pe)
                pe.wait_ge(self.loaded, 32)
                for t in range(2):
                    for g2 in range(KD // 2):
                        n = 4 * t + g2
                        if n >= 4:
                            pe.wait_ge(self.chan_moved, n - 3)
                        for q in range(2):
                            g = 2 * g2 + q
                            last = nc.tensor.matmul(bank[n % 4][:, q * 256:(q + 1) * 256], h[:, g, t * P:(t + 1) * P],
                                                    self.cs[:, :], start=True, stop=True)
                        last.then_inc(self.chan, 1)
                for g2 in range(KD // 2):
                    pe.wait_ge(self.chan_moved, 5 + g2)
                    for q in range(2):
                        g = 2 * g2 + q
                        for t in range(2):
                            for part in range(2):
                                last = nc.tensor.matmul(bank[g2][:, q * 256:(q + 1) * 256],
                                                        self.a[:, t, g, part * P:(part + 1) * P],
                                                        self.tt[:, part, t, :], start=(t + part == 0), stop=(t + part == 2))
                    last.then_inc(self.tok, 1)
                self.proj.tensor(pe)

            def vector(self, dve):
                for n in range(8):
                    t, g2 = divmod(n, 4)
                    dve.wait_ge(self.chan, n + 1)
                    nc.vector.tensor_copy(self.a[:, t, 2 * g2:2 * g2 + 2, :].rearrange("p g c -> p (g c)"), bank[n % 4][:, :]).then_inc(self.chan_moved, 1)
                for g2 in range(KD // 2):
                    dve.wait_ge(self.tok, g2 + 1)
                    nc.vector.tensor_copy(self.f[:, 2 * g2:2 * g2 + 2, :].rearrange("p g c -> p (g c)"), bank[g2][:, :]).then_inc(self.tok_moved, 1)

            def scalar(self, act):
                self.proj.scalar(act)

        MIXER = {0: Mla, 1: Hyena, 2: S5, 3: Fnet}
        stages = [Setup()]
        live = [l for l in range(DEPTH) if l in layers]
        mods = {l: Modulation(l) for l in live}
        stages.append(mods[live[0]].part(0))
        for l in live:
            mod = mods[l]
            n_in = TOK if l < 3 else LAT
            n_out = TOK if l < 2 else LAT
            pre = PreNorm(mod, False, n_in, split=(l == 2))
            gate = mod.part(1)
            post = PostNorm(mod, False, n_out)
            mixer = MIXER[l](pre, post, n_in, n_out)
            post.number()
            scale2 = mod.part(2)
            pre2 = PreNorm(mod, True, n_out)
            gate2 = mod.part(3)
            post2 = PostNorm(mod, True, n_out)
            ffn = Ffn(l, n_out, pre2, post2)
            post2.number()
            stages += [pre, gate, mixer, post, scale2, pre2, gate2, ffn, post2]
            if l != live[-1]:
                stages.append(mods[live[live.index(l) + 1]].part(0))

        out_turned = sem("out_turned")
        out_moved = sem("out_moved")
        stored = sem("stored")
        orow = area(2 * KD * TOK, 2, D)

        class Store:

            def tensor(self, pe):
                for t in range(2):
                    for half in range(2):
                        for q in range(4):
                            k = 4 * half + q
                            if t == 0:
                                post2.wait(pe, k)
                            last = nc.tensor.transpose(bank[2 * t + half][:, q * P:(q + 1) * P],
                                                       x[:, k, t * P:(t + 1) * P], ident[:, :])
                        last.then_inc(out_turned, 1)

            def vector(self, dve):
                for t in range(2):
                    for half in range(2):
                        dve.wait_ge(out_turned, 2 * t + half + 1)
                        nc.vector.tensor_copy(orow[:, t, half * 512:(half + 1) * 512], bank[2 * t + half][:, :]).then_inc(out_moved, 1)

            def sync(self, sp):
                for t in range(2):
                    sp.wait_ge(out_moved, 2 * t + 2)
                    sp.dma_start(out[0, t * P:(t + 1) * P, :], orow[:, t, :]).then_inc(stored, 16)
                sp.wait_ge(stored, 32)
        stages.append(Store())

        block = ctx.enter_context(nc.Block())

        @block.sync
        def _(sp):
            for s in stages[:-1]:
                if hasattr(s, "sync"):
                    s.sync(sp)
            sp_issue(sp, len(panels))
            stages[-1].sync(sp)

        @block.scalar
        def _(act):
            for s in stages:
                if hasattr(s, "scalar"):
                    s.scalar(act)

        @block.vector
        def _(dve):
            for s in stages:
                if hasattr(s, "vector"):
                    s.vector(dve)

        @block.gpsimd
        def _(pool):
            for s in stages:
                if hasattr(s, "gpsimd"):
                    s.gpsimd(pool)

        @block.tensor
        def _(pe):
            for s in stages:
                if hasattr(s, "tensor"):
                    s.tensor(pe)


def constants():
    f8 = np.float64
    c = {}
    ch = np.arange(P, dtype=f8)
    ang = 2 * np.pi * np.outer(ch, ch) / P
    c["k_dft128"] = np.concatenate([np.cos(ang), np.sin(ang)], axis=1) / math.sqrt(LAT * P)
    t = np.arange(LAT, dtype=f8)
    ang = 2 * np.pi * (np.outer(t, t) % LAT) / LAT
    c["k_dft256"] = np.stack([np.cos(ang), -np.sin(ang)]).reshape(2, 2, P, LAT).transpose(2, 0, 1, 3)
    tok = np.arange(LAT)
    freq = 1.0 / 10000.0 ** (np.arange(0, 32, 2, dtype=f8) / 32)
    row, col = np.outer(freq, tok // 64), np.outer(freq, tok % 64)
    ang = np.concatenate([row, row, col, col])
    c["k_rope"] = np.stack([np.cos(ang), np.sin(ang)], axis=1)
    turn = np.zeros((ROPE, ROPE))
    for b in (0, 32):
        for i in range(16):
            turn[b + 16 + i, b + i] = -1.0
            turn[b + i, b + 16 + i] = 1.0
    c["k_turn"] = turn
    f4 = np.float32
    tt = np.linspace(0.0, 1.0, LAT, dtype=f4)[:, None]
    w = f4(2.0 * math.pi / LAT) * np.arange(LAT, dtype=f4)[:, None]
    bands = np.linspace(1e-4, BANDS - 1, BANDS, dtype=f4)[None, :]
    c["k_hyena_z"] = np.concatenate([tt, np.cos(w * bands), -np.sin(w * bands)], axis=1).T
    deltas = np.abs(np.linspace(math.log(1e-2) / 1.5, math.log(1e-2) / 0.3, D, dtype=f4))
    c["k_hyena_decay"] = np.exp(-tt * deltas).reshape(2, P, D).transpose(1, 0, 2)
    ang = np.pi * (np.outer(t, 2 * np.arange(LAT) + 1) % (4 * LAT)) / (2 * LAT)
    cs = np.stack([np.cos(ang), np.sin(ang)])
    c["k_dft_odd"] = cs.reshape(2, 2, P, LAT).transpose(2, 0, 1, 3)
    ics = np.stack([cs[0].T, -cs[1].T]) / LAT
    c["k_idft_odd"] = ics.reshape(2, 2, P, LAT).transpose(2, 0, 1, 3)
    k = np.arange(STEP)
    chunks = STEP * np.arange(1, BLK + 1)
    fwd = np.concatenate([STEP - 1 - k, k + 1, [1], chunks])
    bwd = np.concatenate([k, STEP - k, [1], chunks])
    c["k_s5_lags"] = np.repeat(np.stack([fwd, bwd]), STATE, axis=0)
    return {k: np.ascontiguousarray(v.astype(np.float32)) for k, v in c.items()}


def kernel(**inputs):
    import concourse.bacc as bacc
    from concourse.bass_utils import run_bass_kernel_spmd

    nc = bacc.Bacc("TRN2", target_bir_lowering=False, num_devices=1)
    arrays = {name: np.ascontiguousarray(a) for name, a in inputs.items()}
    arrays.update(constants())
    A = {name: nc.dram_tensor(name, a.shape, mybir.dt.from_np(a.dtype), kind="ExternalInput").ap()
         for name, a in arrays.items()}
    out = nc.dram_tensor("out", (1, LAT, D), F32, kind="ExternalOutput").ap()
    build(nc, A, out)
    r = run_bass_kernel_spmd(nc, [arrays], core_ids=[0])
    return r.results[0]["out"]
```

```python
import math
from contextlib import ExitStack

import numpy as np

import concourse.bass as bass
from concourse import mybir

F32 = mybir.dt.float32
F32R = mybir.dt.float32r
ACT = mybir.ActivationFunctionType
ALU = mybir.AluOpType
AX = mybir.AxisListType

P = 128
D = 1024
KD = D // P
LAT = 256
CTX = 256
TOK = LAT + CTX
DEPTH = 4
MODS = 6
FFN = 2816
KF = FFN // P
EPS = 1e-6

HEADS = 8
NOPE = 128
ROPE = 64
VDIM = 128
KVR = 256
QR = 768

BANDS = 16
EMB = 2 * BANDS + 1
WIDTH = 64

GROUPS = 64
GC = 16
STATE = 64
STEP = 8
CH = LAT // STEP
HALF = GROUPS // 2
BLK = 8
LAGS = 2 * STEP + 1 + BLK

RING = 2
SPLIT = 2
SLOT = 12 * 256
UP_CHUNKS = (12, 10)
ARENA = 32768

TWO_PI = 2.0 * math.pi
ROUND = 1.5 * 2.0 ** 23
PI_HI = 6.28125
PI_MID = float(np.float32(TWO_PI - PI_HI))
PI_LO = float(np.float32(TWO_PI - PI_HI - PI_MID))
PI_IN = 3.1415925

VEC = {}


def _rows():
    tiles = [
        [("mod_b01", 2 * MODS * KD)],
        [("mod_b23", 2 * MODS * KD)],
        [("mix_pre_g", DEPTH * KD), ("mix_post_g", DEPTH * KD), ("ffn_pre_g", DEPTH * KD), ("ffn_post_g", DEPTH * KD)],
        [("hy_b_in", 24), ("hy_conv_w", 72), ("hy_conv_b", 24)],
        [("hy_skip", 8), ("hy_b_out", 8), ("s5_d", 8), ("s5_b_glu", 16), ("fn_b_o", 8),
         ("mla_q_norm_g", 6), ("mla_kv_norm_g", 2), ("c", 8), ("c_ctx", 8)],
    ]
    for t, rows in enumerate(tiles):
        at = 0
        for name, n in rows:
            VEC[name] = (t, at, n)
            at += n
    return [sum(n for _, n in rows) for rows in tiles]


VEC_ROWS = _rows()


def region_base(nc, region):
    return nc.sbuf_base - int(np.prod(region.shape[1:]))


def build(nc, A, out, layers=(0, 1, 2, 3)):
    ctx = ExitStack()
    with ctx:
        def sb(name, shape):
            return ctx.enter_context(nc.sbuf_tensor(name, shape, F32))

        def sem(name):
            return ctx.enter_context(nc.semaphore(name))

        region = ctx.enter_context(nc.sbuf_tensor("region", [P, (2 * KD * TOK + ARENA) * 4], mybir.dt.uint8))
        base = region_base(nc, region)

        def place(name, at, shape, dtype=F32):
            return nc.alloc_sbuf_tensor_at(name, [P] + shape, dtype, offset=base + 4 * at)

        h = place("h_sb", 0, [KD, TOK])
        arena = place("arena", KD * TOK, [ARENA])
        h_hi = place("h_hi", 0, [KD, TOK], F32R)
        at = KD * TOK + 2 * KD * TOK
        w_hi, w_lo = (place(n, at + i * SPLIT * SLOT, [SPLIT, SLOT], F32R) for i, n in enumerate(("w_hi", "w_lo")))
        at += 2 * SPLIT * SLOT
        g_hi, g_lo = (place(n, at + i * UP_CHUNKS[0] * TOK, [UP_CHUNKS[0], TOK], F32R) for i, n in enumerate(("g_hi", "g_lo")))
        h_lo = place("h_lo", KD * TOK + ARENA, [KD, TOK], F32R)
        at += 2 * UP_CHUNKS[0] * TOK
        assert at <= KD * TOK + ARENA
        mod_rows = place("mod_rows", KD * TOK + ARENA, [2 * D])
        gate_rows = place("gate_rows", at - D, [D])
        x = sb("x_sb", [P, KD, TOK])
        ring = sb("ring", [P, RING, SLOT])
        vec = sb("vec", [P, 5, P])
        rstd = sb("rstd", [P, TOK])
        ident = sb("ident", [P, P])
        ones = sb("ones", [P, P])
        silu_c = sb("silu_c", [P, KD, 2])
        modv = sb("modv", [P, 2, MODS * KD, 2])
        affine = sb("affine", [P, 2, 6, KD, 2])
        small = sb("small", [P, 64])
        bank = [ctx.enter_context(nc.psum_tensor(f"bank{i}", [P, 512], F32)) for i in range(8)]
        SUMS, MODP = bank[6], bank[7]


        def area(at, *dims):
            n = int(np.prod(dims))
            assert at + n <= ARENA, (at, n)
            v = arena[:, at:at + n]
            if len(dims) == 2:
                v = v.rearrange("p (a b) -> p a b", b=dims[1])
            if len(dims) == 3:
                v = v.rearrange("p (a b c) -> p a b c", b=dims[1], c=dims[2])
            if len(dims) == 4:
                v = v.rearrange("p (a b c d) -> p a b c d", b=dims[1], c=dims[2], d=dims[3])
            return v

        def vcol(name, j, n=1):
            t, at, _ = VEC[name]
            return vec[:, t, at + j:at + j + n]

        w_arrived = [sem(f"w_arrived{i}") for i in range(RING)]
        panels = []
        slot_count = [0] * RING

        class Weights:

            def __init__(self, sources, freed):
                self.p0 = len(panels)
                self.arrived = []
                for i, loads in enumerate(sources):
                    slot = len(panels) % RING
                    slot_count[slot] += 16 * len(loads)
                    self.arrived.append((slot, slot_count[slot]))
                    panels.append((loads, freed(i)))

            def slot(self, i):
                return ring[:, (self.p0 + i) % RING, :]

            def view(self, i, kk, width):
                return self.slot(i)[:, 0:kk * width].rearrange("p (k n) -> p k n", n=width)

            def wait(self, pe, i):
                slot, value = self.arrived[i]
                pe.wait_ge(w_arrived[slot], value)

        def cols_of(w, c0, n):
            return w[:, c0:c0 + n].rearrange("(k p) n -> p k n", p=P)

        issued = [0]

        def sp_issue(sp, upto):
            while issued[0] < min(upto, len(panels)):
                p = issued[0]
                if p >= RING:
                    sp.wait_ge(*panels[p - RING][1])
                at = 0
                for src in panels[p][0]:
                    kk, nn = src.shape[1], src.shape[2]
                    dst = ring[:, p % RING, at:at + kk * nn].rearrange("p (k n) -> p k n", n=nn)
                    at += kk * nn
                    sp.dma_start(dst, src).then_inc(w_arrived[p % RING], 16)
                issued[0] += 1

        vec_loaded = sem("vec_loaded")
        consts_set = sem("consts_set")
        vec_turned = sem("vec_turned")
        vec_ready = sem("vec_ready")
        silu_ready = sem("silu_ready")
        x_loaded = sem("x_loaded")
        rows = area(0, 5, P)
        xrow = area(2 * KD * TOK, 4, D)
        x_turned = sem("x_turned")
        x_ready = sem("x_ready")

        class Setup:
            def sync(self, sp):
                sp.dma_start(xrow[:, 0:2, :], A["x"][0].rearrange("(b p) d -> p b d", p=P)).then_inc(x_loaded, 16)
                sp.dma_start(xrow[:, 2:4, :], A["ctx"][0].rearrange("(b p) d -> p b d", p=P)).then_inc(x_loaded, 16)

            def scalar(self, act):
                loads = [
                    ("mod_b01", A["mod_b"][0:2].rearrange("l (j p) -> (l j) p", p=P)),
                    ("mod_b23", A["mod_b"][2:4].rearrange("l (j p) -> (l j) p", p=P)),
                    ("mix_pre_g", A["mix_pre_g"].rearrange("l (j p) -> (l j) p", p=P)),
                    ("mix_post_g", A["mix_post_g"].rearrange("l (j p) -> (l j) p", p=P)),
                    ("ffn_pre_g", A["ffn_pre_g"].rearrange("l (j p) -> (l j) p", p=P)),
                    ("ffn_post_g", A["ffn_post_g"].rearrange("l (j p) -> (l j) p", p=P)),
                    ("hy_b_in", A["hy_b_in"][0].rearrange("(j p) -> j p", p=P)),
                    ("hy_conv_w", A["hy_conv_w"][0].rearrange("w (j p) -> (w j) p", p=P)),
                    ("hy_conv_b", A["hy_conv_b"][0].rearrange("(j p) -> j p", p=P)),
                    ("hy_skip", A["hy_skip"][0, 0].rearrange("(j p) -> j p", p=P)),
                    ("hy_b_out", A["hy_b_out"][0].rearrange("(j p) -> j p", p=P)),
                    ("s5_d", A["s5_d"][0].rearrange("(j p) -> j p", p=P)),
                    ("s5_b_glu", A["s5_b_glu"][0].rearrange("(j p) -> j p", p=P)),
                    ("fn_b_o", A["fn_b_o"][0].rearrange("(j p) -> j p", p=P)),
                    ("mla_q_norm_g", A["mla_q_norm_g"][0].rearrange("(j p) -> j p", p=P)),
                    ("mla_kv_norm_g", A["mla_kv_norm_g"][0].rearrange("(j p) -> j p", p=P)),
                    ("c", A["c"][0].rearrange("(j p) -> j p", p=P)),
                    ("c_ctx", A["c_ctx"].rearrange("(j p) -> j p", p=P)),
                ]
                for name, src in loads:
                    t, at, n = VEC[name]
                    act.dma_start(rows[at:at + n, t, :], src).then_inc(vec_loaded, 16)
                self.n_loads = len(loads)
                act.wait_ge(vec_ready, 5)
                nc.scalar.activation(silu_c[:, :, 0], vcol("c", 0, KD), ACT.Silu).then_inc(silu_ready, 1)
                nc.scalar.activation(silu_c[:, :, 1], vcol("c_ctx", 0, KD), ACT.Silu).then_inc(silu_ready, 1)

            def gpsimd(self, pool):
                nc.gpsimd.memset(ones[:, :], 1.0).then_inc(consts_set, 1)
                nc.gpsimd.memset(ident[:, :], 0.0).then_inc(consts_set, 1)
                pool.wait_ge(consts_set, 2)
                nc.gpsimd.affine_select(out=ident[:, :], in_=ident[:, :], compare_op=ALU.not_equal, fill=1.0, base=0,
                                        pattern=[[-1, P]], channel_multiplier=1).then_inc(consts_set, 1)

            def tensor(self, pe):
                pe.wait_ge(consts_set, 3)
                pe.wait_ge(vec_loaded, 16 * 18)
                for t, n in enumerate(VEC_ROWS):
                    nc.tensor.transpose(bank[t][:, 0:n], rows[0:n, t, :], ident[0:n, 0:n]).then_inc(vec_turned, 1)
                pe.wait_ge(vec_ready, 5)
                pe.wait_ge(x_loaded, 32)
                for k in range(KD):
                    b = 4 + k % 2
                    if k >= 2:
                        pe.wait_ge(x_ready, k - 1)
                    for t in range(4):
                        last = nc.tensor.transpose(bank[b][:, t * P:(t + 1) * P], xrow[:, t, k * P:(k + 1) * P], ident[:, :])
                    last.then_inc(x_turned, 1)

            def vector(self, dve):
                for t, n in enumerate(VEC_ROWS):
                    dve.wait_ge(vec_turned, t + 1)
                    nc.vector.tensor_copy(vec[:, t, 0:n], bank[t][:, 0:n]).then_inc(vec_ready, 1)
                for k in range(KD):
                    b = 4 + k % 2
                    dve.wait_ge(x_turned, k + 1)
                    nc.vector.tensor_copy(x[:, k, :], bank[b][:, :]).then_inc(x_ready, 1)

        mod_summed, mod_moved, mod_turned = sem("mod_summed"), sem("mod_moved"), sem("mod_turned")
        mod_ready = sem("mod_ready")
        mod_parts = []
        PER_CHUNK = D // 256

        class Modulation:

            PARTS = ((0, 2), (2, 1), (3, 2), (5, 1))

            def __init__(self, layer):
                self.layer, self.buf = layer, layer % 2
                self.parts = {}

            def part(self, n):
                self.parts[n] = ModPart(self, n)
                return self.parts[n]

            def wait(self, eng, n):
                eng.wait_ge(mod_ready, 3 * (self.parts[n].u + 1))

            def shift(self, ffn, k, s):
                j = (3 if ffn else 0) * KD + k
                return modv[:, self.buf, j, s:s + 1]

            def factor(self, n, k, s):
                return affine[:, self.buf, n, k, s:s + 1]

        class ModPart:
            BIAS = {1: "hy_b_out", 3: "fn_b_o"}

            def __init__(self, mod, n):
                self.mod, self.n = mod, n
                self.first, self.count = Modulation.PARTS[n]
                self.banks = bank[0:4] if self.count == 2 else bank[4:6]
                self.rows = gate_rows if n in (1, 3) else mod_rows
                self.u = len(mod_parts)
                mod_parts.append(self)
                self.p0 = PER_CHUNK * sum(p.count for p in mod_parts[:-1])
                w = A["mod_w"][mod.layer]
                self.w = Weights([[cols_of(w, self.first * D + i * 256, 256)] for i in range(PER_CHUNK * self.count)],
                                 lambda i: (mod_summed, self.p0 + i + 1))

            def tensor(self, pe):
                if self.u == 0:
                    pe.wait_ge(silu_ready, 2)
                if self.n == 2:
                    pe.wait_ge(rms_root, self.after.rms.u + 1)
                for i in range(PER_CHUNK * self.count):
                    self.w.wait(pe, i)
                    v = self.w.view(i, KD, 256)
                    for k in range(KD):
                        last = nc.tensor.matmul(self.banks[i // 2][0:2, i % 2 * 256:i % 2 * 256 + 256], silu_c[:, k, :], v[:, k, :],
                                                start=(k == 0), stop=(k == KD - 1))
                    last.then_inc(mod_summed, 1)
                if self.u:
                    pe.wait_ge(mod_ready, 3 * (self.u - 1) + 1)
                for j in range(self.count * KD):
                    if j % 4 == 0:
                        pe.wait_ge(mod_moved, self.p0 // 2 + j // 4 + 1)
                    at = 2 * (self.first * KD + j)
                    last = nc.tensor.transpose(MODP[:, at:at + 2], self.rows[0:2, j * P:(j + 1) * P], ident[0:2, 0:2])
                last.then_inc(mod_turned, 1)

            def vector(self, dve):
                for i in range(PER_CHUNK * self.count // 2):
                    dve.wait_ge(mod_summed, self.p0 + 2 * i + 2)
                    nc.vector.tensor_copy(self.rows[0:2, i * 512:(i + 1) * 512], self.banks[i][0:2, :]).then_inc(mod_moved, 1)
                l, b, base = self.mod.layer, self.mod.buf, 3 * self.u
                j0, nj = self.first * KD, self.count * KD
                m = modv[:, b]
                dve.wait_ge(mod_turned, self.u + 1)
                bias = vcol("mod_b01" if l < 2 else "mod_b23", (l % 2) * MODS * KD + j0, nj).unsqueeze(2).to_broadcast([P, nj, 2])
                nc.vector.tensor_tensor(m[:, j0:j0 + nj, :], MODP[:, 2 * j0:2 * (j0 + nj)].rearrange("p (j s) -> p j s", s=2), bias,
                                        ALU.add).then_inc(mod_ready, 1)
                dve.wait_ge(mod_ready, base + 1)
                g, at, plus = (("mix_pre_g", 1, 1.0), ("mix_post_g", 2, 0.0), ("ffn_pre_g", 4, 1.0), ("ffn_post_g", 5, 0.0))[self.n]
                gv = vcol(g, l * KD, KD).unsqueeze(2).to_broadcast([P, KD, 2])
                nc.vector.scalar_tensor_tensor(affine[:, b, self.n], m[:, at * KD:(at + 1) * KD, :], plus, gv,
                                               ALU.add, ALU.mult).then_inc(mod_ready, 1)
                dve.wait_ge(mod_ready, base + 2)
                bo = vcol(self.BIAS.get(l, "hy_b_out"), 0, KD).unsqueeze(2).to_broadcast([P, KD, 2])
                nc.vector.tensor_tensor(affine[:, b, 4 + self.n // 2], affine[:, b, self.n], bo, ALU.mult).then_inc(mod_ready, 1)

        squared = sem("squared")
        sq_added = sem("sq_added")
        sq_summed = sem("sq_summed")
        rms_step = sem("rms_step")
        rms_root = sem("rms_root")
        n_sq, n_add, n_rms = [0], [0], [0]

        class Rms:

            def __init__(self, kk, n, sq, feats, src=None, ready=None, on_pe=False):
                self.src, self.kk, self.n, self.sq, self.ready, self.feats = src, kk, n, sq, ready, feats
                self.on_pe = on_pe
                self.sq0, self.add0, self.u = n_sq[0], n_add[0], n_rms[0]
                n_sq[0] += kk
                n_add[0] += 0 if on_pe else kk - 1
                n_rms[0] += 1

            def squares(self, act):
                for k in range(self.kk):
                    self.ready(act, k)
                    nc.scalar.activation(self.sq[:, k, 0:self.n], self.src[:, k, 0:self.n], ACT.Square).then_inc(squared, 1)

            def root(self, act):
                act.wait_ge(rms_step, 2 * self.u + 1)
                nc.scalar.activation(rstd[:, 0:self.n], rstd[:, 0:self.n], ACT.Sqrt).then_inc(rms_root, 1)

            def vector(self, dve):
                n = self.n
                acc = self.sq[:, 0, 0:n]
                for k in range(1, 0 if self.on_pe else self.kk):
                    dve.wait_ge(squared, self.sq0 + k + 1)
                    if k > 1:
                        dve.wait_ge(sq_added, self.add0 + k - 1)
                    nc.vector.tensor_tensor(acc, acc, self.sq[:, k, 0:n], ALU.add).then_inc(sq_added, 1)
                dve.wait_ge(sq_summed, self.u + 1)
                nc.vector.tensor_scalar(rstd[:, 0:n], SUMS[:, 0:n], 1.0 / self.feats, EPS,
                                        ALU.mult, ALU.add).then_inc(rms_step, 1)
                dve.wait_ge(rms_root, self.u + 1)
                nc.vector.reciprocal(rstd[:, 0:n], rstd[:, 0:n]).then_inc(rms_step, 1)
                dve.wait_ge(rms_step, 2 * self.u + 2)

            def tensor(self, pe):
                kk = self.kk if self.on_pe else 1
                for k in range(kk):
                    if self.on_pe:
                        pe.wait_ge(squared, self.sq0 + k + 1)
                    else:
                        pe.wait_ge(sq_added, self.add0 + self.kk - 1)
                    last = nc.tensor.matmul(SUMS[:, 0:self.n], ones[:, :], self.sq[:, k, 0:self.n],
                                            start=(k == 0), stop=(k == kk - 1))
                last.then_inc(sq_summed, 1)

        normed = sem("normed")
        h_ready = sem("h_ready")
        h_rounded, h_split_ready = sem("h_rounded"), sem("h_split_ready")
        n_parted = [0]
        n_pre = [0]
        x_updated, x_updated_pool = sem("x_updated"), sem("x_updated_pool")
        POOL_CHUNKS = (3, 6)
        DVE_CHUNKS = tuple(k for k in range(KD) if k not in POOL_CHUNKS)

        def x_updated_wait(eng, posts, k):
            if k in POOL_CHUNKS:
                eng.wait_ge(x_updated_pool, len(POOL_CHUNKS) * posts + POOL_CHUNKS.index(k) + 1)
            else:
                eng.wait_ge(x_updated, len(DVE_CHUNKS) * posts + DVE_CHUNKS.index(k) + 1)
        n_post = [0]

        SQ = area(0, KD, TOK)

        def segments(n):
            return [(0, 0, LAT)] + ([(1, LAT, TOK)] if n == TOK else [])

        h_split = h[:, :, :].rearrange("p k t -> p (k t)").rearrange("p (s k z m) -> p s k z m", k=KD, z=2, m=CH)

        class PreNorm:

            def __init__(self, mod, ffn, n, split=False, parts=False):
                self.mod, self.ffn, self.n, self.split, self.parts = mod, ffn, n, split, parts
                self.u = n_pre[0]
                n_pre[0] += 1
                self.f = n_parted[0]
                n_parted[0] += parts
                posts = self.posts = n_post[0]

                def ready(eng, k):
                    if posts == 0:
                        eng.wait_ge(x_ready, k + 1)
                    else:
                        x_updated_wait(eng, posts - 1, k)
                self.rms = Rms(KD, n, SQ, D, x, ready, on_pe=True)

            def dst(self, k, a, b):
                if not self.split:
                    return h[:, k, a:b]
                return h_split[:, :, k, a // LAT, :].rearrange("p s m -> p m s")

            def src(self, k, a, b):
                if not self.split:
                    return SQ[:, k, a:b]
                return SQ[:, k, a:b].rearrange("p (m s) -> p m s", s=STEP)

            def wait_x(self, eng):
                if self.posts:
                    eng.wait_ge(x_updated, len(DVE_CHUNKS) * self.posts)
                    eng.wait_ge(x_updated_pool, len(POOL_CHUNKS) * self.posts)
                else:
                    eng.wait_ge(x_ready, KD)

            def vector(self, dve):
                self.rms.vector(dve)

                def remainder(k):
                    dve.wait_ge(h_rounded, KD * self.f + k + 1)
                    nc.vector.tensor_tensor(h_lo[:, k, 0:self.n], SQ[:, k, 0:self.n], h_hi[:, k, 0:self.n].bitcast(F32),
                                            ALU.subtract).then_inc(h_split_ready, 1)
                for k in range(KD):
                    nc.vector.tensor_tensor(SQ[:, k, 0:self.n], x[:, k, 0:self.n], rstd[:, 0:self.n],
                                            ALU.mult).then_inc(normed, 1)
                    if self.parts and k >= 3:
                        remainder(k - 3)
                for k in range(KD - 3, KD if self.parts else 0):
                    remainder(k)

            def tensor(self, pe):
                self.rms.tensor(pe)

            def scalar(self, act):
                self.rms.squares(act)
                self.rms.root(act)
                self.mod.wait(act, 2 if self.ffn else 0)
                for k in range(KD):
                    act.wait_ge(normed, KD * self.u + k + 1)
                    for s, a, b in segments(self.n):
                        last = nc.scalar.activation(SQ[:, k, a:b] if self.parts else self.dst(k, a, b), self.src(k, a, b),
                                                    ACT.Identity, bias=self.mod.shift(self.ffn, k, s),
                                                    scale=self.mod.factor(2 if self.ffn else 0, k, s))
                    last.then_inc(h_ready, 1)
                    if self.parts:
                        act.wait_ge(h_ready, KD * self.u + k + 1)
                        nc.scalar.activation(h_hi[:, k, 0:self.n], SQ[:, k, 0:self.n], ACT.Copy).then_inc(h_rounded, 1)

            def wait(self, eng, k=KD - 1):
                if self.parts:
                    eng.wait_ge(h_split_ready, KD * self.f + k + 1)
                else:
                    eng.wait_ge(h_ready, KD * self.u + k + 1)

        Y = area(KD * TOK, KD, TOK)
        y_normed, y_normed_pool = sem("y_normed"), sem("y_normed_pool")

        class PostNorm:

            def __init__(self, mod, ffn, n):
                self.mod, self.ffn, self.n = mod, ffn, n

            def number(self):
                self.u = n_post[0]
                n_post[0] += 1
                self.rms = Rms(KD, self.n, SQ, D)

            def move(self, act, c, src, bias=None):
                n, f = self.n, 3 if self.ffn else 1
                if c == 0:
                    self.mod.wait(act, f)
                if bias is None:
                    nc.scalar.activation(SQ[:, c, 0:n], src[:, 0:n], ACT.Square).then_inc(squared, 1)
                else:
                    nc.scalar.activation(SQ[:, c, 0:n], src[:, 0:n], ACT.Square, bias=vcol(bias, c)).then_inc(squared, 1)
                for s, a, b in segments(n):
                    if bias is None:
                        last = nc.scalar.activation(Y[:, c, a:b], src[:, a:b], ACT.Copy, scale=self.mod.factor(f, c, s))
                    else:
                        last = nc.scalar.activation(Y[:, c, a:b], src[:, a:b], ACT.Identity,
                                                    bias=self.mod.factor(4 + f // 2, c, s), scale=self.mod.factor(f, c, s))
                return last

            def scalar(self, act):
                self.rms.root(act)

            def tensor(self, pe):
                self.rms.tensor(pe)

            def gpsimd(self, pool):
                n = self.n
                pool.wait_ge(rms_step, 2 * self.rms.u + 2)
                for i, k in enumerate(POOL_CHUNKS):
                    nc.gpsimd.tensor_tensor(Y[:, k, 0:n], Y[:, k, 0:n], rstd[:, 0:n], ALU.mult).then_inc(y_normed_pool, 1)
                for i, k in enumerate(POOL_CHUNKS):
                    pool.wait_ge(y_normed_pool, len(POOL_CHUNKS) * self.u + i + 1)
                    nc.gpsimd.tensor_tensor(x[:, k, 0:n], x[:, k, 0:n], Y[:, k, 0:n], ALU.add).then_inc(x_updated_pool, 1)

            def vector(self, dve):
                self.rms.vector(dve)
                n = self.n

                def norm(i):
                    k = DVE_CHUNKS[i]
                    nc.vector.tensor_tensor(Y[:, k, 0:n], Y[:, k, 0:n], rstd[:, 0:n], ALU.mult).then_inc(y_normed, 1)
                norm(0)
                for i, k in enumerate(DVE_CHUNKS):
                    if i + 1 < len(DVE_CHUNKS):
                        norm(i + 1)
                    dve.wait_ge(y_normed, len(DVE_CHUNKS) * self.u + i + 1)
                    nc.vector.tensor_tensor(x[:, k, 0:n], x[:, k, 0:n], Y[:, k, 0:n], ALU.add).then_inc(x_updated, 1)
                dve.wait_ge(y_normed_pool, len(POOL_CHUNKS) * (self.u + 1))

            def wait(self, eng, k=KD - 1):
                x_updated_wait(eng, self.u, k)

        class Linear:

            def __init__(self, name, w, kk, rhs, n, ready, move, banks=(0, 1, 2, 3)):
                self.mm, self.moved = sem(name + "_summed"), sem(name + "_moved")
                self.kk, self.rhs, self.n, self.ready, self.move = kk, rhs, n, ready, move
                self.banks = [bank[i] for i in banks]
                self.parts = (kk + 10) // 11
                self.kp = kk // self.parts
                self.chunks = w.shape[1] // P
                rows = self.kp * P
                self.w = Weights([[cols_of(w[r * rows:(r + 1) * rows, :], i * 256, 256)]
                                  for i in range(self.chunks // 2) for r in range(self.parts)],
                                 lambda i: (self.mm, self.nth(i // self.parts, i % self.parts, 1)))

            def nth(self, i, r, q):
                return 2 * (self.parts * i + r) + q + 1

            def tensor(self, pe):
                for i in range(self.chunks // 2):
                    for r in range(self.parts):
                        self.w.wait(pe, self.parts * i + r)
                        v = self.w.view(self.parts * i + r, self.kp, 256)
                        for q in range(2):
                            c = 2 * i + q
                            if c >= 4 and r == 0:
                                pe.wait_ge(self.moved, c - 3)
                            for kl in range(self.kp):
                                k = r * self.kp + kl
                                if c == 0:
                                    self.ready(pe, k)
                                last = nc.tensor.matmul(self.banks[c % 4][:, 0:self.n], v[:, kl, q * P:(q + 1) * P], self.rhs(k),
                                                        start=(k == 0), stop=(k == self.kk - 1))
                            last.then_inc(self.mm, 1)

            def scalar(self, act):
                for c in range(self.chunks):
                    act.wait_ge(self.mm, self.nth(c // 2, self.parts - 1, c % 2))
                    self.move(act, c, self.banks[c % 4]).then_inc(self.moved, 1)

            def wait(self, eng, c=None):
                eng.wait_ge(self.moved, (self.chunks if c is None else c + 1))

        class Gated:

            def __init__(self, name, w, cols, rhs, n, ready, done):
                self.mm, self.done = sem(name + "_summed"), done
                self.rhs, self.n, self.ready = rhs, n, ready
                self.chunks = cols // P
                self.w = Weights([[cols_of(w, t * cols + i * 256, 256)] for i in range(self.chunks // 2) for t in range(2)],
                                 lambda i: (self.mm, 2 * (i + 1)))

            def bank(self, c, t):
                return bank[2 * t + c % 2]

            def summed(self, eng, c, t):
                eng.wait_ge(self.mm, 4 * (c // 2) + 2 * t + c % 2 + 1)

            def tensor(self, pe):
                for c2 in range(self.chunks // 2):
                    for t in range(2):
                        self.w.wait(pe, 2 * c2 + t)
                        v = self.w.view(2 * c2 + t, KD, 256)
                        for q in range(2):
                            c = 2 * c2 + q
                            if c >= 2:
                                pe.wait_ge(self.done, c - 1)
                            for k in range(KD):
                                if c == 0 and t == 0:
                                    self.ready(pe, k)
                                last = nc.tensor.matmul(self.bank(c, t)[:, 0:self.n], v[:, k, q * P:(q + 1) * P], self.rhs(k),
                                                        start=(k == 0), stop=(k == KD - 1))
                            last.then_inc(self.mm, 1)

        w_rounded, w_split_ready = sem("w_rounded"), sem("w_split_ready")
        n_split = [0]

        class Split:

            def __init__(self, loads, shapes, summed, hi=w_hi, lo=w_lo):
                self.shapes, self.summed, self.hi, self.lo = shapes, summed, hi, lo
                self.s0 = n_split[0]
                n_split[0] += len(loads)
                self.w = Weights(loads, lambda i: (w_split_ready, 2 * (self.s0 + i + 1)))

            def halves(self, i):
                kk, width = self.shapes[i]
                return [(0, kk // 2 * width), (kk // 2 * width, kk * width)]

            def round(self, act, i):
                self.w.wait(act, i)
                if i >= SPLIT:
                    act.wait_ge(*self.summed(i - SPLIT))
                for a, b in self.halves(i):
                    nc.scalar.activation(self.hi[:, i % SPLIT, a:b], self.w.slot(i)[:, a:b], ACT.Copy).then_inc(w_rounded, 1)

            def remain(self, dve, i):
                for j, (a, b) in enumerate(self.halves(i)):
                    dve.wait_ge(w_rounded, 2 * (self.s0 + i) + j + 1)
                    nc.vector.tensor_tensor(self.lo[:, i % SPLIT, a:b], self.w.slot(i)[:, a:b], self.hi[:, i % SPLIT, a:b].bitcast(F32),
                                            ALU.subtract).then_inc(w_split_ready, 1)

            def ahead(self, step, eng, i=None):
                for j in (range(min(SPLIT, len(self.shapes))) if i is None else (i + SPLIT,)):
                    if j < len(self.shapes):
                        step(eng, j)

            def parts(self, i):
                kk, width = self.shapes[i]
                return [v[:, i % SPLIT, 0:kk * width].rearrange("p (k n) -> p k n", n=width) for v in (self.hi, self.lo)]

            def wait(self, pe, i, k):
                if k in (0, self.shapes[i][0] // 2):
                    pe.wait_ge(w_split_ready, 2 * (self.s0 + i) + 1 + (k > 0))

        def product(o, w, v, first, last):
            nc.tensor.matmul(o, w[0], v[0], start=first, stop=False)
            nc.tensor.matmul(o, w[0], v[1], start=False, stop=False)
            return nc.tensor.matmul(o, w[1], v[0], start=False, stop=last)

        class Ffn:

            def __init__(self, layer, n, pre, post):
                self.n, self.pre, self.post = n, pre, post
                s = lambda name: sem(f"ffn{layer}_{name}")
                self.summed, self.silu, self.product, self.g_rounded, self.g = s("summed"), s("silu"), s("product"), s("g_rounded"), s("g")
                self.partial, self.total = s("partial"), s("total")
                self.silus = area(KD * TOK, 2, TOK)
                self.plan = []
                loads = []
                up, down = A["ffn_w13"][layer], A["ffn_w2"][layer]
                f0 = 0
                for part, nf in enumerate(UP_CHUNKS):
                    for c in range(0, nf, 2):
                        for t in range(2):
                            self.plan.append((t, part, KD, c))
                            loads.append([cols_of(up, t * FFN + (f0 + c) * P, 256)])
                    for c in range(0, KD, 2):
                        self.plan.append((2, part, nf, c))
                        loads.append([cols_of(down[f0 * P:(f0 + nf) * P, :], c * P, 256)])
                    f0 += nf
                self.w = Split(loads, [(p[2], 256) for p in self.plan], lambda i: (self.summed, 2 * (i + 1)))

            def out(self, i, q):
                kind, part, kk, c = self.plan[i]
                return bank[2 * kind + q] if kind < 2 else bank[(4, 5, 0, 1)[(c + q) % 4]]

            def f_of(self, i):
                return sum(UP_CHUNKS[:self.plan[i][1]]) + self.plan[i][3]

            def tensor(self, pe):
                n = self.n
                for i, (kind, part, kk, c) in enumerate(self.plan):
                    hi, lo = self.w.parts(i)
                    for q in range(2):
                        if kind < 2:
                            f = self.f_of(i) + q
                            if part and c == 0:
                                pe.wait_ge(self.partial, KD)
                            if c >= 2:
                                pe.wait_ge(self.product, f - 1)
                        elif c + q >= 4:
                            pe.wait_ge(*self.moved(part, c + q - 4))
                        o = self.out(i, q)[:, 0:n]
                        for k in range(kk):
                            if q == 0:
                                self.w.wait(pe, i, k)
                            if i == 0 and q == 0:
                                self.pre.wait(pe, k)
                            if kind == 2 and c + q == 0:
                                pe.wait_ge(self.g, sum(UP_CHUNKS[:part]) + k + 1)
                            v_hi, v_lo = (h_hi, h_lo) if kind < 2 else (g_hi, g_lo)
                            cols = slice(q * P, (q + 1) * P)
                            last = product(o, (hi[:, k, cols], lo[:, k, cols]), (v_hi[:, k, 0:n], v_lo[:, k, 0:n]), k == 0, k == kk - 1)
                        last.then_inc(self.summed, 1)

            def moved(self, part, c):
                return (self.total, c + 1) if part else (self.partial, c + 1)

            def scalar(self, act):
                n = self.n
                self.w.ahead(self.w.round, act)
                for i, (kind, part, kk, c) in enumerate(self.plan):
                    f = self.f_of(i)
                    for q in range(2):
                        if kind == 0:
                            act.wait_ge(self.summed, 2 * i + q + 1)
                            if f + q >= 2:
                                act.wait_ge(self.g, f + q - 1)
                            nc.scalar.activation(self.silus[:, q, 0:n], self.out(i, q)[:, 0:n], ACT.Silu).then_inc(self.silu, 1)
                        elif kind == 1:
                            act.wait_ge(self.product, f + q + 1)
                            if part and c == 0 and q == 0:
                                act.wait_ge(self.partial, KD)
                            nc.scalar.activation(g_hi[:, c + q, 0:n], self.silus[:, q, 0:n], ACT.Copy).then_inc(self.g_rounded, 1)
                        elif part == 0:
                            act.wait_ge(self.summed, 2 * i + q + 1)
                            nc.scalar.activation(SQ[:, c + q, 0:n], self.out(i, q)[:, 0:n], ACT.Copy).then_inc(self.partial, 1)
                        else:
                            act.wait_ge(self.total, c + q + 1)
                            self.post.move(act, c + q, h[:, c + q, :])
                    self.w.ahead(self.w.round, act, i)

            def vector(self, dve):
                n = self.n
                self.w.ahead(self.w.remain, dve)
                for i, (kind, part, kk, c) in enumerate(self.plan):
                    f = self.f_of(i)
                    for q in range(2):
                        if kind == 1:
                            dve.wait_ge(self.summed, 2 * i + q + 1)
                            dve.wait_ge(self.silu, f + q + 1)
                            nc.vector.tensor_tensor(self.silus[:, q, 0:n], self.silus[:, q, 0:n], self.out(i, q)[:, 0:n],
                                                    ALU.mult).then_inc(self.product, 1)
                        elif kind == 2 and part == 1:
                            dve.wait_ge(self.summed, 2 * i + q + 1)
                            dve.wait_ge(self.partial, KD)
                            nc.vector.tensor_tensor(h[:, c + q, 0:n], self.out(i, q)[:, 0:n], SQ[:, c + q, 0:n],
                                                    ALU.add).then_inc(self.total, 1)
                    for q in range(2 if kind == 1 else 0):
                        dve.wait_ge(self.g_rounded, f + q + 1)
                        nc.vector.tensor_tensor(g_lo[:, c + q, 0:n], self.silus[:, q, 0:n], g_hi[:, c + q, 0:n].bitcast(F32),
                                                ALU.subtract).then_inc(self.g, 1)
                    self.w.ahead(self.w.remain, dve, i)

        class Mla:

            def __init__(self, pre, post, n_in, n):
                self.pre = pre
                at = KD * TOK
                self.z = area(at, 8, TOK)
                at = 2 * KD * TOK
                self.v = area(at, 4, D)
                self.kn = area(at + 4096, HEADS, TOK)
                self.qn = area(at + 8192, HEADS, TOK)
                self.qr = area(at + 12288, HEADS, TOK)
                self.qrot = area(at + 16384, HEADS, LAT)
                self.kr = area(at + 18432, TOK)
                self.krot = area(at + 18944, LAT)
                self.tab = area(at + 19200, 2, LAT)
                self.turn = area(at + 19712, ROPE)
                self.tmp = area(at + 19776, 2, 2, LAT)
                self.e = area(at + 20800, 2, TOK)
                self.pt = area(at + 21824, 2, TOK)
                self.mx = small[:, 0:2]
                self.sm = small[:, 2:4]
                self.loaded = sem("mla_tables_loaded")
                w = A["mla_w_in"][0]
                self.order = (6, 7, 8, 0, 1, 2, 3, 4, 5)
                self.panel = (0, 0, 1, 2, 2, 3, 3, 4, 4)
                self.z_summed, self.z_moved = sem("mla_z_summed"), sem("mla_z_moved")
                self.win = Split([[cols_of(w, c0, n)] for c0, n in ((768, 256), (1024, ROPE), (0, 256), (256, 256), (512, 256))],
                                 [(KD, 256), (KD, ROPE)] + [(KD, 256)] * 3, lambda i: (self.z_summed, (2, 3, 5, 7, 9)[i]))
                self.zn, self.z_ready = sem("mla_z_normed"), sem("mla_z_ready")
                self.z_rounded, self.z_split_ready = sem("mla_z_rounded"), sem("mla_z_split_ready")
                self.rms_kv = Rms(2, TOK, SQ[:, 6:8, :], KVR, self.z[:, 6:8, :], lambda eng, k: eng.wait_ge(self.z_moved, k + 1))
                self.rms_q = Rms(6, TOK, SQ, QR, self.z, lambda eng, k: eng.wait_ge(self.z_moved, k + 4))
                self.kv_summed, self.kv_moved = sem("mla_kv_summed"), sem("mla_kv_moved")
                self.wukv = Weights([[cols_of(A["mla_w_ukv"][0], i * 1024, 1024)] for i in range(2)],
                                    lambda i: (self.kv_summed, 8 * (i + 1)))
                self.q_summed, self.q_moved = sem("mla_q_summed"), sem("mla_q_moved")
                hi, lo = (place(n, KD * TOK + a, [SPLIT, 6 * 192], F32R) for n, a in (("mla_q_hi", 0), ("mla_q_lo", at + 19776)))
                self.wuq = Split([[cols_of(A["mla_w_uq"][0], i * 192, 192)] for i in range(HEADS)], [(6, 192)] * HEADS,
                                 lambda i: (self.q_summed, 2 * (i + 1)), hi, lo)
                self.turned, self.rot = sem("mla_turned"), sem("mla_rotated")
                self.rot_step = sem("mla_rot_step")
                self.scored, self.maxed, self.negated = sem("mla_scored"), sem("mla_maxed"), sem("mla_negated")
                self.exped, self.recip, self.probs = sem("mla_exped"), sem("mla_recip"), sem("mla_probs")
                self.p_turned, self.p_moved = sem("mla_p_turned"), sem("mla_p_moved")
                self.o_summed, self.o_moved = sem("mla_o_summed"), sem("mla_o_moved")
                self.o_split, self.out_summed, self.out_moved = sem("mla_o_split"), sem("mla_out_summed"), sem("mla_out_moved")
                self.wo = []
                for j, (a_hi, a_lo) in enumerate(((0, KD * TOK), (at + 4096, at + 8192))):
                    hi, lo = (place(f"mla_o_{n}{j}", KD * TOK + a, [SPLIT, KD * 256], F32R) for n, a in (("hi", a_hi), ("lo", a_lo)))
                    self.wo.append(Split([[cols_of(A["mla_w_o"][0], (2 * j + i) * 256, 256)] for i in range(2)], [(KD, 256)] * 2, None, hi, lo))
                self.post = post
                self.units = [(hd, qb, 0 if qb < 2 else LAT, 4 if qb < 2 else 2) for hd in range(HEADS) for qb in range(4)]

            def gpsimd(self, pool):
                pool.wait_ge(x_ready, KD)
                pool.dma_start(self.tab[0:ROPE], A["k_rope"]).then_inc(self.loaded, 16)
                pool.dma_start(self.turn[0:ROPE], A["k_turn"]).then_inc(self.loaded, 16)

            def tensor(self, pe):
                for n, (c, i) in enumerate(zip(self.order, self.panel)):
                    m = ROPE if c == 8 else P
                    hi, lo = self.win.parts(i)
                    q = n > 0 and self.panel[n - 1] == i
                    cols = slice(q * P, q * P + m)
                    if n >= 4:
                        pe.wait_ge(self.z_moved, n - 3)
                    for k in range(KD):
                        if n == 0:
                            self.pre.wait(pe, k)
                        if not q:
                            self.win.wait(pe, i, k)
                        last = product(bank[n % 4][0:m, :], (hi[:, k, cols], lo[:, k, cols]), (h_hi[:, k, :], h_lo[:, k, :]), k == 0, k == KD - 1)
                    last.then_inc(self.z_summed, 1)
                    if n == 4:
                        self.rms_kv.tensor(pe)
                pe.wait_ge(self.z_ready, 2)
                for c in range(16):
                    half, r = divmod(c, 8)
                    if r == 0:
                        self.wukv.wait(pe, half)
                        wv = self.wukv.view(half, 2, 1024)
                    if c < 4:
                        pe.wait_ge(self.z_moved, 9)
                    else:
                        pe.wait_ge(self.kv_moved, c - 3)
                    for k in range(2):
                        if r < 4:
                            last = nc.tensor.matmul(bank[c % 4][:, :], wv[:, k, r * 256:r * 256 + P], self.z[:, 6 + k, :],
                                                    start=(k == 0), stop=(k == 1))
                        else:
                            t = r - 4
                            vals = wv[:, k, :].rearrange("p (h n) -> p h n", n=256)[:, :, P:256]
                            last = nc.tensor.matmul(bank[c % 4][:, :].rearrange("p (h n) -> p h n", n=P),
                                                    self.z[:, 6 + k, t * P:(t + 1) * P], vals, start=(k == 0), stop=(k == 1))
                    last.then_inc(self.kv_summed, 1)
                    if c == 5:
                        self.rms_q.tensor(pe)
                for c in range(16):
                    hd, part = divmod(c, 2)
                    hi, lo = self.wuq.parts(hd)
                    c0 = part * P
                    m = ROPE if part else P
                    cols = slice(c0, c0 + m)
                    if c < 4:
                        pe.wait_ge(self.kv_moved, 13 + c)
                    else:
                        pe.wait_ge(self.q_moved, c - 3)
                    for k in range(6):
                        if c == 0:
                            pe.wait_ge(self.z_split_ready, k + 1)
                        if part == 0:
                            self.wuq.wait(pe, hd, k)
                        last = product(bank[c % 4][0:m, :], (hi[:, k, cols], lo[:, k, cols]), (h_hi[:, k, :], h_lo[:, k, :]), k == 0, k == 5)
                    last.then_inc(self.q_summed, 1)
                pe.wait_ge(self.q_moved, 16)
                pe.wait_ge(self.loaded, 32)
                for i in range(9):
                    if i >= 2:
                        pe.wait_ge(self.rot, i - 1)
                    src = self.kr[0:ROPE, 0:LAT] if i == 0 else self.qr[0:ROPE, i - 1, 0:LAT]
                    nc.tensor.matmul(bank[4 + i % 2][0:ROPE, 0:LAT], self.turn[0:ROPE, :], src,
                                     start=True, stop=True).then_inc(self.turned, 1)

                def scores(u):
                    hd, qb, k0, nk = self.units[u]
                    if u < 2:
                        pe.wait_ge(self.rot, 9)
                    else:
                        pe.wait_ge(self.exped, u - 1)
                    b = bank[u % 2]
                    q = slice(qb * P, (qb + 1) * P)
                    if qb < 2:
                        nc.tensor.matmul(b[:, :], self.qn[:, hd, q], self.kn[:, hd, :], start=True, stop=False)
                        nc.tensor.matmul(b[:, 0:LAT], self.qrot[0:ROPE, hd, q], self.krot[0:ROPE, :], start=False, stop=False)
                        nc.tensor.matmul(b[:, LAT:TOK], self.qr[0:ROPE, hd, q], self.kr[0:ROPE, LAT:TOK],
                                         start=False, stop=True).then_inc(self.scored, 1)
                    else:
                        nc.tensor.matmul(b[:, 0:LAT], self.qn[:, hd, q], self.kn[:, hd, LAT:TOK], start=True, stop=False)
                        nc.tensor.matmul(b[:, 0:LAT], self.qr[0:ROPE, hd, q], self.kr[0:ROPE, LAT:TOK],
                                         start=False, stop=True).then_inc(self.scored, 1)

                def weigh(u):
                    hd, qb, k0, nk = self.units[u]
                    pe.wait_ge(self.probs, u + 1)
                    if u >= 2:
                        pe.wait_ge(self.p_moved, u - 1)
                    for j in range(nk):
                        last = nc.tensor.transpose(bank[2 + u % 2][:, j * P:(j + 1) * P], self.e[:, u % 2, j * P:(j + 1) * P], ident[:, :])
                    last.then_inc(self.p_turned, 1)

                def values(u):
                    hd, qb, k0, nk = self.units[u]
                    pe.wait_ge(self.p_moved, u + 1)
                    if u >= 2:
                        pe.wait_ge(self.o_split, u - 1)
                    for j in range(nk):
                        last = nc.tensor.matmul(bank[4 + u % 2][:, 0:P], self.v[:, k0 // P + j, hd * P:(hd + 1) * P],
                                                self.pt[:, u % 2, j * P:(j + 1) * P], start=(j == 0), stop=(j == nk - 1))
                    last.then_inc(self.o_summed, 1)
                n = len(self.units)
                scores(0)
                scores(1)
                for u in range(n):
                    weigh(u)
                    if u + 2 < n:
                        scores(u + 2)
                    if u >= 1:
                        values(u - 1)
                values(n - 1)
                for c in range(KD):
                    i, q = divmod(c, 2)
                    wo = self.wo[i // 2]
                    hi, lo = wo.parts(i % 2)
                    cols = slice(q * P, (q + 1) * P)
                    if c == 0:
                        pe.wait_ge(self.exped, n)
                        pe.wait_ge(self.p_moved, n)
                    if c >= 4:
                        pe.wait_ge(self.out_moved, c - 3)
                    for k in range(KD):
                        if c == 0:
                            pe.wait_ge(self.o_split, min(4 * k + 4, n))
                        if q == 0:
                            wo.wait(pe, i % 2, k)
                        last = product(bank[c % 4][:, :], (hi[:, k, cols], lo[:, k, cols]), (h_hi[:, k, :], h_lo[:, k, :]), k == 0, k == KD - 1)
                    last.then_inc(self.out_summed, 1)

            def scalar(self, act):
                def z(n):
                    c = self.order[n]
                    act.wait_ge(self.z_summed, n + 1)
                    dst, m = (self.kr[0:ROPE, :], ROPE) if c == 8 else (self.z[:, c, :], P)
                    nc.scalar.activation(dst, bank[n % 4][0:m, :], ACT.Copy).then_inc(self.z_moved, 1)

                def kv(c):
                    half, r = divmod(c, 8)
                    act.wait_ge(self.kv_summed, c + 1)
                    dst = self.kn[:, 4 * half + r, :] if r < 4 else self.v[:, r - 4, half * 512:(half + 1) * 512]
                    nc.scalar.activation(dst, bank[c % 4][:, :], ACT.Copy).then_inc(self.kv_moved, 1)

                ahead = self.win.ahead
                ahead(self.win.round, act)
                z(0)
                z(1)
                ahead(self.win.round, act, 0)
                z(2)
                ahead(self.win.round, act, 1)
                self.rms_kv.squares(act)
                z(3)
                z(4)
                ahead(self.win.round, act, 2)
                self.rms_kv.root(act)
                z(5)
                for k in range(2):
                    act.wait_ge(self.zn, k + 1)
                    nc.scalar.activation(self.z[:, 6 + k, :], self.z[:, 6 + k, :], ACT.Copy, scale=vcol("mla_kv_norm_g", k)).then_inc(self.z_ready, 1)
                for n in range(6, 9):
                    z(n)
                self.rms_q.squares(act)
                for c in range(6):
                    kv(c)
                self.rms_q.root(act)
                for k in range(6):
                    kv(6 + k)
                    act.wait_ge(self.zn, 2 + k + 1)
                    nc.scalar.activation(self.z[:, k, :], self.z[:, k, :], ACT.Copy, scale=vcol("mla_q_norm_g", k)).then_inc(self.z_ready, 1)
                    act.wait_ge(self.z_ready, 2 + k + 1)
                    nc.scalar.activation(h_hi[:, k, :], self.z[:, k, :], ACT.Copy).then_inc(self.z_rounded, 1)
                kv(12)
                kv(13)
                self.wuq.round(act, 0)
                kv(14)
                kv(15)
                self.wuq.round(act, 1)
                for c in range(16):
                    act.wait_ge(self.q_summed, c + 1)
                    hd, part = divmod(c, 2)
                    dst, m = (self.qr[0:ROPE, hd, :], ROPE) if part else (self.qn[:, hd, :], P)
                    nc.scalar.activation(dst, bank[c % 4][0:m, :], ACT.Copy).then_inc(self.q_moved, 1)
                    if part:
                        self.wuq.ahead(self.wuq.round, act, hd)
                self.wo[0].ahead(self.wo[0].round, act)
                scale = float((NOPE + ROPE) ** -0.5)

                def out(u):
                    hd, qb, k0, nk = self.units[u]
                    act.wait_ge(self.o_summed, u + 1)
                    nc.scalar.activation(h_hi[:, hd, qb * P:(qb + 1) * P], bank[4 + u % 2][:, 0:P], ACT.Copy).then_inc(self.o_moved, 1)
                for u, (hd, qb, k0, nk) in enumerate(self.units):
                    act.wait_ge(self.negated, u + 1)
                    if u >= 2:
                        act.wait_ge(self.p_turned, u - 1)
                    nc.scalar.activation(self.e[:, u % 2, 0:nk * P], bank[u % 2][:, 0:nk * P], ACT.Exp, bias=self.mx[:, u % 2:u % 2 + 1],
                                         scale=scale, accum_out=self.sm[:, u % 2:u % 2 + 1]).then_inc(self.exped, 1)
                    if u >= 2:
                        out(u - 2)
                out(len(self.units) - 2)
                out(len(self.units) - 1)
                self.wo[1].ahead(self.wo[1].round, act)
                for c in range(KD):
                    act.wait_ge(self.out_summed, max(c + 1, 2))
                    self.post.move(act, c, bank[c % 4]).then_inc(self.out_moved, 1)

            def vector(self, dve):
                ahead = self.win.ahead
                ahead(self.win.remain, dve)
                ahead(self.win.remain, dve, 0)
                ahead(self.win.remain, dve, 1)
                self.rms_kv.vector(dve)
                for k in range(2):
                    nc.vector.tensor_tensor(self.z[:, 6 + k, :], self.z[:, 6 + k, :], rstd[:, :], ALU.mult).then_inc(self.zn, 1)
                ahead(self.win.remain, dve, 2)
                dve.wait_ge(self.zn, 2)
                self.rms_q.vector(dve)
                for k in range(6):
                    nc.vector.tensor_tensor(self.z[:, k, :], self.z[:, k, :], rstd[:, :], ALU.mult).then_inc(self.zn, 1)
                for k in range(6):
                    dve.wait_ge(self.z_rounded, k + 1)
                    nc.vector.tensor_tensor(h_lo[:, k, :], self.z[:, k, :], h_hi[:, k, :].bitcast(F32), ALU.subtract).then_inc(self.z_split_ready, 1)
                self.wuq.ahead(self.wuq.remain, dve)
                for i in range(HEADS):
                    self.wuq.ahead(self.wuq.remain, dve, i)
                cos, sin = self.tab[0:ROPE, 0, :], self.tab[0:ROPE, 1, :]
                dve.wait_ge(self.loaded, 32)
                for i in range(9):
                    src = self.kr[0:ROPE, 0:LAT] if i == 0 else self.qr[0:ROPE, i - 1, 0:LAT]
                    dst = self.krot[0:ROPE, :] if i == 0 else self.qrot[0:ROPE, i - 1, :]
                    dve.wait_ge(self.turned, i + 1)
                    if i >= 2:
                        dve.wait_ge(self.rot, i - 1)
                    nc.vector.tensor_tensor(self.tmp[0:ROPE, i % 2, 0, :], bank[4 + i % 2][0:ROPE, 0:LAT], sin, ALU.mult).then_inc(self.rot_step, 1)
                    nc.vector.tensor_tensor(self.tmp[0:ROPE, i % 2, 1, :], src, cos, ALU.mult).then_inc(self.rot_step, 1)
                    dve.wait_ge(self.rot_step, 2 * i + 2)
                    nc.vector.tensor_tensor(dst, self.tmp[0:ROPE, i % 2, 0, :], self.tmp[0:ROPE, i % 2, 1, :], ALU.add).then_inc(self.rot, 1)
                scale = float((NOPE + ROPE) ** -0.5)
                n = len(self.units)

                def peak(u):
                    hd, qb, k0, nk = self.units[u]
                    dve.wait_ge(self.scored, u + 1)
                    nc.vector.reduce_max(self.mx[:, u % 2:u % 2 + 1], bank[u % 2][:, 0:nk * P], axis=AX.X).then_inc(self.maxed, 1)
                    dve.wait_ge(self.maxed, u + 1)
                    nc.vector.tensor_scalar(self.mx[:, u % 2:u % 2 + 1], self.mx[:, u % 2:u % 2 + 1], -scale, None, ALU.mult).then_inc(self.negated, 1)

                def remainder(u):
                    hd, qb, k0, nk = self.units[u]
                    q = slice(qb * P, (qb + 1) * P)
                    dve.wait_ge(self.o_moved, u + 1)
                    nc.vector.tensor_tensor(h_lo[:, hd, q], bank[4 + u % 2][:, 0:P], h_hi[:, hd, q].bitcast(F32),
                                            ALU.subtract).then_inc(self.o_split, 1)
                peak(0)
                peak(1)
                self.wo[0].ahead(self.wo[0].remain, dve)
                for u, (hd, qb, k0, nk) in enumerate(self.units):
                    dve.wait_ge(self.exped, u + 1)
                    nc.vector.reciprocal(self.sm[:, u % 2:u % 2 + 1], self.sm[:, u % 2:u % 2 + 1]).then_inc(self.recip, 1)
                    dve.wait_ge(self.recip, u + 1)
                    nc.vector.tensor_scalar(self.e[:, u % 2, 0:nk * P], self.e[:, u % 2, 0:nk * P], self.sm[:, u % 2:u % 2 + 1],
                                            None, ALU.mult).then_inc(self.probs, 1)
                    if u + 2 < n:
                        peak(u + 2)
                    dve.wait_ge(self.p_turned, u + 1)
                    if u >= 2:
                        dve.wait_ge(self.o_summed, u - 1)
                    nc.vector.tensor_copy(self.pt[:, u % 2, 0:nk * P], bank[2 + u % 2][:, 0:nk * P]).then_inc(self.p_moved, 1)
                    if u >= 2:
                        remainder(u - 2)
                remainder(n - 2)
                remainder(n - 1)
                self.wo[1].ahead(self.wo[1].remain, dve)

        class Hyena:

            SEQS = 2
            SIN_STEPS = 6
            SINES = (8, 12, 16)

            def __init__(self, pre, post, n_in, n):
                self.pre = pre
                self.pad = area(0, 2, 2, LAT + 2)
                self.w3 = area(2048, 2 * D)
                self.absh = area(0, 4, D)
                self.tmp = area(0, 4, 512)
                self.zt = area(4096, LAT)
                self.w1 = area(4352, WIDTH)
                self.w2 = area(4416, 2, WIDTH)
                self.fcol = area(4544, 8)
                self.a = area(4608, LAT)
                self.k = area(4864, LAT)
                self.sd = area(4096, 2, 2, D)
                self.u = area(8192, 24, TOK)
                self.v = area(8192 + 16 * TOK, 8, TOK)
                self.vt = area(8192 + 8 * TOK, 4, D)
                self.kf = area(20480, 4, D)
                self.dec = area(5120, 2, D)
                self.hfb = area(24576, 2, 2, D)
                self.prod = area(24576, 4, D)
                self.cs = area(28672, 2, 2, LAT)
                self.ics = area(29696, 2, 2, LAT)
                self.loaded, self.loaded2 = sem("hy_small_loaded"), sem("hy_tables_loaded")
                self.padded = sem("hy_pads_zeroed")
                self.u_summed, self.u_moved, self.conv_step = sem("hy_u_summed"), sem("hy_u_moved"), sem("hy_conv_step")
                self.conv = sem("hy_convolved")
                hi, lo = (place(n, KD * TOK + 20480 + i * SPLIT * KD * 256, [SPLIT, KD * 256], F32R) for i, n in enumerate(("hy_w_hi", "hy_w_lo")))
                self.win = Split([[cols_of(A["hy_w_in"][0], i * 256, 256)] for i in range(12)], [(KD, 256)] * 12,
                                 lambda i: (self.u_summed, 2 * (i + 1)), hi, lo)
                self.v_gated, self.v_turned, self.v_moved = sem("hy_v_gated"), sem("hy_v_turned"), sem("hy_v_moved")
                self.f_summed, self.f_step, self.f_sin = sem("hy_f_summed"), sem("hy_f_step"), sem("hy_f_sin")
                self.t_summed, self.t_decayed, self.t_masked = sem("hy_taps_summed"), sem("hy_taps_decayed"), sem("hy_taps_masked")
                self.t_abs, self.t_norm, self.t_inv, self.t_mixed = sem("hy_taps_abs"), sem("hy_taps_normed"), sem("hy_taps_inverse"), sem("hy_taps_mixed")
                self.t_folded = sem("hy_taps_folded")
                self.k_summed, self.k_moved = sem("hy_k_summed"), sem("hy_k_moved")
                self.s_summed, self.s_prod, self.s_step = sem("hy_spectrum_summed"), sem("hy_spectrum_product"), sem("hy_product_step")
                self.y_summed, self.y_scaled, self.y_skip, self.y_gated = sem("hy_y_summed"), sem("hy_y_scaled"), sem("hy_y_skip"), sem("hy_y_gated")
                self.ytmp = area(2048, 2, LAT)
                self.proj = Linear("hy_out", A["hy_w_out"][0], KD, lambda k: h[:, k, :], TOK,
                                   lambda pe, k: pe.wait_ge(self.y_gated, KD + k + 1),
                                   lambda act, c, b: post.move(act, c, b, "hy_b_out"))

            def gpsimd(self, pool):
                self.pre.wait(pool)
                one = lambda v: v.rearrange("(p o) -> p o", o=1)
                with nc.allow_non_contiguous_dma(reason="64 words"):
                    for j, v in enumerate([A["hy_f_b1"][0], A["hy_f_b2"][0, 0], A["hy_f_b2"][0, 1], A["hy_f_freq"][0]]):
                        pool.dma_start(self.fcol[0:WIDTH, j:j + 1], one(v)).then_inc(self.loaded, 16)
                pool.dma_start(self.zt[0:EMB, :], A["k_hyena_z"]).then_inc(self.loaded, 16)
                pool.dma_start(self.w1[0:EMB, :], A["hy_f_w1"][0]).then_inc(self.loaded, 16)
                pool.dma_start(self.w2[0:WIDTH], A["hy_f_w2"][0].rearrange("i p n -> p i n")).then_inc(self.loaded, 16)
                pool.dma_start(self.w3[0:WIDTH], A["hy_f_w3"][0]).then_inc(self.loaded, 16)
                pool.dma_start(self.cs, A["k_dft_odd"]).then_inc(self.loaded2, 16)
                pool.dma_start(self.ics, A["k_idft_odd"]).then_inc(self.loaded2, 16)
                for b in range(2):
                    nc.gpsimd.memset(self.pad[:, b, :, 0:1], 0.0).then_inc(self.padded, 1)
                    nc.gpsimd.memset(self.pad[:, b, :, LAT + 1:LAT + 2], 0.0).then_inc(self.padded, 1)
                pool.dma_start(self.dec, A["k_hyena_decay"]).then_inc(self.loaded2, 16)
                pool.wait_ge(self.t_abs, 1)
                nc.gpsimd.tensor_tensor(self.absh[:, 0:2, :], self.absh[:, 0:2, :], self.absh[:, 2:4, :], ALU.add).then_inc(self.t_folded, 1)
                pool.wait_ge(self.t_folded, 1)
                nc.gpsimd.tensor_tensor(self.absh[:, 0, :], self.absh[:, 0, :], self.absh[:, 1, :], ALU.add).then_inc(self.t_folded, 1)

            def tensor(self, pe):
                def sine(r):
                    if r == 0:
                        pe.wait_ge(self.loaded, 16 * 8)
                    else:
                        pe.wait_ge(self.f_sin, r)
                    lhs = self.w1[0:EMB, :] if r == 0 else self.w2[0:WIDTH, r - 1, :]
                    rhs = self.zt[0:EMB, :] if r == 0 else self.a[0:WIDTH, :]
                    nc.tensor.matmul(bank[5][0:WIDTH, 0:LAT], lhs, rhs, start=True, stop=True).then_inc(self.f_summed, 1)
                for c in range(24):
                    if c in self.SINES:
                        sine(self.SINES.index(c))
                    i, q = divmod(c, 2)
                    hi, lo = self.win.parts(i)
                    cols = slice(q * P, (q + 1) * P)
                    if c >= 4:
                        pe.wait_ge(self.u_moved, c - 3)
                    for k in range(KD):
                        if c == 0:
                            self.pre.wait(pe, k)
                        if q == 0:
                            self.win.wait(pe, i, k)
                        last = product(bank[c % 4][:, :], (hi[:, k, cols], lo[:, k, cols]), (h_hi[:, k, :], h_lo[:, k, :]), k == 0, k == KD - 1)
                    last.then_inc(self.u_summed, 1)
                pe.wait_ge(self.u_moved, 24)
                pe.wait_ge(self.f_sin, 3)
                for n in range(8):
                    t, q = divmod(n, 4)
                    if n >= 4:
                        pe.wait_ge(self.t_decayed, n - 3)
                    nc.tensor.matmul(bank[n % 4][:, :], self.a[0:WIDTH, t * P:(t + 1) * P], self.w3[0:WIDTH, q * 512:(q + 1) * 512],
                                     start=True, stop=True).then_inc(self.t_summed, 1)
                pe.wait_ge(self.t_mixed, 2)
                pe.wait_ge(self.loaded2, 48)
                for n in range(8):
                    part, fb, half = n // 4, n // 2 % 2, n % 2
                    if n >= 4:
                        pe.wait_ge(self.k_moved, n - 3)
                    for t in range(2):
                        last = nc.tensor.matmul(bank[n % 4][:, :], self.cs[:, part, t, fb * P:(fb + 1) * P],
                                                self.sd[:, part, t, half * 512:(half + 1) * 512], start=(t == 0), stop=(t == 1))
                    last.then_inc(self.k_summed, 1)
                pe.wait_ge(self.t_folded, 2)
                for c in range(KD):
                    last = nc.tensor.matmul(bank[5][:, c:c + 1], self.absh[:, 0, c * P:(c + 1) * P], ones[:, 0:1], start=True, stop=True)
                last.then_inc(self.t_norm, 1)
                pe.wait_ge(self.v_gated, KD)
                for n in range(8):
                    t, half = divmod(n, 2)
                    if n < 4:
                        pe.wait_ge(self.k_moved, 5 + n)
                    else:
                        pe.wait_ge(self.v_moved, n - 3)
                    for q in range(4):
                        last = nc.tensor.transpose(bank[n % 4][:, q * P:(q + 1) * P], self.v[:, 4 * half + q, t * P:(t + 1) * P], ident[:, :])
                    last.then_inc(self.v_turned, 1)
                for s in range(self.SEQS):
                    for n in range(4):
                        fb, half = divmod(n, 2)
                        m = 4 * s + n
                        if m == 0:
                            pe.wait_ge(self.v_moved, 8)
                        if m >= 2:
                            pe.wait_ge(self.s_prod, m - 1)
                        for part in range(2):
                            for t in range(2):
                                last = nc.tensor.matmul(bank[2 * (m % 2) + part][:, :], self.cs[:, part, t, fb * P:(fb + 1) * P],
                                                        self.vt[:, 2 * s + t, half * 512:(half + 1) * 512], start=(t == 0), stop=(t == 1))
                        last.then_inc(self.s_summed, 1)
                    for c in range(KD):
                        pe.wait_ge(self.s_prod, 4 * s + 4)
                        m = KD * s + c
                        if m >= 2:
                            pe.wait_ge(self.y_scaled, m - 1)
                        else:
                            pe.wait_ge(self.t_inv, 1)
                        for fb in range(2):
                            for part in range(2):
                                last = nc.tensor.matmul(bank[4 + m % 2][:, 0:LAT], self.prod[:, 2 * part + fb, c * P:(c + 1) * P],
                                                        self.ics[:, part, fb, :], start=(fb + part == 0), stop=(fb + part == 2))
                        last.then_inc(self.y_summed, 1)
                self.proj.tensor(pe)

            def scalar(self, act):
                self.win.ahead(self.win.round, act)
                act.wait_ge(self.padded, 4)
                for c in range(24):
                    act.wait_ge(self.u_summed, c + 1)
                    if c >= 2:
                        act.wait_ge(self.conv, c - 1)
                    nc.scalar.activation(self.pad[:, c % 2, :, 1:LAT + 1], bank[c % 4][:, :].rearrange("p (s t) -> p s t", s=2),
                                         ACT.Identity, bias=vcol("hy_b_in", c)).then_inc(self.u_moved, 1)
                    if c - 2 in self.SINES:
                        act.wait_ge(self.f_step, self.SIN_STEPS * (self.SINES.index(c - 2) + 1))
                        nc.scalar.activation(self.a[0:WIDTH, :], self.a[0:WIDTH, :], ACT.Sin).then_inc(self.f_sin, 1)
                    if c % 2:
                        self.win.ahead(self.win.round, act, c // 2)
                act.wait_ge(self.t_masked, 1)
                nc.scalar.activation(self.absh.rearrange("p a b -> p (a b)"), self.hfb.rearrange("p a b c -> p (a b c)"), ACT.Abs).then_inc(self.t_abs, 1)
                for n in range(8):
                    part, fb, half = n // 4, n // 2 % 2, n % 2
                    act.wait_ge(self.k_summed, n + 1)
                    nc.scalar.activation(self.kf[:, 2 * part + fb, half * 512:(half + 1) * 512], bank[n % 4][:, :], ACT.Copy).then_inc(self.k_moved, 1)
                for n in range(8):
                    t, half = divmod(n, 2)
                    act.wait_ge(self.v_turned, n + 1)
                    nc.scalar.activation(self.vt[:, t, half * 512:(half + 1) * 512], bank[n % 4][:, :], ACT.Copy).then_inc(self.v_moved, 1)
                act.wait_ge(self.t_inv, 1)
                for m in range(2 * KD):
                    s, c = divmod(m, KD)
                    act.wait_ge(self.y_summed, m + 1)
                    if m >= 2:
                        act.wait_ge(self.y_skip, m - 1)
                    nc.scalar.activation(self.ytmp[:, m % 2, :], bank[4 + m % 2][:, 0:LAT], ACT.Copy, scale=small[:, 8 + c:9 + c]).then_inc(self.y_scaled, 1)
                self.proj.scalar(act)

            def vector(self, dve):
                def sine(r):
                    if r == 0:
                        dve.wait_ge(self.loaded, 16 * 8)
                    a, k = self.a[0:WIDTH, :], self.k[0:WIDTH, :]
                    dve.wait_ge(self.f_summed, r + 1)
                    at = self.SIN_STEPS * r
                    nc.vector.tensor_scalar(a, bank[5][0:WIDTH, 0:LAT], self.fcol[0:WIDTH, r:r + 1], self.fcol[0:WIDTH, 3:4],
                                            ALU.add, ALU.mult).then_inc(self.f_step, 1)
                    dve.wait_ge(self.f_step, at + 1)
                    nc.vector.tensor_scalar(k, a, 1.0 / TWO_PI, ROUND, ALU.mult, ALU.add).then_inc(self.f_step, 1)
                    dve.wait_ge(self.f_step, at + 2)
                    nc.vector.tensor_scalar(k, k, -ROUND, None, ALU.add).then_inc(self.f_step, 1)
                    for n, c in enumerate((PI_HI, PI_MID)):
                        dve.wait_ge(self.f_step, at + 3 + n)
                        nc.vector.scalar_tensor_tensor(a, k, -c, a, ALU.mult, ALU.add).then_inc(self.f_step, 1)
                    dve.wait_ge(self.f_step, at + 5)
                    nc.vector.tensor_scalar(a, a, PI_IN, -PI_IN, ALU.min, ALU.max).then_inc(self.f_step, 1)
                self.win.ahead(self.win.remain, dve)
                for c in range(24):
                    dve.wait_ge(self.u_moved, c + 1)
                    p, dst = self.pad[:, c % 2], self.u[:, c, :].rearrange("p (s t) -> p s t", s=2)
                    nc.vector.tensor_scalar(dst, p[:, :, 1:LAT + 1], vcol("hy_conv_w", 24 + c), vcol("hy_conv_b", c),
                                            ALU.mult, ALU.add).then_inc(self.conv_step, 1)
                    dve.wait_ge(self.conv_step, 2 * c + 1)
                    nc.vector.scalar_tensor_tensor(dst, p[:, :, 0:LAT], vcol("hy_conv_w", c), dst, ALU.mult, ALU.add).then_inc(self.conv_step, 1)
                    dve.wait_ge(self.conv_step, 2 * c + 2)
                    nc.vector.scalar_tensor_tensor(dst, p[:, :, 2:LAT + 2], vcol("hy_conv_w", 48 + c), dst, ALU.mult, ALU.add).then_inc(self.conv, 1)
                    if c >= 16:
                        dve.wait_ge(self.conv, c + 1)
                        nc.vector.tensor_tensor(self.u[:, c, :], self.u[:, c, :], self.u[:, c - 8, :], ALU.mult).then_inc(self.v_gated, 1)
                    if c % 2:
                        self.win.ahead(self.win.remain, dve, c // 2)
                    if c in self.SINES:
                        sine(self.SINES.index(c))
                dve.wait_ge(self.loaded2, 48)
                for n in range(8):
                    t, q = divmod(n, 4)
                    dr, half = divmod(q, 2)
                    dve.wait_ge(self.t_summed, n + 1)
                    nc.vector.tensor_tensor(self.hfb[:, t, dr, half * 512:(half + 1) * 512], bank[n % 4][:, :],
                                            self.dec[:, t, half * 512:(half + 1) * 512], ALU.mult).then_inc(self.t_decayed, 1)
                dve.wait_ge(self.t_decayed, 8)
                nc.vector.memset(self.hfb[0:1, 0, 1, :], 0.0).then_inc(self.t_masked, 1)
                dve.wait_ge(self.t_masked, 1)
                hf, hb = self.hfb[:, :, 0, :], self.hfb[:, :, 1, :]
                nc.vector.tensor_tensor(self.sd[:, 0], hf, hb, ALU.add).then_inc(self.t_mixed, 1)
                nc.vector.tensor_tensor(self.sd[:, 1], hb, hf, ALU.subtract).then_inc(self.t_mixed, 1)
                dve.wait_ge(self.t_norm, 1)
                nc.vector.reciprocal(small[:, 8:16], bank[5][:, 0:KD]).then_inc(self.t_inv, 1)
                dve.wait_ge(self.k_moved, 8)
                for s in range(self.SEQS):
                    for n in range(4):
                        fb, half = divmod(n, 2)
                        m = 4 * s + n
                        cols = slice(half * 512, (half + 1) * 512)
                        vr, vi = bank[2 * (m % 2)][:, :], bank[2 * (m % 2) + 1][:, :]
                        kr, ki = self.kf[:, fb, cols], self.kf[:, 2 + fb, cols]
                        dve.wait_ge(self.s_summed, m + 1)
                        if m == 4:
                            dve.wait_ge(self.y_summed, KD)
                        if m >= 1:
                            dve.wait_ge(self.s_prod, m)
                        nc.vector.tensor_tensor(self.tmp[:, 0, :], vr, kr, ALU.mult).then_inc(self.s_step, 1)
                        nc.vector.tensor_tensor(self.tmp[:, 1, :], vi, ki, ALU.mult).then_inc(self.s_step, 1)
                        nc.vector.tensor_tensor(self.tmp[:, 2, :], vr, ki, ALU.mult).then_inc(self.s_step, 1)
                        nc.vector.tensor_tensor(self.tmp[:, 3, :], vi, kr, ALU.mult).then_inc(self.s_step, 1)
                        dve.wait_ge(self.s_step, 5 * m + 2)
                        nc.vector.tensor_tensor(self.prod[:, fb, cols], self.tmp[:, 0, :], self.tmp[:, 1, :], ALU.add).then_inc(self.s_step, 1)
                        dve.wait_ge(self.s_step, 5 * m + 5)
                        nc.vector.tensor_tensor(self.prod[:, 2 + fb, cols], self.tmp[:, 2, :], self.tmp[:, 3, :], ALU.subtract).then_inc(self.s_prod, 1)
                    for c in range(KD):
                        m = KD * s + c
                        v = self.v[:, c, s * LAT:(s + 1) * LAT]
                        dve.wait_ge(self.y_scaled, m + 1)
                        nc.vector.scalar_tensor_tensor(v, v, vcol("hy_skip", c), self.ytmp[:, m % 2, :], ALU.mult, ALU.add).then_inc(self.y_skip, 1)
                        dve.wait_ge(self.y_skip, m + 1)
                        nc.vector.tensor_tensor(h[:, c, s * LAT:(s + 1) * LAT], v, self.u[:, c, s * LAT:(s + 1) * LAT], ALU.mult).then_inc(self.y_gated, 1)

        class S5:

            BATCH = 4
            NB = HALF // BATCH

            def __init__(self, pre, post, n_in, n):
                self.pre = pre
                self.u = area(0, GROUPS, 2 * CH)
                self.yf = area(27776, STEP, KD * CH)
                self.t = area(4096, 2, LAGS, GROUPS)
                self.b = area(7296, 2, GROUPS, GC)
                self.c = area(9344, 2, GROUPS, GC)
                self.f = area(11392, HALF, 2, P)
                self.m0 = area(19584, HALF, P)
                self.e = area(23680, HALF, 2, 2 * CH)
                self.pw = area(27776, self.BATCH, 2, P)
                self.et = area(28800, self.BATCH, 2, P)
                self.s2 = area(27776, HALF, 2, CH)
                self.t0 = area(29824, 512)
                self.gst = area(30336, self.BATCH, 240)
                self.lab = area(31296, 2, GROUPS, 2)
                self.mi = area(26880, 15, GROUPS)
                self.t1 = rstd
                self.lags = small[:, 20:20 + LAGS]
                self.rc = area(11392, 2, 8, P)
                self.rl = area(13440, 2, P)
                self.ldt = area(13696, GROUPS)
                self.rb = area(13760, 2, GROUPS, GC)
                self.w = area(15808, 5, LAGS, GROUPS)
                self.y = x[:, :, LAT:TOK]
                self.h_dram = nc.dram_tensor("s5_tokens", [P, KD * TOK], F32, kind="Internal").ap()
                self.y_dram = nc.dram_tensor("s5_outputs", [P, KD * LAT], F32, kind="Internal").ap()
                s = lambda n: sem("s5_" + n)
                self.h_stored, self.y_stored = s("h_stored"), s("y_stored")
                self.loaded, self.u_loaded, self.m_loaded, self.y_loaded = s("loaded"), s("u_loaded"), s("toeplitz_loaded"), s("y_loaded")
                self.turned, self.param, self.prep, self.act_prep = s("params_turned"), s("params_moved"), s("prep_step"), s("prep_act")
                self.in_step, self.in_ready, self.out_step, self.out_ready = s("in_step"), s("in_ready"), s("out_step"), s("out_ready")
                self.in_turned, self.et_moved = s("in_turned"), s("in_moved")
                self.g_summed, self.g_moved = s("taps_summed"), s("taps_moved")
                self.e_summed, self.e_moved = s("inject_summed"), s("inject_moved")
                self.step, self.s_moved = s("scan_step"), s("states_moved")
                self.y_summed, self.y_moved, self.skipped, self.gelu = s("y_summed"), s("y_moved"), s("skipped"), s("gelu")
                self.gate, self.glu, self.moved = s("glu_gate"), s("glu"), s("glu_moved")
                self.up = Gated("s5_glu", A["s5_w_glu"][0], D, lambda k: self.yf.rearrange("p s (k m) -> p k s m", m=CH)[:, k], LAT,
                                lambda pe, k: pe.wait_ge(self.gelu, k + 1), self.glu)
                self.post = post
                self.yk = self.yf.rearrange("p s (k m) -> p k s m", m=CH)

            def sync(self, sp):
                sp_issue(sp, self.up.w.p0 + RING)
                self.pre.wait(sp)
                sp.dma_start(self.h_dram, h[:, :, :].rearrange("p k t -> p (k t)")).then_inc(self.h_stored, 16)
                sp.wait_ge(self.h_stored, 16)
                for gl in range(8):
                    src = self.h_dram.rearrange("(g c) (s n) -> g s c n", c=GC, s=STEP)[gl]
                    dst = self.u[:, gl * 8:(gl + 1) * 8, :].rearrange("p g j -> p (g j)")
                    sp.dma_start(dst, src).then_inc(self.u_loaded, 16)
                for n in range(2 * self.NB):
                    hf, b = divmod(n, self.NB)
                    sp.wait_ge(self.g_moved, 2 * n + 2)
                    if n == self.NB:
                        sp.wait_ge(self.y_summed, 2)
                    for k in range(STEP):
                        sp.dma_start(self.m0[k * GC:(k + 1) * GC, b * self.BATCH:(b + 1) * self.BATCH, :],
                                     self.gst[0:GC, :, (7 - k) * GC:(7 - k) * GC + P]).then_inc(self.m_loaded, 16)
                for hf in range(2):
                    sp.wait_ge(self.y_moved, 2 * (hf + 1))
                    sp.dma_start(self.y_dram[:, hf * D:(hf + 1) * D].rearrange("p (g n) -> p g n", g=4),
                                 self.y[:, 4 * hf:4 * hf + 4, :]).then_inc(self.y_stored, 16)
                    sp.wait_ge(self.y_stored, 16 * (hf + 1))
                    if hf == 0:
                        sp.wait_ge(self.y_summed, 4)
                    for gl in range(4 * hf, 4 * hf + 4):
                        src = self.y_dram.rearrange("(s c) (g n) -> g c s n", c=GC, g=8)[gl]
                        sp.dma_start(self.yf[gl * GC:(gl + 1) * GC], src).then_inc(self.y_loaded, 16)

            def gpsimd(self, pool):
                self.pre.wait_x(pool)
                for i, (lam, cc, bb) in enumerate((("s5_lambda_re", "s5_c_re", "s5_b_re"), ("s5_lambda_im", "s5_c_im", "s5_b_im"))):
                    pool.dma_start(self.rl[0:GROUPS, i].rearrange("g (d s) -> g d s", d=2), A[lam][0].rearrange("d g s -> g d s")).then_inc(self.loaded, 16)
                    for d in range(2):
                        pool.dma_start(self.rc[:, i].rearrange("p k (d s) -> p k d s", d=2)[:, :, d, :],
                                       A[cc][0, d].rearrange("(k g) c s -> (g c) k s", k=8)).then_inc(self.loaded, 16)
                        pool.dma_start(self.rb[d * STATE:(d + 1) * STATE, i], A[bb][0, d].rearrange("g s c -> s g c")).then_inc(self.loaded, 16)
                for d in range(2):
                    pool.dma_start(self.ldt[d * STATE:(d + 1) * STATE], A["s5_log_dt"][0, d:d + 1, :].to_broadcast([STATE, GROUPS])).then_inc(self.loaded, 16)
                pool.dma_start(self.lags, A["k_s5_lags"]).then_inc(self.loaded, 16)
                pool.wait_ge(self.prep, self.PREP)
                for n in range(2 * self.NB):
                    hf, b = divmod(n, self.NB)
                    if n == self.NB:
                        pool.wait_ge(self.y_summed, 2)
                    g0 = n * self.BATCH
                    pr, pi = (self.lag(i, STEP, g0) for i in range(2))
                    cr, ci = (self.chan(self.c, i, g0) for i in range(2))
                    dst = [self.f[:, b * self.BATCH:(b + 1) * self.BATCH, i].rearrange("p g (s c) -> p g s c", c=GC) for i in range(2)]
                    t1 = self.t1[:, :].rearrange("p (g s c) -> p g s c", s=STEP, c=GC)
                    at = 6 * n
                    tt = nc.gpsimd.tensor_tensor
                    if n:
                        pool.wait_ge(self.out_step, at)
                    tt(dst[0], pr, cr, ALU.mult).then_inc(self.out_step, 1)
                    tt(dst[1], pr, ci, ALU.mult).then_inc(self.out_step, 1)
                    tt(t1, pi, ci, ALU.mult).then_inc(self.out_step, 1)
                    pool.wait_ge(self.out_step, at + 3)
                    tt(dst[0], dst[0], t1, ALU.add).then_inc(self.out_step, 1)
                    pool.wait_ge(self.out_step, at + 4)
                    tt(t1, pi, cr, ALU.mult).then_inc(self.out_step, 1)
                    pool.wait_ge(self.out_step, at + 5)
                    tt(dst[1], dst[1], t1, ALU.subtract).then_inc(self.out_step, 1)

            def lag(self, i, slot, g0):
                return self.t[:, i, slot:slot + STEP, self.of(g0)].rearrange("p s g -> p g s").unsqueeze(3) \
                    .to_broadcast([P, self.BATCH, STEP, GC])

            def of(self, place, n=None):
                g = place % 8 * 8 + place // 8
                return slice(g, g + 8 * ((n or self.BATCH) - 1) + 1, 8)

            def chan(self, src, i, g0):
                return src[:, i, self.of(g0), :].unsqueeze(2).to_broadcast([P, self.BATCH, STEP, GC])

            PREP = 43

            def vector(self, dve):
                V = nc.vector
                for i in range(2):
                    dve.wait_ge(self.turned, 1 + i)
                    V.tensor_copy(self.mi[:, i, :], bank[i][:, 0:GROUPS]).then_inc(self.param, 1)
                for n in range(4):
                    i, half = divmod(n, 2)
                    dve.wait_ge(self.turned, 3 + n)
                    dst = self.c[:, i, half * 32:(half + 1) * 32, :].rearrange("p g c -> p (g c)")
                    V.tensor_scalar(dst, bank[2 + n][:, :], -1.0 if i else 1.0, None, ALU.mult).then_inc(self.param, 1)
                dve.wait_ge(self.param, 6)
                dve.wait_ge(self.act_prep, 1)
                dve.wait_ge(self.loaded, 16 * 13)
                steps = [0]

                def then(ins):
                    steps[0] += 1
                    ins.then_inc(self.prep, 1)
                    dve.wait_ge(self.prep, steps[0])
                m = lambda j: self.mi[:, j, :]
                w = lambda j: self.w[:, j]
                lr, li, dt = m(0), m(1), m(2)
                lag3 = self.lags.unsqueeze(2).to_broadcast([P, LAGS, GROUPS])
                per = lambda v: v.unsqueeze(1).to_broadcast([P, LAGS, GROUPS])
                then(V.tensor_tensor(m(3), lr, dt, ALU.mult))
                then(V.tensor_tensor(m(4), li, dt, ALU.mult))
                then(V.tensor_tensor(w(0), lag3, per(m(3)), ALU.mult))
                then(V.tensor_tensor(w(1), lag3, per(m(4)), ALU.mult))
                then(V.tensor_scalar(w(2), w(1), 1.0 / TWO_PI, ROUND, ALU.mult, ALU.add))
                then(V.tensor_scalar(w(2), w(2), -ROUND, None, ALU.add))
                for c in (PI_HI, PI_MID, PI_LO):
                    then(V.scalar_tensor_tensor(w(1), w(2), -c, w(1), ALU.mult, ALU.add))
                then(V.tensor_scalar(w(1), w(1), PI_IN, -PI_IN, ALU.min, ALU.max))
                assert steps[0] == 10
                dve.wait_ge(self.act_prep, 5)
                then(V.tensor_tensor(w(4), w(2), w(2), ALU.mult))
                then(V.tensor_scalar(w(1), w(4), -2.0, 1.0, ALU.mult, ALU.add))
                then(V.tensor_tensor(self.t[:, 0], w(0), w(1), ALU.mult))
                then(V.tensor_tensor(self.t[:, 1], w(0), w(3), ALU.mult))
                e1, c1, q1 = self.w[:, 0, 16, :], self.w[:, 1, 16, :], self.w[:, 4, 16, :]
                then(V.scalar_tensor_tensor(m(5), e1, 1.0, m(5), ALU.add, ALU.mult))
                then(V.tensor_tensor(m(5), m(5), c1, ALU.mult))
                then(V.scalar_tensor_tensor(m(5), q1, -2.0, m(5), ALU.mult, ALU.add))
                xr, xi = m(5), self.t[:, 1, 16, :]
                then(V.tensor_tensor(m(8), lr, lr, ALU.mult))
                then(V.tensor_tensor(m(9), li, li, ALU.mult))
                then(V.tensor_tensor(m(8), m(8), m(9), ALU.add))
                then(V.reciprocal(m(8), m(8)))
                then(V.tensor_tensor(m(6), xr, lr, ALU.mult))
                then(V.tensor_tensor(m(9), xi, li, ALU.mult))
                then(V.tensor_tensor(m(6), m(6), m(9), ALU.add))
                then(V.tensor_tensor(m(6), m(6), m(8), ALU.mult))
                then(V.tensor_tensor(m(7), xi, lr, ALU.mult))
                then(V.tensor_tensor(m(9), xr, li, ALU.mult))
                then(V.tensor_tensor(m(7), m(7), m(9), ALU.subtract))
                then(V.tensor_tensor(m(7), m(7), m(8), ALU.mult))
                qr, qi = (m(j).unsqueeze(2).to_broadcast([P, GROUPS, GC]) for j in (6, 7))
                br, bi = self.rb[:, 0], self.rb[:, 1]
                tmp = self.w[:, 0:1].rearrange("p a b c -> p (a b c)")[:, 0:GROUPS * GC].rearrange("p (g c) -> p g c", c=GC)
                then(V.tensor_tensor(self.b[:, 0], qr, br, ALU.mult))
                then(V.tensor_tensor(tmp, qi, bi, ALU.mult))
                then(V.tensor_tensor(self.b[:, 0], self.b[:, 0], tmp, ALU.subtract))
                then(V.tensor_tensor(self.b[:, 1], qr, bi, ALU.mult))
                then(V.tensor_tensor(tmp, qi, br, ALU.mult))
                then(V.tensor_tensor(self.b[:, 1], self.b[:, 1], tmp, ALU.add))
                la, lb = self.lab[:, 0], self.lab[:, 1]
                l8r, l8i = (self.t[:, i, 17, :].rearrange("p (k g) -> p g k", k=8) for i in range(2))
                then(V.tensor_copy(la[:, :, 0].rearrange("p (g k) -> p g k", k=8), l8r))
                then(V.tensor_copy(la[:, :, 1].rearrange("p (g k) -> p g k", k=8), l8r))
                then(V.tensor_copy(lb[:, :, 0].rearrange("p (g k) -> p g k", k=8), l8i))
                then(V.tensor_scalar(lb[:, :, 1].rearrange("p (g k) -> p g k", k=8), l8i, -1.0, None, ALU.mult))
                while steps[0] < self.PREP:
                    then(V.tensor_copy(m(14), m(0)))
                assert steps[0] == self.PREP, steps[0]
                t0 = self.t0[:, :].rearrange("p (g s c) -> p g s c", s=STEP, c=GC)

                def inputs(n):
                    g0 = n * self.BATCH
                    pr, pi = (self.lag(i, 0, g0) for i in range(2))
                    br, bi = (self.chan(self.b, i, g0) for i in range(2))
                    dst = [self.pw[:, :, i].rearrange("p g (s c) -> p g s c", c=GC) for i in range(2)]
                    at = 5 * n
                    if n:
                        dve.wait_ge(self.in_turned, 2 * n)
                    if n == self.NB:
                        dve.wait_ge(self.y_summed, 2)
                    tt = V.tensor_tensor
                    tt(dst[0], pr, br, ALU.mult).then_inc(self.in_step, 1)
                    tt(dst[1], pr, bi, ALU.mult).then_inc(self.in_step, 1)
                    tt(t0, pi, bi, ALU.mult).then_inc(self.in_step, 1)
                    dve.wait_ge(self.in_step, at + 3)
                    tt(dst[0], dst[0], t0, ALU.subtract).then_inc(self.in_step, 1)
                    dve.wait_ge(self.in_step, at + 4)
                    tt(t0, pi, br, ALU.mult).then_inc(self.in_step, 1)
                    dve.wait_ge(self.in_step, at + 5)
                    tt(dst[1], dst[1], t0, ALU.add).then_inc(self.in_ready, 1)

                def taps_out(n):
                    for q in range(2):
                        dve.wait_ge(self.g_summed, 2 * n + q + 1)
                        if n and q == 0:
                            dve.wait_ge(self.m_loaded, 16 * STEP * n)
                        taps = [bank[i + q][0:GC, 0:480].rearrange("p (g n) -> p g n", g=2) for i in (2, 5)]
                        V.tensor_copy(self.gst[0:GC, 2 * q:2 * q + 2, 0:112], taps[1][:, :, 0:112])
                        V.tensor_copy(self.gst[0:GC, 2 * q:2 * q + 2, 112:240], taps[0][:, :, 112:240]).then_inc(self.g_moved, 1)

                steps2 = [0]

                def scan(ins):
                    steps2[0] += 1
                    ins.then_inc(self.step, 1)
                    dve.wait_ge(self.step, steps2[0])
                for hf in range(2):
                    inputs(hf * self.NB)
                    for b in range(self.NB):
                        n = hf * self.NB + b
                        if b + 1 < self.NB:
                            inputs(n + 1)
                        taps_out(n)
                    dve.wait_ge(self.e_moved, 2 * self.NB * (hf + 1))
                    dve.wait_ge(self.out_step, 6 * self.NB * (hf + 1))
                    blocks = 2 * CH // BLK
                    sa, sb_ = (v[:, hf * HALF:(hf + 1) * HALF, :] for v in (la, lb))
                    wide = lambda v: v.unsqueeze(3).to_broadcast([P, HALF, 2, blocks])
                    ta, tb = (v[:, 0:HALF * 2 * blocks].rearrange("p (g r b) -> p g r b", r=2, b=blocks) for v in (self.t0, self.t1))
                    e5 = self.e.rearrange("p g r (b q) -> p g r b q", q=BLK)
                    base = steps2[0]
                    with dve.Fori(1, BLK) as i:
                        prev = e5[:, :, :, :, bass.ds(i - 1, 1)].rearrange("p g r b o -> p g r (b o)")
                        cur = e5[:, :, :, :, bass.ds(i, 1)].rearrange("p g r b o -> p g r (b o)")
                        V.tensor_tensor(ta, wide(sa), prev, ALU.mult).then_inc(self.step, 1)
                        V.tensor_tensor(tb[:, :, ::-1, :], wide(sb_), prev, ALU.mult).then_inc(self.step, 1)
                        dve.wait_ge(self.step, base + 4 * i - 2)
                        V.tensor_tensor(ta, ta, tb, ALU.add).then_inc(self.step, 1)
                        dve.wait_ge(self.step, base + 4 * i - 1)
                        V.tensor_tensor(cur, cur, ta, ALU.add).then_inc(self.step, 1)
                        dve.wait_ge(self.step, base + 4 * i)
                    steps2[0] += 4 * (BLK - 1)
                    def table(i, slot0, n):
                        v = self.t[:, i, slot0:slot0 + n, :].rearrange("p q (k g) -> p g k q", k=8)
                        return v[:, 4 * hf:4 * hf + 4]
                    halfv = lambda v: v.rearrange("p (g k) q -> p g k q", k=8)
                    er, ei = (self.e[:, :, r, :] for r in range(2))
                    s0, s1 = (v[:, 0:HALF].unsqueeze(2) for v in (self.t0, self.t1))
                    c_r, c_i = table(0, 24, 1), table(1, 24, 1)
                    for blk in range(1, blocks):
                        pcol, ccol = BLK * blk - 1, BLK * blk + BLK - 1
                        pr_, pi_ = halfv(er[:, :, pcol:pcol + 1]), halfv(ei[:, :, pcol:pcol + 1])
                        for c, (va, vb, op) in ((er, (pr_, pi_, ALU.subtract)), (ei, (pi_, pr_, ALU.add))):
                            cc = c[:, :, ccol:ccol + 1]
                            V.tensor_tensor(halfv(s0), c_r, va, ALU.mult)
                            scan(V.tensor_tensor(halfv(s1), c_i, vb, ALU.mult))
                            scan(V.tensor_tensor(s0, s0, s1, op))
                            scan(V.tensor_tensor(cc, cc, s0, ALU.add))
                    nq = BLK - 1
                    for b0 in range(4, 8, 2):
                        for gl in range(4):
                            gs = slice(8 * gl, 8 * gl + 8)
                            lv = lambda v: v[:, gs, BLK * b0:BLK * (b0 + 2)].rearrange("p g (b q) -> p g b q", q=BLK)[:, :, :, 0:nq]
                            ends = lambda v: v[:, gs, BLK * b0 - 1:BLK * b0 + BLK:BLK].unsqueeze(3).to_broadcast([P, 8, 2, nq])
                            tq = [self.t[:, i, 17:17 + nq, 4 * hf + gl:GROUPS:8].rearrange("p q k -> p k q").unsqueeze(2).to_broadcast([P, 8, 2, nq]) for i in range(2)]
                            u0, u1, u2, u3 = ((self.t0, self.t1)[i // 2][:, (i % 2) * 112:(i % 2) * 112 + 112].rearrange("p (g b q) -> p g b q", b=2, q=nq)
                                              for i in range(4))
                            V.tensor_tensor(u0, tq[0], ends(er), ALU.mult)
                            V.tensor_tensor(u1, tq[1], ends(ei), ALU.mult)
                            V.tensor_tensor(u2, tq[0], ends(ei), ALU.mult)
                            scan(V.tensor_tensor(u3, tq[1], ends(er), ALU.mult))
                            V.tensor_tensor(u0, u0, u1, ALU.subtract)
                            scan(V.tensor_tensor(u2, u2, u3, ALU.add))
                            V.tensor_tensor(lv(er), lv(er), u0, ALU.add)
                            scan(V.tensor_tensor(lv(ei), lv(ei), u2, ALU.add))
                    V.tensor_copy(self.s2[0:STATE], self.e[0:STATE, :, :, CH - 1:2 * CH - 1]).then_inc(self.s_moved, 1)
                    V.tensor_copy(self.s2[STATE:P], self.e[STATE:P, :, :, 2 * CH - 2:CH - 2:-1]).then_inc(self.s_moved, 1)
                    for q in range(2):
                        dve.wait_ge(self.y_summed, 2 * hf + q + 1)
                        gl = 4 * hf + 2 * q
                        V.tensor_copy(self.y[:, gl:gl + 2, :], bank[5 + q][:, :].rearrange("p (g n) -> p g n", g=2)).then_inc(self.y_moved, 1)
                dve.wait_ge(self.y_loaded, 16 * 8)
                for k in range(KD):
                    yv = self.yk[:, k]
                    V.scalar_tensor_tensor(yv, h_split[:, :, k, 0, :], vcol("s5_d", k), yv, ALU.mult, ALU.add).then_inc(self.skipped, 1)
                for c in range(KD):
                    dve.wait_ge(self.gate, c + 1)
                    dst = Y[:, c, 0:LAT].rearrange("p (m s) -> p s m", s=STEP)
                    V.scalar_tensor_tensor(dst, self.up.bank(c, 0)[:, 0:LAT].rearrange("p (s m) -> p s m", m=CH), vcol("s5_b_glu", c),
                                           self.sig[:, c % 2, :].rearrange("p (s m) -> p s m", m=CH), ALU.add, ALU.mult).then_inc(self.glu, 1)

            def tensor(self, pe):
                self.pre.wait(pe)
                pe.wait_ge(self.loaded, 16 * 13)
                for i in range(2):
                    nc.tensor.transpose(bank[i][:, 0:GROUPS], self.rl[0:GROUPS, i, :], ident[0:GROUPS, 0:GROUPS]).then_inc(self.turned, 1)
                for n in range(4):
                    i, half = divmod(n, 2)
                    for q in range(4):
                        last = nc.tensor.transpose(bank[2 + n][:, q * P:(q + 1) * P], self.rc[:, i, 4 * half + q, :], ident[:, :])
                    last.then_inc(self.turned, 1)
                pe.wait_ge(self.param, 6)
                pe.wait_ge(self.u_loaded, 16 * 8)
                for hf in range(2):
                    for b in range(self.NB):
                        n = hf * self.NB + b
                        g0 = n * self.BATCH
                        pe.wait_ge(self.in_ready, n + 1)
                        for q in range(2):
                            if n:
                                pe.wait_ge(self.et_moved, 2 * n)
                            for j in range(4):
                                last = nc.tensor.transpose(bank[q][:, j * P:(j + 1) * P], self.pw[:, 2 * q + j // 2, j % 2, :], ident[:, :])
                            last.then_inc(self.in_turned, 1)
                        pe.wait_ge(self.out_step, 6 * (n + 1))
                        for q in range(2):
                            if n:
                                pe.wait_ge(self.g_moved, 2 * n - 1 + q)
                            for j in range(2):
                                gb = 2 * q + j
                                g, gh = self.of(g0 + gb, 1).start, b * self.BATCH + gb
                                if n == self.NB:
                                    pe.wait_ge(self.y_moved, 2)
                                for lo, hi, rows, rhs in (
                                        (112, 128, slice(0, P), lambda i: self.c[:, i, g, :]),
                                        (128, 240, slice(0, STATE), lambda i: self.f[0:STATE, gh, i, 0:112]),
                                        (0, 112, slice(STATE, P), lambda i: self.f[STATE:P, gh, i, 16:P])):
                                    for i in range(2):
                                        last = nc.tensor.matmul(bank[(2 if lo else 5) + q][0:GC, j * 240 + lo:j * 240 + hi], self.b[rows, i, g, :], rhs(i),
                                                                start=(i == 0), stop=(i == 1))
                            last.then_inc(self.g_summed, 1)
                        pe.wait_ge(self.et_moved, 2 * n + 2)
                        if n:
                            pe.wait_ge(self.e_moved, 2 * n)
                        for gb in range(self.BATCH):
                            for i in range(2):
                                o = (2 * gb + i) * 2 * CH
                                last = nc.tensor.matmul(bank[4][:, o:o + 2 * CH], self.et[:, gb, i, :], self.u[:, g0 + gb, :],
                                                        start=True, stop=True)
                        last.then_inc(self.e_summed, 1)
                    pe.wait_ge(self.m_loaded, 16 * STEP * self.NB * (hf + 1))
                    pe.wait_ge(self.s_moved, 2 * hf + 2)
                    for q in range(2):
                        for j in range(16):
                            gh = q * 16 + j
                            g = hf * HALF + gh
                            o = bank[5 + q][:, j * CH:(j + 1) * CH]
                            nc.tensor.matmul(o, self.m0[:, gh, :], self.u[:, g, 0:CH], start=True, stop=False)
                            nc.tensor.matmul(o, self.f[:, gh, 0, :], self.s2[:, gh, 0, :], start=False, stop=False)
                            last = nc.tensor.matmul(o, self.f[:, gh, 1, :], self.s2[:, gh, 1, :], start=False, stop=True)
                        last.then_inc(self.y_summed, 1)
                self.up.tensor(pe)

            @property
            def sig(self):
                return area(23680, 2, LAT)

            def scalar(self, act):
                act.wait_ge(self.loaded, 16 * 13)
                nc.scalar.activation(self.mi[:, 2, :], self.ldt, ACT.Exp).then_inc(self.act_prep, 1)
                act.wait_ge(self.prep, 10)
                nc.scalar.activation(self.w[:, 0], self.w[:, 0], ACT.Exp).then_inc(self.act_prep, 1)
                nc.scalar.activation(self.mi[:, 5, :], self.mi[:, 3, :], ACT.Tanh, scale=0.5).then_inc(self.act_prep, 1)
                nc.scalar.activation(self.w[:, 2], self.w[:, 1], ACT.Sin, scale=0.5).then_inc(self.act_prep, 1)
                nc.scalar.activation(self.w[:, 3], self.w[:, 1], ACT.Sin).then_inc(self.act_prep, 1)
                for n in range(2 * self.NB):
                    hf, b = divmod(n, self.NB)
                    for q in range(2):
                        act.wait_ge(self.in_turned, 2 * n + q + 1)
                        if n:
                            act.wait_ge(self.e_summed, n)
                        if n == self.NB:
                            act.wait_ge(self.y_summed, 2)
                        nc.scalar.activation(self.et[:, 2 * q:2 * q + 2].rearrange("p g i n -> p (g i n)"), bank[q][:, :], ACT.Copy).then_inc(self.et_moved, 1)
                    act.wait_ge(self.e_summed, n + 1)
                    if n == self.NB:
                        act.wait_ge(self.s_moved, 2)
                    dst = self.e[:, b * self.BATCH:(b + 1) * self.BATCH]
                    src = bank[4][:, :].rearrange("p (g z m) -> p g z m", z=2, m=CH)
                    fw = dst[0:STATE].rearrange("p g r (z m) -> p (g r) z m", m=CH)
                    nc.scalar.activation(fw[:, :, ::-1, :], src[0:STATE], ACT.Copy).then_inc(self.e_moved, 1)
                    bw = dst[STATE:P].rearrange("p g r j -> p (g r) j")
                    nc.scalar.activation(bw[:, :, ::-1], bank[4][STATE:P, :].rearrange("p (g j) -> p g j", j=2 * CH), ACT.Copy).then_inc(self.e_moved, 1)
                for k in range(KD):
                    act.wait_ge(self.skipped, k + 1)
                    nc.scalar.activation(self.yk[:, k], self.yk[:, k], ACT.Gelu).then_inc(self.gelu, 1)
                def take(c):
                    act.wait_ge(self.glu, c + 1)
                    self.post.move(act, c, Y[:, c, :]).then_inc(self.moved, 1)
                for c in range(KD):
                    self.up.summed(act, c, 1)
                    if c >= 2:
                        act.wait_ge(self.glu, c - 1)
                    nc.scalar.activation(self.sig[:, c % 2, :], self.up.bank(c, 1)[:, 0:LAT], ACT.Sigmoid,
                                         bias=vcol("s5_b_glu", KD + c)).then_inc(self.gate, 1)
                    if c >= 1:
                        take(c - 1)
                take(KD - 1)

        class Fnet:

            def __init__(self, pre, post, n_in, n):
                self.pre = pre
                self.loaded, self.chan, self.chan_moved = sem("fn_loaded"), sem("fn_channels"), sem("fn_channels_moved")
                self.tok, self.tok_moved = sem("fn_tokens"), sem("fn_tokens_moved")
                at = 2 * KD * TOK
                self.cs = area(at, 2 * P)
                self.tt = area(at + 256, 2, 2, LAT)
                self.a = area(at + 1280, 2, KD, 2 * P)
                self.f = area(3 * P * KD * 8, KD, LAT)
                self.proj = Linear("fn_out", A["fn_w_o"][0], KD, lambda k: self.f[:, k, :], LAT,
                                   lambda pe, k: pe.wait_ge(self.tok_moved, k // 2 + 1),
                                   lambda act, c, b: post.move(act, c, b, "fn_b_o"))

            def sync(self, sp):
                sp_issue(sp, self.proj.w.p0)
                self.pre.wait_x(sp)
                sp.dma_start(self.cs, A["k_dft128"]).then_inc(self.loaded, 16)
                sp.dma_start(self.tt, A["k_dft256"]).then_inc(self.loaded, 16)

            def tensor(self, pe):
                self.pre.wait(pe)
                pe.wait_ge(self.loaded, 32)
                for t in range(2):
                    for g2 in range(KD // 2):
                        n = 4 * t + g2
                        if n >= 4:
                            pe.wait_ge(self.chan_moved, n - 3)
                        for q in range(2):
                            g = 2 * g2 + q
                            last = nc.tensor.matmul(bank[n % 4][:, q * 256:(q + 1) * 256], h[:, g, t * P:(t + 1) * P],
                                                    self.cs[:, :], start=True, stop=True)
                        last.then_inc(self.chan, 1)
                for g2 in range(KD // 2):
                    pe.wait_ge(self.chan_moved, 5 + g2)
                    for q in range(2):
                        g = 2 * g2 + q
                        for t in range(2):
                            for part in range(2):
                                last = nc.tensor.matmul(bank[g2][:, q * 256:(q + 1) * 256],
                                                        self.a[:, t, g, part * P:(part + 1) * P],
                                                        self.tt[:, part, t, :], start=(t + part == 0), stop=(t + part == 2))
                    last.then_inc(self.tok, 1)
                self.proj.tensor(pe)

            def vector(self, dve):
                for n in range(8):
                    t, g2 = divmod(n, 4)
                    dve.wait_ge(self.chan, n + 1)
                    nc.vector.tensor_copy(self.a[:, t, 2 * g2:2 * g2 + 2, :].rearrange("p g c -> p (g c)"), bank[n % 4][:, :]).then_inc(self.chan_moved, 1)
                for g2 in range(KD // 2):
                    dve.wait_ge(self.tok, g2 + 1)
                    nc.vector.tensor_copy(self.f[:, 2 * g2:2 * g2 + 2, :].rearrange("p g c -> p (g c)"), bank[g2][:, :]).then_inc(self.tok_moved, 1)

            def scalar(self, act):
                self.proj.scalar(act)

        MIXER = {0: Mla, 1: Hyena, 2: S5, 3: Fnet}
        stages = [Setup()]
        live = [l for l in range(DEPTH) if l in layers]
        mods = {l: Modulation(l) for l in live}
        stages.append(mods[live[0]].part(0))
        for l in live:
            mod = mods[l]
            n_in = TOK if l < 3 else LAT
            n_out = TOK if l < 2 else LAT
            pre = PreNorm(mod, False, n_in, split=(l == 2), parts=(l < 2))
            gate = mod.part(1)
            post = PostNorm(mod, False, n_out)
            mixer = MIXER[l](pre, post, n_in, n_out)
            post.number()
            scale2 = mod.part(2)
            scale2.after = post
            pre2 = PreNorm(mod, True, n_out, parts=True)
            gate2 = mod.part(3)
            post2 = PostNorm(mod, True, n_out)
            ffn = Ffn(l, n_out, pre2, post2)
            post2.number()
            stages += [pre, gate, mixer, post, scale2, pre2, gate2, ffn, post2]
            if l != live[-1]:
                stages.append(mods[live[live.index(l) + 1]].part(0))

        out_turned = sem("out_turned")
        out_moved = sem("out_moved")
        stored = sem("stored")
        orow = area(2 * KD * TOK, 2, D)

        class Store:

            def tensor(self, pe):
                for t in range(2):
                    for half in range(2):
                        for q in range(4):
                            k = 4 * half + q
                            if t == 0:
                                post2.wait(pe, k)
                            last = nc.tensor.transpose(bank[2 * t + half][:, q * P:(q + 1) * P],
                                                       x[:, k, t * P:(t + 1) * P], ident[:, :])
                        last.then_inc(out_turned, 1)

            def vector(self, dve):
                for t in range(2):
                    for half in range(2):
                        dve.wait_ge(out_turned, 2 * t + half + 1)
                        nc.vector.tensor_copy(orow[:, t, half * 512:(half + 1) * 512], bank[2 * t + half][:, :]).then_inc(out_moved, 1)

            def sync(self, sp):
                for t in range(2):
                    sp.wait_ge(out_moved, 2 * t + 2)
                    sp.dma_start(out[0, t * P:(t + 1) * P, :], orow[:, t, :]).then_inc(stored, 16)
                sp.wait_ge(stored, 32)
        stages.append(Store())

        block = ctx.enter_context(nc.Block())

        @block.sync
        def _(sp):
            for s in stages[:-1]:
                if hasattr(s, "sync"):
                    s.sync(sp)
            sp_issue(sp, len(panels))
            stages[-1].sync(sp)

        @block.scalar
        def _(act):
            for s in stages:
                if hasattr(s, "scalar"):
                    s.scalar(act)

        @block.vector
        def _(dve):
            for s in stages:
                if hasattr(s, "vector"):
                    s.vector(dve)

        @block.gpsimd
        def _(pool):
            for s in stages:
                if hasattr(s, "gpsimd"):
                    s.gpsimd(pool)

        @block.tensor
        def _(pe):
            for s in stages:
                if hasattr(s, "tensor"):
                    s.tensor(pe)


def constants():
    f8 = np.float64
    c = {}
    ch = np.arange(P, dtype=f8)
    ang = 2 * np.pi * np.outer(ch, ch) / P
    c["k_dft128"] = np.concatenate([np.cos(ang), np.sin(ang)], axis=1) / math.sqrt(LAT * P)
    t = np.arange(LAT, dtype=f8)
    ang = 2 * np.pi * (np.outer(t, t) % LAT) / LAT
    c["k_dft256"] = np.stack([np.cos(ang), -np.sin(ang)]).reshape(2, 2, P, LAT).transpose(2, 0, 1, 3)
    tok = np.arange(LAT)
    freq = 1.0 / 10000.0 ** (np.arange(0, 32, 2, dtype=f8) / 32)
    row, col = np.outer(freq, tok // 64), np.outer(freq, tok % 64)
    ang = np.concatenate([row, row, col, col])
    c["k_rope"] = np.stack([np.cos(ang), np.sin(ang)], axis=1)
    turn = np.zeros((ROPE, ROPE))
    for b in (0, 32):
        for i in range(16):
            turn[b + 16 + i, b + i] = -1.0
            turn[b + i, b + 16 + i] = 1.0
    c["k_turn"] = turn
    f4 = np.float32
    tt = np.linspace(0.0, 1.0, LAT, dtype=f4)[:, None]
    w = f4(2.0 * math.pi / LAT) * np.arange(LAT, dtype=f4)[:, None]
    bands = np.linspace(1e-4, BANDS - 1, BANDS, dtype=f4)[None, :]
    c["k_hyena_z"] = np.concatenate([tt, np.cos(w * bands), -np.sin(w * bands)], axis=1).T
    deltas = np.abs(np.linspace(math.log(1e-2) / 1.5, math.log(1e-2) / 0.3, D, dtype=f4))
    c["k_hyena_decay"] = np.exp(-tt * deltas).reshape(2, P, D).transpose(1, 0, 2)
    ang = np.pi * (np.outer(t, 2 * np.arange(LAT) + 1) % (4 * LAT)) / (2 * LAT)
    cs = np.stack([np.cos(ang), np.sin(ang)])
    c["k_dft_odd"] = cs.reshape(2, 2, P, LAT).transpose(2, 0, 1, 3)
    ics = np.stack([cs[0].T, -cs[1].T]) / LAT
    c["k_idft_odd"] = ics.reshape(2, 2, P, LAT).transpose(2, 0, 1, 3)
    k = np.arange(STEP)
    chunks = STEP * np.arange(1, BLK + 1)
    fwd = np.concatenate([STEP - 1 - k, k + 1, [1], chunks])
    bwd = np.concatenate([k, STEP - k, [1], chunks])
    c["k_s5_lags"] = np.repeat(np.stack([fwd, bwd]), STATE, axis=0)
    return {k: np.ascontiguousarray(v.astype(np.float32)) for k, v in c.items()}


def kernel(**inputs):
    import concourse.bacc as bacc
    from concourse.bass_utils import run_bass_kernel_spmd

    nc = bacc.Bacc("TRN2", target_bir_lowering=False, num_devices=1)
    arrays = {name: np.ascontiguousarray(a) for name, a in inputs.items()}
    arrays.update(constants())
    A = {name: nc.dram_tensor(name, a.shape, mybir.dt.from_np(a.dtype), kind="ExternalInput").ap()
         for name, a in arrays.items()}
    out = nc.dram_tensor("out", (1, LAT, D), F32, kind="ExternalOutput").ap()
    build(nc, A, out)
    r = run_bass_kernel_spmd(nc, [arrays], core_ids=[0])
    return r.results[0]["out"]
```
